# Optimizing a Trainium2 kernel written in Bass

```python
import jax, jax.numpy as jnp
from jax import lax
import numpy as np

D_MODEL = 1024
BATCH = 1
SEQ = 128
DEPTH = 4
DEC_BATCH = 1
DEC_SEQ = 512
PAST_LEN = 128

GRID_W = 64
N_MIXERS = 3
N_HEADS = 16
N_KV_HEADS = 4
HEAD_DIM = D_MODEL // N_HEADS
Q_PER_KV = N_HEADS // N_KV_HEADS
QKV_DIM = (N_HEADS + 2 * N_KV_HEADS) * HEAD_DIM
WINDOW = 128
BLOCK = 128
ROPE_THETA = 10000.0
POOL_WINDOWS = (2, 4, 8, 16)
N_POOL_GROUPS = 4
POOL_GROUP_DIM = D_MODEL // N_POOL_GROUPS
N_FFT_GROUPS = 4
FFT_GROUP_DIM = D_MODEL // N_FFT_GROUPS
D_FF = ((8 * D_MODEL // 3 + 127) // 128) * 128
CONV_W = 3
EPS = 1e-6
NEG_INF = -1e30
N_ATTN_LAYERS = (DEPTH + 2) // 3
N_POOL_LAYERS = (DEPTH + 1) // 3
N_FFT_LAYERS = DEPTH // 3

kernel_name = 'hybrid_diffusion_prefix_trunk_step'

def rmsnorm(x, g):
    xf = x.astype(jnp.float32)
    y = xf * lax.rsqrt(jnp.mean(xf * xf, axis=-1, keepdims=True) + EPS)
    return (y * g.astype(jnp.float32)).astype(x.dtype)

def ada_mods(cond, w, b):
    cond = cond.reshape(-1, D_MODEL)
    mod = (jax.nn.silu(cond) @ w + b)[:, None, :]
    return jnp.split(mod, 6, axis=-1)

def modulate(h, shift, scale):
    return h * (1 + scale) + shift

def axial_rope(x):
    L = x.shape[1]
    rows_n = L // GRID_W
    rows = jnp.repeat(jnp.arange(rows_n), GRID_W)
    cols = jnp.tile(jnp.arange(GRID_W), rows_n)
    half = HEAD_DIM // 2
    inv_freq = 1.0 / (ROPE_THETA ** (jnp.arange(0, half, 2, dtype=jnp.float32) / half))

    def rot(xp, pos):
        ang = pos.astype(jnp.float32)[:, None] * inv_freq
        cos = jnp.cos(ang)[None, :, None, :]
        sin = jnp.sin(ang)[None, :, None, :]
        x1, x2 = jnp.split(xp.astype(jnp.float32), 2, axis=-1)
        return jnp.concatenate([x1 * cos - x2 * sin, x1 * sin + x2 * cos], axis=-1)

    return jnp.concatenate([rot(x[..., :half], rows), rot(x[..., half:], cols)], axis=-1).astype(x.dtype)

def qkv_proj(h, w_qkv, q_norm, k_norm):
    B, L, _ = h.shape
    q, k, v = jnp.split(h @ w_qkv, [N_HEADS * HEAD_DIM, (N_HEADS + N_KV_HEADS) * HEAD_DIM], axis=-1)
    q = rmsnorm(q.reshape(B, L, N_HEADS, HEAD_DIM), q_norm)
    k = rmsnorm(k.reshape(B, L, N_KV_HEADS, HEAD_DIM), k_norm)
    v = v.reshape(B, L, N_KV_HEADS, HEAD_DIM)
    return q, k, v

def attend_block(qb, keys, values, masks, sink):
    scale = HEAD_DIM ** -0.5
    scores = []
    for kp, mk in zip(keys, masks):
        s = jnp.einsum('bqkgd,bskd->bkgqs', qb, kp).astype(jnp.float32) * scale
        if mk is not None:
            s = jnp.where(mk, s, NEG_INF)
        scores.append(s)
    sink_f = sink.astype(jnp.float32).reshape(1, N_KV_HEADS, Q_PER_KV, 1)
    m = sink_f
    for s in scores:
        m = jnp.maximum(m, jnp.max(s, axis=-1))
    denom = jnp.exp(sink_f - m)
    out = jnp.zeros(qb.shape, jnp.float32)
    for s, vp in zip(scores, values):
        p = jnp.exp(s - m[..., None])
        denom = denom + jnp.sum(p, axis=-1)
        out = out + jnp.einsum('bkgqs,bskd->bqkgd', p.astype(vp.dtype), vp).astype(jnp.float32)
    out = out / jnp.moveaxis(denom, -1, 1)[..., None]
    return out.astype(qb.dtype)

def context_attention(q, k, v, sink):
    B, S = q.shape[:2]
    nqb = S // BLOCK
    qg = jnp.moveaxis(q.reshape(B, nqb, BLOCK, N_KV_HEADS, Q_PER_KV, HEAD_DIM), 1, 0)
    out = lax.map(lambda qb: attend_block(qb, [k], [v], [None], sink), qg)
    return jnp.moveaxis(out, 0, 1).reshape(B, S, N_HEADS * HEAD_DIM)

def latent_attention(q, k, v, ctx_k, ctx_v, sink):
    B, L = q.shape[:2]
    nqb = L // BLOCK
    qg = jnp.moveaxis(q.reshape(B, nqb, BLOCK, N_KV_HEADS, Q_PER_KV, HEAD_DIM), 1, 0)
    pad = ((0, 0), (BLOCK, BLOCK), (0, 0), (0, 0))
    k_pad = jnp.pad(k, pad)
    v_pad = jnp.pad(v, pad)
    qi = jnp.arange(BLOCK)
    sj = jnp.arange(3 * BLOCK)
    band = jnp.abs((sj[None, :] - BLOCK) - qi[:, None]) <= WINDOW

    def one_block(args):
        n, qb = args
        kw = lax.dynamic_slice_in_dim(k_pad, n * BLOCK, 3 * BLOCK, axis=1)
        vw = lax.dynamic_slice_in_dim(v_pad, n * BLOCK, 3 * BLOCK, axis=1)
        kpos = n * BLOCK - BLOCK + sj
        mask = band & ((kpos >= 0) & (kpos < L))[None, :]
        return attend_block(qb, [kw, ctx_k], [vw, ctx_v], [mask, None], sink)

    out = lax.map(one_block, (jnp.arange(nqb), qg))
    return jnp.moveaxis(out, 0, 1).reshape(B, L, N_HEADS * HEAD_DIM)

def pool_mix(h, w, scale):
    B, L, D = h.shape
    hf = h.astype(jnp.float32)
    cs = jnp.concatenate([jnp.zeros((B, 1, D), jnp.float32), jnp.cumsum(hf, axis=1)], axis=1)
    t = jnp.arange(L)
    outs = []
    for g, win in enumerate(POOL_WINDOWS):
        lo = win // 2
        hi = win - lo - 1
        start = jnp.clip(t - lo, 0, L)
        end = jnp.clip(t + hi + 1, 0, L)
        csg = cs[..., g * POOL_GROUP_DIM:(g + 1) * POOL_GROUP_DIM]
        mean = (csg[:, end] - csg[:, start]) / (end - start).astype(jnp.float32)[None, :, None]
        outs.append(mean - hf[..., g * POOL_GROUP_DIM:(g + 1) * POOL_GROUP_DIM])
    pooled = jnp.stack(outs, axis=2).astype(h.dtype)
    mixed = jnp.einsum('blgc,gcd->blgd', pooled, w).reshape(B, L, D)
    return mixed * scale

def fourier_mix(h, w):
    B, L, D = h.shape
    hg = h.astype(jnp.float32).reshape(B, L, N_FFT_GROUPS, FFT_GROUP_DIM)
    f = jnp.fft.fft2(hg, axes=(1, 3), norm='ortho').real
    return f.reshape(B, L, D).astype(h.dtype) @ w

def conv_ffn(h, w_in, conv_w, conv_b, w_out):
    u = h @ w_in
    up = jnp.pad(u, ((0, 0), (1, 1), (0, 0)))
    u = up[:, :-2] * conv_w[0] + up[:, 1:-1] * conv_w[1] + up[:, 2:] * conv_w[2] + conv_b
    gate, val = jnp.split(u, 2, axis=-1)
    return (jax.nn.silu(gate) * val) @ w_out

def trunk(x, cond, ctx_k_cache, ctx_v_cache, weights):
    (norm_mix, norm_ffn, ada_w, ada_b, attn_w_qkv, attn_q_norm, attn_k_norm, attn_sink, attn_w_o,
     pool_w, pool_scale, fnet_w, ffn_w_in, ffn_conv_w, ffn_conv_b, ffn_w_out) = weights
    is_latent = ctx_k_cache is not None
    ks, vs = [], []
    for i in range(DEPTH):
        kind, j = i % N_MIXERS, i // N_MIXERS
        sh1, sc1, g1, sh2, sc2, g2 = ada_mods(cond, ada_w[i], ada_b[i])
        h = modulate(rmsnorm(x, norm_mix[i]), sh1, sc1)
        if kind == 0:
            q, k, v = qkv_proj(h, attn_w_qkv[j], attn_q_norm[j], attn_k_norm[j])
            if is_latent:
                o = latent_attention(axial_rope(q), axial_rope(k), v,
                                     ctx_k_cache[:, j], ctx_v_cache[:, j], attn_sink[j])
            else:
                o = context_attention(q, k, v, attn_sink[j])
                ks.append(k)
                vs.append(v)
            mix = o @ attn_w_o[j]
        elif kind == 1:
            mix = pool_mix(h, pool_w[j], pool_scale[j])
        else:
            mix = fourier_mix(h, fnet_w[j])
        x = x + g1 * mix
        h = modulate(rmsnorm(x, norm_ffn[i]), sh2, sc2)
        x = x + g2 * conv_ffn(h, ffn_w_in[i], ffn_conv_w[i], ffn_conv_b[i], ffn_w_out[i])
    return x, ks, vs

def setup_inputs(seed: int = 0) -> dict:
    key = jax.random.key(seed)
    ks = jax.random.split(key, 24)

    def nrm(k, shape, scale=1.0):
        return jax.random.normal(k, shape, jnp.float32) * scale

    cache_shape = (DEC_BATCH, N_ATTN_LAYERS, PAST_LEN, N_KV_HEADS, HEAD_DIM)
    return {
        'x_prompt': nrm(ks[0], (BATCH, SEQ, D_MODEL)),
        'x_sample': nrm(ks[1], (DEC_BATCH, DEC_SEQ, D_MODEL)),
        'cache_k': nrm(ks[2], cache_shape),
        'cache_v': nrm(ks[3], cache_shape),
        'c': nrm(ks[4], (DEC_BATCH, D_MODEL)),
        'c_ctx': nrm(ks[5], (D_MODEL,)),
        'norm_mix': 1.0 + nrm(ks[6], (DEPTH, D_MODEL), 0.1),
        'norm_ffn': 1.0 + nrm(ks[7], (DEPTH, D_MODEL), 0.1),
        'ada_w': nrm(ks[8], (DEPTH, D_MODEL, 6 * D_MODEL), 0.5 * D_MODEL ** -0.5),
        'ada_b': nrm(ks[9], (DEPTH, 6 * D_MODEL), 0.02),
        'attn_w_qkv': nrm(ks[10], (N_ATTN_LAYERS, D_MODEL, QKV_DIM), D_MODEL ** -0.5),
        'attn_q_norm': 1.0 + nrm(ks[11], (N_ATTN_LAYERS, HEAD_DIM), 0.1),
        'attn_k_norm': 1.0 + nrm(ks[12], (N_ATTN_LAYERS, HEAD_DIM), 0.1),
        'attn_sink': nrm(ks[13], (N_ATTN_LAYERS, N_HEADS)),
        'attn_w_o': nrm(ks[14], (N_ATTN_LAYERS, N_HEADS * HEAD_DIM, D_MODEL), (N_HEADS * HEAD_DIM) ** -0.5),
        'pool_w': nrm(ks[15], (N_POOL_LAYERS, N_POOL_GROUPS, POOL_GROUP_DIM, POOL_GROUP_DIM), POOL_GROUP_DIM ** -0.5),
        'pool_scale': 1.0 + nrm(ks[16], (N_POOL_LAYERS, D_MODEL), 0.1),
        'fnet_w': nrm(ks[17], (N_FFT_LAYERS, D_MODEL, D_MODEL), D_MODEL ** -0.5),
        'ffn_w_in': nrm(ks[18], (DEPTH, D_MODEL, 2 * D_FF), D_MODEL ** -0.5),
        'ffn_conv_w': nrm(ks[19], (DEPTH, CONV_W, 2 * D_FF), CONV_W ** -0.5),
        'ffn_conv_b': nrm(ks[20], (DEPTH, 2 * D_FF), 0.02),
        'ffn_w_out': nrm(ks[21], (DEPTH, D_FF, D_MODEL), D_FF ** -0.5),
    }

def reference(x_prompt, x_sample, cache_k, cache_v, c, c_ctx, norm_mix, norm_ffn, ada_w, ada_b,
              attn_w_qkv, attn_q_norm, attn_k_norm, attn_sink, attn_w_o, pool_w, pool_scale, fnet_w,
              ffn_w_in, ffn_conv_w, ffn_conv_b, ffn_w_out):
    weights = (norm_mix, norm_ffn, ada_w, ada_b, attn_w_qkv, attn_q_norm, attn_k_norm, attn_sink,
               attn_w_o, pool_w, pool_scale, fnet_w, ffn_w_in, ffn_conv_w, ffn_conv_b, ffn_w_out)
    y_prompt, ctx_ks, ctx_vs = trunk(x_prompt, c_ctx, None, None, weights)
    new_cache_k = jnp.stack(ctx_ks, axis=1)
    new_cache_v = jnp.stack(ctx_vs, axis=1)
    y_sample, _, _ = trunk(x_sample, c, cache_k, cache_v, weights)
    return (y_prompt, y_sample, new_cache_k, new_cache_v)


_drawn_inputs = setup_inputs


def setup_inputs(seed=0):
    import zlib

    import numpy as np

    out = dict(_drawn_inputs(seed))
    spreads = {}
    factors = {'cache_k': 3.174, 'attn_q_norm': 8.0, 'attn_sink': 8.0, 'ffn_conv_b': 5.079}
    for name, (base, spread) in spreads.items():
        noise = np.random.default_rng([zlib.crc32(name.encode()), seed]).standard_normal(out[name].shape)
        drawn = base * np.exp(spread * noise) if base else spread * noise
        out[name] = __import__('jax').numpy.asarray(drawn.astype(out[name].dtype))
    for name, factor in factors.items():
        out[name] = (out[name] * factor).astype(out[name].dtype)
    return out
```

```python
from contextlib import ExitStack

import numpy as np

import concourse.bass as bass
from concourse import mybir

F32 = mybir.dt.float32
F32R = mybir.dt.float32r
ALU = mybir.AluOpType
ACT = mybir.ActivationFunctionType

P = 128
D = 1024
KT = D // P
LAT, CTX = 512, 128
LAT0, CTX0 = 1, 514
NT = 644
NH = NT // 2
DEPTH = 4
KINDS = ("attn", "pool", "fnet", "attn")
HD = 64
NHEADS = 16
FF = 2816
FT = FF // P
HALF = FT // 2
AW = 256
NCH = 6 * D // AW
CT = AW // P
EPS = 1e-6
NEG = -1e30
POOL_PAD = 8
POOL_W = 672
POOL_LAT, POOL_CTX = 8, 536
WINDOWS = (2, 4, 8, 16)

MIX_UNITS = {"attn": 20, "pool": 8, "fnet": 8}
FFN_UNITS = 2 * (2 * HALF + KT)
UNIT0 = [sum(MIX_UNITS[k] + FFN_UNITS for k in KINDS[:i]) for i in range(DEPTH + 1)]
SQ0 = [sum(2 * KT + (10 if k == "attn" else 0) for k in KINDS[:i]) for i in range(DEPTH)]
RMS0 = [sum(2 + (10 if k == "attn" else 0) for k in KINDS[:i]) for i in range(DEPTH)]
STREAMS = ((LAT0, LAT, 0), (CTX0, CTX, 1))


class Chain:

    def __init__(self, eng, sem):
        self.eng, self.sem, self.n, self.off = eng, sem, 0, 0

    def link(self, ins):
        self.n += 1
        ins.then_inc(self.sem, 1)
        self.eng.wait_ge(self.sem, self.n + self.off)

    def enter(self, i, per):
        self.off, self.start, self.per = i * per, self.n, per

    def leave(self, iterations):
        assert self.n - self.start == self.per
        self.off, self.n = 0, self.start + self.per * iterations


def build(nc, t):
    with ExitStack() as ctx:
        def sb(name, shape, dt=F32, stack=None):
            return (stack or ctx).enter_context(nc.sbuf_tensor(name, shape, dt))

        def sem(name):
            return ctx.enter_context(nc.semaphore(name))

        x = sb("x", [P, KT, NT])
        h_hi = sb("h_hi", [P, KT, NT], F32R)
        h_lo = sb("h_lo", [P, KT, NT], F32R)
        w_raw = [sb(f"w_raw{s}", [P, HALF, P]) for s in range(2)]
        w_hi = [sb(f"w_hi{s}", [P, HALF, P], F32R) for s in range(2)]
        w_lo = [sb(f"w_lo{s}", [P, HALF, P], F32R) for s in range(2)]
        ada_w = [sb(f"ada_w{s}", [P, KT, AW]) for s in range(2)]
        ada_rows = sb("ada_rows", [P, AW])
        cond = sb("cond", [P, KT, 32])
        cond_act = sb("cond_act", [P, KT, 32])
        mods = [sb(f"mods{s}", [P, 48, 2]) for s in range(2)]
        ada_bias = sb("ada_bias", [P, DEPTH, 48, 2])
        gains = sb("gains", [P, DEPTH, 2, KT, 2])
        gain_now = sb("gain_now", [P, KT, 2])
        pool_scale = sb("pool_scale", [P, KT, 2])
        pool_gate = sb("pool_gate", [P, KT, 2])
        conv = sb("conv", [P, DEPTH * 2 * FT, 4])
        head_gain = sb("head_gain", [P, 2, 2])
        sink = sb("sink", [P, 2, NHEADS])
        neg_sink = sb("neg_sink", [P, 2, NHEADS])
        ones = sb("ones", [P, P])
        ones_head = sb("ones_head", [P, P])
        ident = sb("ident", [P, P])
        pick = sb("pick", [P, 2])
        eps = sb("eps", [P, 1])
        u_pad = [sb(f"u_pad{s}", [P, NT + 2]) for s in range(2)]

        with ExitStack() as a:
            sq = [sb(f"sq{s}", [P, NT], F32, a) for s in range(2)]
            rms = sb("rms", [P, NT], F32, a)
            rstd = sb("rstd", [P, NT], F32, a)
            xn = [sb(f"xn{s}", [P, NT], F32, a) for s in range(2)]
        with ExitStack() as a:
            conv_out = [sb(f"conv_out{s}", [P, NT], F32, a) for s in range(2)]
            gate_act = sb("gate_act", [P, NT], F32, a)
            prod = sb("prod", [P, NT], F32, a)
        tmp_store = sb("tmp_store", [P, 6 * (NT + 12)])

        with ExitStack() as a:
            f_hi = sb("f_hi", [P, HALF, NT], F32R, a)
            f_lo = sb("f_lo", [P, HALF, NT], F32R, a)
        with ExitStack() as a:
            qkv = sb("qkv", [P, 12, NT], F32, a)
            v_tok = sb("v_tok", [P, 5, 256], F32, a)
            ck = sb("ck", [P, 2, P], F32, a)
            cv = sb("cv", [P, 256], F32, a)
            rope_cos = sb("rope_cos", [P, LAT], F32, a)
            rope_sin = sb("rope_sin", [P, LAT], F32, a)
            band = sb("band", [P, 512], F32, a)
            swapped = sb("swapped", [P, LAT], F32, a)
            prob = [[sb(f"prob{s}{hd}", [P, 512], F32, a) for hd in range(2)] for s in range(2)]
            probT = [[sb(f"probT{s}{hd}", [P, 512], F32, a) for hd in range(2)] for s in range(2)]
            stat = sb("stat", [P, 2, 2, 8], F32, a)
        with ExitStack() as a:
            hp = [sb(f"hp{s}", [P, POOL_W], F32, a) for s in range(2)]
            win = [sb(f"win{s}", [P, POOL_W], F32, a) for s in range(2)]
            inv_count = sb("inv_count", [P, 4, POOL_W - 16], F32, a)
            pooled = [sb(f"pooled{s}", [P, POOL_W - 16], F32, a) for s in range(2)]
        with ExitStack() as a:
            tab_raw = sb("tab_raw", [P, 512], F32, a)
            tab_hi = sb("tab_hi", [P, 11, 512], F32R, a)
            tab_lo = sb("tab_lo", [P, 11, 512], F32R, a)
            ab_hi = sb("ab_hi", [P, 5, 512], F32R, a)
            ab_lo = sb("ab_lo", [P, 5, 512], F32R, a)
        stage_store = sb("stage_store", [P, 66 * 256])
        assert stage_store is not None and tmp_store is not None

        ps = ctx.enter_context(nc.psum_tensor("ps", [P, 8, 512], F32))
        SSQ, ADA_ROWS, ADA_COLS = 4, 6, 7

        const_in = sem("const_in")
        x_in = sem("x_in")
        stage_in = sem("stage_in")
        raw_in = [sem(f"raw_in{s}") for s in range(2)]
        hi_made = sem("hi_made")
        lo_made = sem("lo_made")
        unit_done = sem("unit_done")
        taken = [sem(f"taken{s}") for s in range(2)]
        setup_done = sem("setup_done")
        sq_made = sem("sq_made")
        sq_used = sem("sq_used")
        rms_made = sem("rms_made")
        rstd_made = sem("rstd_made")
        xn_made = sem("xn_made")
        hh_made = sem("hh_made")
        hl_made = sem("hl_made")
        cond_made = sem("cond_made")
        ada_in = [sem(f"ada_in{s}") for s in range(2)]
        ada_mm = sem("ada_mm")
        ada_row = sem("ada_row")
        ada_col = sem("ada_col")
        ada_done = sem("ada_done")
        conv_done = sem("conv_done")
        silu_made = sem("silu_made")
        prod_made = sem("prod_made")
        fl_made = sem("fl_made")
        qk_ready = sem("qk_ready")
        v_turned = sem("v_turned")
        v_ready = sem("v_ready")
        s_done = sem("s_done")
        max_made = sem("max_made")
        exp_made = sem("exp_made")
        p_ready = sem("p_ready")
        t_done = sem("t_done")
        pt_made = sem("pt_made")
        o_done = sem("o_done")
        oh_made = sem("oh_made")
        ol_made = sem("ol_made")
        pool_made = sem("pool_made")
        ph_made = sem("ph_made")
        tab_in = sem("tab_in")
        tabh_made = sem("tabh_made")
        tabl_made = sem("tabl_made")
        ft_mm = sem("ft_mm")
        fth_made = sem("fth_made")
        ftl_made = sem("ftl_made")
        out_sent = sem("out_sent")
        dve_own = sem("dve_own")

        def wait_taken(eng, u):
            eng.wait_ge(taken[u % 2], u // 2 + 1)

        def halves(ap):
            return ap.rearrange("p (a b) -> p a b", a=2)

        def product(s):
            return ps[:, 2 * s:2 * s + 2, 0:NH]

        units = []
        for layer, kind in enumerate(KINDS):
            if kind == "attn":
                a = layer // 3
                units += [(KT, t["w_qkv"], 12 * a + n) for n in range(12)]
                units += [(KT, t["w_o"], KT * a + n) for n in range(KT)]
            elif kind == "pool":
                units += [(2, t["w_pool"], n) for n in range(KT)]
            else:
                units += [(KT, t["w_fnet"], n) for n in range(KT)]
            for half in range(2):
                units += [(KT, t["w_in"], (2 * layer + half) * 2 * HALF + n) for n in range(2 * HALF)]
                units += [(HALF, t["w_out"], (2 * layer + half) * KT + n) for n in range(KT)]
        assert len(units) == UNIT0[DEPTH]

        CONSTS = ((cond, "cond"), (ada_bias, "ada_bias"), (gains, "gains"), (pool_scale, "pool_scale"),
                  (pick, "pick"), (ones_head, "ones_head"), (ident, "ident"), (conv, "conv"),
                  (head_gain, "head_gain"), (sink, "sink"))
        PADS = ((0, LAT0), (LAT0 + LAT, 1), (CTX0 + CTX, NT - CTX0 - CTX))
        N_SETUP = 6 + 2 * len(PADS)
        STAGE_IN = (5, 6, 6, 11)
        TOKEN_BLOCKS = [LAT0 + P * n for n in range(LAT // P)] + [CTX0]
        KEYS = ((128, 384), (0, 384), (0, 384), (0, 256), (128, 256))
        BLOCKS = ((1, 2, 3), (0, 1, 2, 3), (0, 1, 2, 3), (0, 1, 3), (1,))
        WORK = [(nb, tile) for nb in range(5) for tile in range(KT)]

        block = ctx.enter_context(nc.Block())

        @block.sync
        def _(sp):
            def load_unit(u, par, k, src):
                if not isinstance(u, int) or u >= 2:
                    sp.wait_ge(lo_made, u - 1)
                sp.dma_start(w_raw[par][:, 0:k, :], src).then_inc(raw_in[par], 16)

            def load_units(u0, n):
                for u in range(u0, u0 + n):
                    k, arr, row = units[u]
                    load_unit(u, u % 2, k, arr[row].rearrange("p (k c) -> p k c", k=k))

            def load_chunk(c, par, src):
                if not isinstance(c, int) or c >= 2:
                    sp.wait_ge(ada_mm, c - 1)
                sp.dma_start(ada_w[par][:], src).then_inc(ada_in[par], 16)

            def chunk_rows(c):
                return t["ada_w"][c].rearrange("p (k c) -> p k c", k=KT)

            def looped(arr, k, row):
                return arr[bass.ds(row, 1)].rearrange("a p (k c) -> p (a k) c", k=k)

            for dst, src in CONSTS:
                sp.dma_start(dst[:], t[src]).then_inc(const_in, 16)
            load_units(0, 2)
            for c in range(2):
                load_chunk(c, c, chunk_rows(c))
            sp.dma_start(x[:], t["x"]).then_inc(x_in, 16)
            for c in range(2, NCH):
                load_chunk(c, c % 2, chunk_rows(c))

            for layer, kind in enumerate(KINDS):
                u0 = UNIT0[layer]
                if layer:
                    load_units(u0, 2)
                    sp.wait_ge(unit_done, u0)
                a = layer // 3
                if kind == "attn":
                    for dst, src in ((rope_cos[:], t["rope_cos"]), (rope_sin[:], t["rope_sin"]),
                                     (band[:], t["band"]), (ck[:], t["cache_k"][a]), (cv[:], t["cache_v"][a])):
                        sp.dma_start(dst, src).then_inc(stage_in, 16)
                elif kind == "pool":
                    sp.dma_start(inv_count[:], t["inv_count"]).then_inc(stage_in, 16)
                else:
                    for n in range(11):
                        if n:
                            sp.wait_ge(tabl_made, n)
                        sp.dma_start(tab_raw[:], t["dft"][n]).then_inc(tab_in, 16)
                load_units(u0 + 2, MIX_UNITS[kind] - 2)
                if kind == "attn":
                    sp.wait_ge(qk_ready, 10 * (a + 1))
                    wait_taken(sp, u0 + 10)
                    wait_taken(sp, u0 + 11)
                    sp.dma_start(t["new_k"][a], qkv[:, 8:10, CTX0:CTX0 + CTX]).then_inc(out_sent, 16)
                    sp.dma_start(t["new_v"][a], qkv[:, 10:12, CTX0:CTX0 + CTX]).then_inc(out_sent, 16)
                for half in range(2):
                    ub = u0 + MIX_UNITS[kind] + half * (2 * HALF + KT)
                    up_row = (2 * layer + half) * 2 * HALF
                    c0 = NCH * (layer + 1) + half * NCH // 2
                    with sp.Fori(0, HALF // 2) as i:
                        for n in range(4):
                            load_unit(i * 4 + (ub + n), n % 2, KT, looped(t["w_in"], KT, i * 4 + (up_row + n)))
                            if n % 2 and layer + 1 < DEPTH:
                                c = i * 2 + (c0 + n // 2)
                                load_chunk(c, n // 2, looped(t["ada_w"], KT, c))
                    load_units(ub + 2 * HALF - 2, 2)
                    if layer + 1 < DEPTH:
                        for c in range(c0 + HALF - 1, c0 + HALF + 1):
                            load_chunk(c, c % 2, chunk_rows(c))
                    with sp.Fori(0, KT // 2) as i:
                        for n in range(2):
                            load_unit(i * 2 + (ub + 2 * HALF + n), n, HALF,
                                      looped(t["w_out"], HALF, i * 2 + ((2 * layer + half) * KT + n)))
            for o in range(KT):
                wait_taken(sp, UNIT0[DEPTH] - KT + o)
                sp.dma_start(t["y"][:, o, :], x[:, o, :]).then_inc(out_sent, 16)
            sp.wait_ge(out_sent, 16 * (4 + KT))

        @block.gpsimd
        def _(pool):
            pool.memset(ones[:], 1.0).then_inc(setup_done, 1)
            pool.memset(eps[:], EPS).then_inc(setup_done, 1)
            pool.sem_inc(conv_done, 2)
            pool.sem_inc(prod_made, 1)
            pool.sem_inc(fl_made, 1)
            for s in range(2):
                pool.memset(u_pad[s][:, 0:1], 0.0).then_inc(setup_done, 1)
                pool.memset(u_pad[s][:, NT + 1:NT + 2], 0.0).then_inc(setup_done, 1)
            for hx in (h_hi, h_lo):
                for a0, n in PADS:
                    pool.memset(hx[:, :, a0:a0 + n].bitcast(F32), 0.0).then_inc(setup_done, 1)

        @block.tensor
        def _(pe):
            def unit(u, par, k, rhs, ready=None, prior=None):
                pe.wait_ge(lo_made, u + 1)
                if prior is None or not isinstance(prior, int) or prior > 0:
                    pe.wait_ge(taken[par], prior)
                for kk in range(k):
                    if ready:
                        ready(kk)
                    b_hi, b_lo = rhs(kk)
                    for n, (w, b) in enumerate(((w_hi, b_hi), (w_hi, b_lo), (w_lo, b_hi))):
                        for hf in range(2):
                            mm = pe.matmul(ps[:, 2 * par + hf, 0:NH], w[par][:, kk, :],
                                           b[:, hf * NH:(hf + 1) * NH],
                                           start=(kk == 0 and n == 0), stop=(kk == k - 1 and n == 2))
                mm.then_inc(unit_done, 1)

            def h_tiles(kk):
                return h_hi[:, kk, :], h_lo[:, kk, :]

            def f_tiles(kk):
                return f_hi[:, kk, :], f_lo[:, kk, :]

            def sum_squares(i, k, weights, first, last, rms_before):
                pe.wait_ge(sq_made, i + 1)
                if first and rms_before:
                    pe.wait_ge(rms_made, rms_before)
                for hf in range(2):
                    mm = pe.matmul(ps[:, SSQ + hf, 0:NH], weights[:], sq[i % 2][:, hf * NH:(hf + 1) * NH],
                                   start=first, stop=last)
                mm.then_inc(sq_used, 1)

            def ada_multiply(c, par, turn):
                pe.wait_ge(ada_in[par], turn * 16 + 16)
                if not isinstance(c, int) or c >= 1:
                    pe.wait_ge(ada_row, c)
                for r in range(2):
                    for j in range(4):
                        mm = pe.matmul(ps[32 * j:32 * j + 32, ADA_ROWS, 0:AW], cond_act[:, 4 * r + j, :],
                                       ada_w[par][:, 4 * r + j, :], start=(r == 0), stop=(r == 1),
                                       skip_group_check=True)
                mm.then_inc(ada_mm, 1)

            def ada_turn(c):
                pe.wait_ge(ada_row, c + 1)
                if not isinstance(c, int) or c >= 1:
                    pe.wait_ge(ada_done, c)
                for n in range(CT):
                    mm = pe.matmul(ps[:, ADA_COLS, 2 * n:2 * n + 2], ada_rows[:, n * P:(n + 1) * P], pick[:],
                                   start=True, stop=True)
                mm.then_inc(ada_col, 1)

            def norm(layer, second):
                base = SQ0[layer] + (KT + (10 if KINDS[layer] == "attn" else 0) if second else 0)
                r0 = RMS0[layer] + (1 + (10 if KINDS[layer] == "attn" else 0) if second else 0)
                for kk in range(KT):
                    sum_squares(base + kk, kk, ones, kk == 0, kk == KT - 1, r0)

            def mixer_units(layer, first, n):
                for m in range(n):
                    u = UNIT0[layer] + first + m
                    ready = None
                    if first == 0 and m == 0:
                        def ready(kk):
                            pe.wait_ge(hl_made, KT * 2 * layer + kk + 1)
                    unit(u, u % 2, KT, h_tiles, ready, u // 2)

            pe.wait_ge(const_in, 16 * len(CONSTS))
            pe.wait_ge(setup_done, N_SETUP)
            pe.wait_ge(cond_made, 1)
            for c in range(NCH):
                ada_multiply(c, c % 2, c // 2)
                if c:
                    ada_turn(c - 1)
            ada_turn(NCH - 1)

            for layer, kind in enumerate(KINDS):
                u0 = UNIT0[layer]
                norm(layer, False)
                if kind == "attn":
                    a = layer // 3
                    sq0, r0 = SQ0[layer] + KT, RMS0[layer] + 1
                    for n in range(12):
                        u = u0 + n
                        ready = None
                        if n == 0:
                            def ready(kk):
                                pe.wait_ge(hl_made, KT * 2 * layer + kk + 1)
                        unit(u, u % 2, KT, h_tiles, ready, u // 2)
                        if 1 <= n <= 10:
                            sum_squares(sq0 + n - 1, 0, ones_head, True, True, r0 + n - 1)
                    wait_taken(pe, u0 + 10)
                    wait_taken(pe, u0 + 11)
                    for v in range(2):
                        if v or a:
                            pe.wait_ge(v_ready, 2 * a + v)
                        for tb in range(5):
                            at = TOKEN_BLOCKS[tb]
                            mm = pe.transpose(ps[:, 6 + tb // 4, (tb % 4) * P:(tb % 4 + 1) * P],
                                              qkv[:, 10 + v, at:at + P], ident[:])
                        mm.then_inc(v_turned, 1)
                    pe.wait_ge(v_ready, 2 * (a + 1))
                    pe.wait_ge(qk_ready, 10 * (a + 1))
                    pe.wait_ge(stage_in, 16 * STAGE_IN[layer])
                    w0 = 40 * a

                    def scores(w):
                        nb, tile = WORK[w - w0]
                        ga = tile // 4
                        if w - w0 >= 2:
                            pe.wait_ge(max_made, 2 * (w - 1))
                        for hd in range(2):
                            rows = slice(HD * hd, HD * hd + HD)
                            q = qkv[rows, tile, TOKEN_BLOCKS[nb]:TOKEN_BLOCKS[nb] + P]
                            out = ps[:, 2 * (w % 2) + hd, :]
                            lo, hi = KEYS[nb]
                            first = TOKEN_BLOCKS[nb] + lo - P
                            mm = pe.matmul(out[:, lo:hi], q, qkv[rows, 8 + ga, first:first + hi - lo],
                                           start=True, stop=True)
                            if nb < 4:
                                mm = pe.matmul(out[:, 384:512], q, ck[rows, ga, :], start=True, stop=True)
                            mm.then_inc(s_done, 1)

                    def turn(w):
                        nb, _ = WORK[w - w0]
                        for hd in range(2):
                            pe.wait_ge(p_ready, 2 * w + hd + 1)
                            if w - w0 >= 1:
                                pe.wait_ge(pt_made, 2 * (w - 1) + hd + 1)
                            for b in BLOCKS[nb]:
                                mm = pe.transpose(ps[:, 4 + hd, b * P:(b + 1) * P],
                                                  prob[w % 2][hd][:, b * P:(b + 1) * P], ident[:])
                            mm.then_inc(t_done, 1)

                    def values(w):
                        nb, tile = WORK[w - w0]
                        ga = tile // 4
                        if w - w0 >= 2:
                            pe.wait_ge(ol_made, w - 1)
                        for hd in range(2):
                            pe.wait_ge(pt_made, 2 * w + hd + 1)
                            kv = slice(HD * (2 * ga + hd), HD * (2 * ga + hd + 1))
                            for b in BLOCKS[nb]:
                                v = cv[:, kv] if b == 3 else v_tok[:, nb - 1 + b, kv]
                                mm = pe.matmul(ps[HD * hd:HD * hd + HD, 6 + w % 2, 0:P], v,
                                               probT[w % 2][hd][:, b * P:(b + 1) * P],
                                               start=(b == BLOCKS[nb][0]), stop=(b == BLOCKS[nb][-1]))
                        mm.then_inc(o_done, 1)

                    for w in range(w0, w0 + 42):
                        if w < w0 + 40:
                            scores(w)
                        if w - w0 >= 2:
                            values(w - 2)
                        if 1 <= w - w0 <= 40:
                            turn(w - 1)
                    pe.wait_ge(ol_made, 40 * (a + 1))
                    for n in range(12, 20):
                        unit(u0 + n, n % 2, KT, h_tiles, None, (u0 + n) // 2)
                elif kind == "pool":
                    for n in range(KT):
                        g = n // 2

                        def ready(kk):
                            pe.wait_ge(hl_made, KT * 2 * layer + 2 * g + kk + 1)
                        unit(u0 + n, n % 2, 2, lambda kk: (h_hi[:, 2 * g + kk, :], h_lo[:, 2 * g + kk, :]),
                             ready, (u0 + n) // 2)
                else:
                    pe.wait_ge(tabl_made, 11)
                    for g in range(4):
                        for tb in range(5):
                            e = 7 * g + tb
                            if g == 0 and tb == 0:
                                pe.wait_ge(hl_made, KT * 2 * layer + KT)
                            if tb == 4:
                                pe.wait_ge(ftl_made, 7 * g + 1)
                            elif g:
                                pe.wait_ge(ftl_made, 7 * (g - 1) + (5 if tb == 0 else tb + 1))
                            at = TOKEN_BLOCKS[tb]
                            for kk in range(2):
                                for n, (hx, tab) in enumerate(((h_hi, tab_hi), (h_hi, tab_lo), (h_lo, tab_hi))):
                                    mm = pe.matmul(ps[:, 4 + tb % 4, :], hx[:, 2 * g + kk, at:at + P],
                                                   tab[:, 8 + kk, :], start=(kk == 0 and n == 0),
                                                   stop=(kk == 1 and n == 2))
                            mm.then_inc(ft_mm, 1)
                        pe.wait_ge(ftl_made, 7 * g + 5)
                        for c in range(2):
                            if g:
                                pe.wait_ge(ftl_made, 7 * (g - 1) + 5 + c + 1)
                            for tb in range(5):
                                latent = tb < 4
                                out = ps[:, 2 * c, :] if latent else ps[:, 2 * c + 1, 0:CTX]
                                for part in range(2):
                                    col = part * 256 + c * P
                                    for n, (ab, tab) in enumerate(((ab_hi, tab_hi), (ab_hi, tab_lo),
                                                                   (ab_lo, tab_hi))):
                                        rhs = (tab[:, 4 * part + tb, :] if latent
                                               else tab[:, 10, part * P:part * P + P])
                                        mm = pe.matmul(out, ab[:, tb, col:col + P], rhs,
                                                       start=(tb in (0, 4) and part == 0 and n == 0),
                                                       stop=(tb in (3, 4) and part == 1 and n == 2))
                            mm.then_inc(ft_mm, 1)
                    pe.wait_ge(ftl_made, 28)
                    for n in range(KT):
                        unit(u0 + n, n % 2, KT, h_tiles, None, (u0 + n) // 2)

                norm(layer, True)
                last = layer + 1 == DEPTH
                for half in range(2):
                    ub = u0 + MIX_UNITS[kind] + half * (2 * HALF + KT)
                    c0 = NCH * (layer + 1) + half * NCH // 2
                    fl0 = (2 * layer + half) * HALF
                    if half == 0:
                        for kk in range(KT):
                            pe.wait_ge(hl_made, KT * (2 * layer + 1) + kk + 1)
                    with pe.Fori(0, HALF // 2) as i:
                        for n in range(4):
                            unit(i * 4 + (ub + n), n % 2, KT, h_tiles, None, i * 2 + (ub + n) // 2)
                            if not last:
                                if n % 2 == 0:
                                    ada_multiply(i * 2 + (c0 + n // 2), n // 2, i + c0 // 2)
                                else:
                                    ada_turn(i * 2 + (c0 + n // 2))
                    for n in range(2 * HALF - 2, 2 * HALF):
                        unit(ub + n, n % 2, KT, h_tiles, None, (ub + n) // 2)
                        if not last:
                            c = c0 + HALF - 1
                            if n % 2 == 0:
                                ada_multiply(c, c % 2, c // 2)
                            else:
                                ada_turn(c)
                                ada_multiply(c + 1, (c + 1) % 2, (c + 1) // 2)

                    def gated(kk):
                        pe.wait_ge(fl_made, fl0 + kk + 2)
                    unit(ub + 2 * HALF, 0, HALF, f_tiles, gated, (ub + 2 * HALF) // 2)
                    if not last:
                        ada_turn(c0 + HALF)
                    unit(ub + 2 * HALF + 1, 1, HALF, f_tiles, None, (ub + 2 * HALF) // 2)
                    with pe.Fori(0, KT // 2 - 1) as i:
                        for n in range(2):
                            u = i * 2 + (ub + 2 * HALF + 2 + n)
                            unit(u, n, HALF, f_tiles, None, i + (ub + 2 * HALF + 2) // 2)

        @block.scalar
        def _(act):
            def split_hi(u, par, k, turn):
                if not isinstance(u, int) or u >= 2:
                    act.wait_ge(unit_done, u - 1)
                act.wait_ge(raw_in[par], turn * 16 + 16)
                act.activation(w_hi[par][:, 0:k, :], w_raw[par][:, 0:k, :], ACT.Copy).then_inc(hi_made, 1)

            def split_next(u):
                if u + 2 < len(units):
                    split_hi(u + 2, u % 2, units[u + 2][0], (u + 2) // 2)

            def square(i, src, free):
                if i >= 2:
                    act.wait_ge(sq_used, i - 1)
                act.activation(sq[i % 2][:] if free else halves(sq[i % 2][:]), src,
                               ACT.Square).then_inc(sq_made, 1)

            def root(i, used, scale):
                act.wait_ge(sq_used, used)
                if i:
                    act.wait_ge(rstd_made, i)
                act.activation(halves(rms[:]), ps[:, SSQ:SSQ + 2, 0:NH], ACT.Sqrt, bias=eps[:, 0:1],
                               scale=scale).then_inc(rms_made, 1)

            def norm(layer, second):
                attn = KINDS[layer] == "attn"
                m = 2 * layer + second
                base = SQ0[layer] + (KT + (10 if attn else 0) if second else 0)
                r = RMS0[layer] + (1 + (10 if attn else 0) if second else 0)
                u_end = UNIT0[layer] + (MIX_UNITS[KINDS[layer]] if second else 0)
                for kk in range(KT):
                    if m:
                        wait_taken(act, u_end - KT + kk)
                    else:
                        act.wait_ge(x_in, 16)
                    square(base + kk, x[:, kk, :], True)
                root(r, base + KT, 1.0 / D)
                shift = 24 if second else 0
                md = mods[layer % 2]
                for kk in range(KT):
                    act.wait_ge(xn_made, KT * m + kk + 1)
                    pooling = KINDS[layer] == "pool" and not second
                    if pooling and kk >= 2:
                        act.wait_ge(pool_made, kk - 1)
                    for at, n, cnd in STREAMS:
                        if pooling:
                            p0 = POOL_LAT if cnd == 0 else POOL_CTX
                            dst = hp[kk % 2][:, p0:p0 + n]
                        else:
                            dst = h_hi[:, kk, at:at + n]
                        op = act.activation(dst, xn[kk % 2][:, at:at + n], ACT.Identity,
                                            bias=md[:, shift + kk, cnd:cnd + 1])
                    op.then_inc(hh_made, 1)
                    if pooling:
                        if kk >= 1:
                            pool_hi(layer, kk - 1)
                if KINDS[layer] == "pool" and not second:
                    pool_hi(layer, KT - 1)

            def pool_hi(layer, kk):
                act.wait_ge(pool_made, kk + 1)
                for at, n, cnd in STREAMS:
                    p0 = (POOL_LAT if cnd == 0 else POOL_CTX) - POOL_PAD
                    op = act.activation(h_hi[:, kk, at:at + n], pooled[kk % 2][:, p0:p0 + n], ACT.Copy)
                op.then_inc(ph_made, 1)

            act.wait_ge(const_in, 16 * len(CONSTS))
            act.wait_ge(setup_done, N_SETUP)
            act.activation(cond_act[:], cond[:], ACT.Silu).then_inc(cond_made, 1)
            for u in range(2):
                split_hi(u, u, units[u][0], 0)
            for layer, kind in enumerate(KINDS):
                u0 = UNIT0[layer]
                norm(layer, False)
                if kind == "attn":
                    a = layer // 3
                    sq0, r0 = SQ0[layer] + KT, RMS0[layer] + 1
                    for n in range(12):
                        u = u0 + n
                        act.wait_ge(unit_done, u + 1)
                        if n < 10:
                            square(sq0 + n, product(n % 2), False)
                        act.activation(halves(qkv[:, n, :]), product(n % 2), ACT.Copy).then_inc(taken[n % 2], 1)
                        split_next(u)
                        if 1 <= n <= 10:
                            root(r0 + n - 1, sq0 + n, 1.0 / HD)
                    w0 = 40 * a

                    def exps(w):
                        nb, tile = WORK[w - w0]
                        ga, r = tile // 4, tile % 4
                        lo, hi = KEYS[nb]
                        hi = 512 if nb < 4 else hi
                        for hd in range(2):
                            head = 8 * ga + 4 * hd + r
                            st = stat[:, w % 2, hd, :]
                            act.wait_ge(max_made, 2 * w + hd + 1)
                            act.activation(prob[w % 2][hd][:, lo:hi], prob[w % 2][hd][:, lo:hi], ACT.Exp,
                                           bias=st[:, 1:2], scale=HD ** -0.5, accum_out=st[:, 2:3])
                            act.activation(st[:, 3:4], sink[:, a, head:head + 1], ACT.Exp,
                                           bias=st[:, 1:2]).then_inc(exp_made, 1)

                    def turned(w):
                        nb, _ = WORK[w - w0]
                        b0, b1 = BLOCKS[nb][0] * P, (BLOCKS[nb][-1] + 1) * P
                        if w - w0 >= 2:
                            act.wait_ge(o_done, w - 1)
                        for hd in range(2):
                            act.wait_ge(t_done, 2 * w + hd + 1)
                            act.activation(probT[w % 2][hd][:, b0:b1], ps[:, 4 + hd, b0:b1],
                                           ACT.Copy).then_inc(pt_made, 1)

                    def out_hi(w):
                        nb, tile = WORK[w - w0]
                        act.wait_ge(o_done, w + 1)
                        act.activation(h_hi[:, tile, TOKEN_BLOCKS[nb]:TOKEN_BLOCKS[nb] + P],
                                       ps[:, 6 + w % 2, 0:P], ACT.Copy).then_inc(oh_made, 1)

                    for w in range(w0, w0 + 42):
                        if w < w0 + 40:
                            exps(w)
                        if w - w0 >= 2:
                            out_hi(w - 2)
                        if 1 <= w - w0 <= 40:
                            turned(w - 1)
                    for n in range(12, 20):
                        split_next(u0 + n)
                elif kind == "pool":
                    for n in range(KT):
                        split_next(u0 + n)
                else:
                    for g in range(4):
                        for tb in range(5):
                            act.wait_ge(ft_mm, 7 * g + tb + 1)
                            act.activation(ab_hi[:, tb, :], ps[:, 4 + tb % 4, :], ACT.Copy).then_inc(fth_made, 1)
                        for c in range(2):
                            act.wait_ge(ft_mm, 7 * g + 5 + c + 1)
                            act.activation(h_hi[:, 2 * g + c, LAT0:LAT0 + LAT], ps[:, 2 * c, :], ACT.Copy)
                            act.activation(h_hi[:, 2 * g + c, CTX0:CTX0 + CTX], ps[:, 2 * c + 1, 0:CTX],
                                           ACT.Copy).then_inc(fth_made, 1)
                    for n in range(KT):
                        split_next(u0 + n)
                norm(layer, True)

                def up_step(u, par, half_u, pair, v, k_next):
                    isint = isinstance(v, int)
                    act.wait_ge(unit_done, u + 1)
                    act.wait_ge(conv_done, v + 1)
                    act.wait_ge(prod_made, pair + 1)
                    act.activation(halves(u_pad[par][:, 1:NT + 1]), product(par), ACT.Copy)
                    act.activation(halves(conv_out[par][:]), product(par), ACT.Identity,
                                   bias=conv[:, v, 3:4] if isint else conv[:, bass.ds(v, 1), 3],
                                   scale=conv[:, v, 1:2] if isint else conv[:, bass.ds(v, 1), 1]
                                   ).then_inc(taken[par], 1)
                    split_hi(u + 2, par, k_next, half_u + 1)
                    if par == 0:
                        act.wait_ge(conv_done, v + 3)
                        act.activation(gate_act[:], conv_out[0][:], ACT.Silu).then_inc(silu_made, 1)

                for half in range(2):
                    ub = u0 + MIX_UNITS[kind] + half * (2 * HALF + KT)
                    v0 = (2 * layer + half) * 2 * HALF
                    with act.Fori(0, HALF // 2) as i:
                        for n in range(4):
                            up_step(i * 4 + (ub + n), n % 2, i * 2 + (ub + n) // 2,
                                    i * 2 + (v0 + n) // 2, i * 4 + (v0 + n), KT)
                    for n in range(2 * HALF - 2, 2 * HALF):
                        up_step(ub + n, n % 2, (ub + n) // 2, (v0 + n) // 2, v0 + n, HALF)
                    ud = ub + 2 * HALF
                    with act.Fori(0, KT // 2 - 1) as i:
                        for n in range(2):
                            split_hi(i * 2 + (ud + n + 2), n, HALF, i + (ud + 2) // 2)
                    for n in range(KT - 2, KT):
                        split_next(ud + n)
                if layer + 1 < DEPTH and KINDS[layer + 1] == "fnet":
                    for n in range(11):
                        if n == 0:
                            act.wait_ge(unit_done, UNIT0[layer + 1])
                        act.wait_ge(tab_in, 16 * (n + 1))
                        act.activation(tab_hi[:, n, :], tab_raw[:], ACT.Copy).then_inc(tabh_made, 1)

        @block.vector
        def _(dve):
            own = Chain(dve, dve_own)

            def split_lo(u, par, k):
                dve.wait_ge(hi_made, u + 1)
                dve.tensor_tensor(w_lo[par][:, 0:k, :], w_raw[par][:, 0:k, :], w_hi[par][:, 0:k, :].bitcast(F32),
                                  ALU.subtract).then_inc(lo_made, 1)

            def split_next(u):
                if u + 2 < len(units):
                    split_lo(u + 2, u % 2, units[u + 2][0])

            def ada_copy(c):
                dve.wait_ge(ada_mm, c + 1)
                if not isinstance(c, int) or c >= 1:
                    dve.wait_ge(ada_col, c)
                dve.tensor_copy(ada_rows[:], ps[:, ADA_ROWS, 0:AW]).then_inc(ada_row, 1)

            def ada_add(c, layer, tile):
                dve.wait_ge(ada_col, c + 1)
                cols = ps[:, ADA_COLS, 0:2 * CT].rearrange("p (n c) -> p n c", c=2)
                if isinstance(tile, int):
                    sl = slice(tile, tile + CT)
                    dve.tensor_tensor(mods[layer % 2][:, sl, :], cols, ada_bias[:, layer, sl, :],
                                      ALU.add).then_inc(ada_done, 1)
                else:
                    dve.tensor_tensor(mods[layer % 2][:, bass.ds(tile, CT), :], cols,
                                      ada_bias[:, layer, bass.ds(tile, CT), :], ALU.add).then_inc(ada_done, 1)

            def norm(layer, second):
                attn = KINDS[layer] == "attn"
                m = 2 * layer + second
                r = RMS0[layer] + (1 + (10 if attn else 0) if second else 0)
                base = KT * m
                md = mods[layer % 2]
                dve.wait_ge(ada_done, NCH * (layer + 1))
                sc = 32 if second else 8
                own.link(dve.scalar_tensor_tensor(gain_now[:], md[:, sc:sc + KT, :], 1.0,
                                                  gains[:, layer, int(second), :, :], ALU.add, ALU.mult))
                if KINDS[layer] == "pool" and not second:
                    own.link(dve.tensor_tensor(pool_gate[:], md[:, 16:16 + KT, :], pool_scale[:], ALU.mult))
                dve.wait_ge(rms_made, r + 1)
                dve.reciprocal(rstd[:], rms[:]).then_inc(rstd_made, 1)
                dve.wait_ge(rstd_made, r + 1)
                if m == 0:
                    dve.wait_ge(x_in, 16)
                shift = 24 if second else 0
                pooling = KINDS[layer] == "pool" and not second

                def scaled(kk):
                    if kk >= 2:
                        if pooling:
                            dve.wait_ge(hh_made, base + kk - 1)
                        else:
                            dve.wait_ge(hl_made, base + kk - 1)
                    for at, n, cnd in STREAMS:
                        op = dve.scalar_tensor_tensor(xn[kk % 2][:, at:at + n], x[:, kk, at:at + n],
                                                      gain_now[:, kk, cnd:cnd + 1], rstd[:, at:at + n],
                                                      ALU.mult, ALU.mult)
                    op.then_inc(xn_made, 1)

                def low(kk):
                    dve.wait_ge(hh_made, base + kk + 1)
                    dve.wait_ge(xn_made, base + kk + 1)
                    for at, n, cnd in STREAMS:
                        op = dve.scalar_tensor_tensor(h_lo[:, kk, at:at + n], xn[kk % 2][:, at:at + n],
                                                      md[:, shift + kk, cnd:cnd + 1],
                                                      h_hi[:, kk, at:at + n].bitcast(F32), ALU.add, ALU.subtract)
                    op.then_inc(hl_made, 1)

                for kk in range(KT + 1):
                    if kk < KT:
                        scaled(kk)
                    if kk >= 1:
                        if pooling:
                            pool_tile(layer, kk - 1, base)
                        else:
                            low(kk - 1)

            def pool_tile(layer, kk, base):
                dve.wait_ge(hh_made, base + kk + 1)
                g = kk // 2
                src, width = hp[kk % 2], 1
                if kk == 0:
                    dve.wait_ge(stage_in, 16 * STAGE_IN[layer])
                for step in range(g + 1):
                    dst = win[step % 2]
                    c0 = 2 * width - 1
                    own.link(dve.tensor_tensor(dst[:, c0:POOL_W], src[:, c0:POOL_W],
                                               src[:, c0 - width:POOL_W - width], ALU.add))
                    src, width = dst, 2 * width
                ahead = width - width // 2 - 1
                pl = pooled[kk % 2]
                if kk >= 2:
                    dve.wait_ge(hl_made, base + kk - 1)
                own.link(dve.tensor_tensor(pl[:], src[:, POOL_PAD + ahead:POOL_W - POOL_PAD + ahead],
                                           inv_count[:, g, :], ALU.mult))
                dve.tensor_tensor(pl[:], pl[:], hp[kk % 2][:, POOL_PAD:POOL_W - POOL_PAD],
                                  ALU.subtract).then_inc(pool_made, 1)
                dve.wait_ge(pool_made, kk + 1)
                dve.wait_ge(ph_made, kk + 1)
                for at, n, cnd in STREAMS:
                    p0 = (POOL_LAT if cnd == 0 else POOL_CTX) - POOL_PAD
                    op = dve.tensor_tensor(h_lo[:, kk, at:at + n], pl[:, p0:p0 + n],
                                           h_hi[:, kk, at:at + n].bitcast(F32), ALU.subtract)
                op.then_inc(hl_made, 1)

            def update(u, par, o, gate):
                dve.wait_ge(unit_done, u + 1)
                for at, n, bank, col, cnd in ((1, NH - 1, 0, 1, 0), (NH, LAT + 1 - NH, 1, 0, 0),
                                              (CTX0, CTX, 1, CTX0 - NH, 1)):
                    if isinstance(o, int):
                        xt, gt = x[:, o, at:at + n], gate[:, o, cnd:cnd + 1]
                    else:
                        xt = x[:, bass.ds(o, 1), at:at + n].rearrange("p a n -> p (a n)")
                        gt = gate[:, bass.ds(o, 1), cnd]
                    op = dve.scalar_tensor_tensor(xt, ps[:, 2 * par + bank, col:col + n], gt, xt,
                                                  ALU.mult, ALU.add)
                op.then_inc(taken[par], 1)

            dve.wait_ge(const_in, 16 * len(CONSTS))
            own.link(dve.tensor_scalar(neg_sink[:], sink[:], -1.0, None, ALU.mult))
            for u in range(2):
                split_lo(u, u, units[u][0])
            for c in range(NCH):
                ada_copy(c)
                if c:
                    ada_add(c - 1, 0, CT * (c - 1))
            ada_add(NCH - 1, 0, CT * (NCH - 1))

            for layer, kind in enumerate(KINDS):
                u0 = UNIT0[layer]
                if kind == "pool":
                    dve.wait_ge(unit_done, u0)
                    for s in range(2):
                        dve.memset(hp[s][:, 0:POOL_LAT], 0.0)
                        dve.memset(hp[s][:, POOL_LAT + LAT:POOL_CTX], 0.0)
                        own.link(dve.memset(hp[s][:, POOL_CTX + CTX:POOL_W], 0.0))
                if kind == "fnet":
                    for n in range(11):
                        dve.wait_ge(tabh_made, n + 1)
                        dve.tensor_tensor(tab_lo[:, n, :], tab_raw[:], tab_hi[:, n, :].bitcast(F32),
                                          ALU.subtract).then_inc(tabl_made, 1)
                norm(layer, False)
                gate = pool_gate if kind == "pool" else mods[layer % 2][:, 16:16 + KT, :]
                if kind == "attn":
                    a = layer // 3
                    r0 = RMS0[layer] + 1
                    dve.wait_ge(stage_in, 16 * STAGE_IN[layer])

                    def rotate(n):
                        dve.wait_ge(rms_made, r0 + n + 1)
                        dve.reciprocal(rstd[:], rms[:]).then_inc(rstd_made, 1)
                        dve.wait_ge(rstd_made, r0 + n + 1)
                        wait_taken(dve, u0 + n)
                        own.link(dve.scalar_tensor_tensor(qkv[:, n, :], qkv[:, n, :],
                                                          head_gain[:, a, n // 8:n // 8 + 1], rstd[:],
                                                          ALU.mult, ALU.mult))
                        lat = qkv[:, n, LAT0:LAT0 + LAT]
                        own.link(dve.stream_shuffle(swapped[:], lat, [(p + 16) % 32 for p in range(32)]))
                        own.link(dve.tensor_tensor(swapped[:], swapped[:], rope_sin[:], ALU.mult))
                        own.link(dve.tensor_tensor(lat, lat, rope_cos[:], ALU.mult))
                        dve.tensor_tensor(lat, lat, swapped[:], ALU.add).then_inc(qk_ready, 1)
                        dve.wait_ge(qk_ready, 10 * a + n + 1)

                    for n in range(12):
                        split_next(u0 + n)
                        if 1 <= n <= 10:
                            rotate(n - 1)
                    for v in range(2):
                        dve.wait_ge(v_turned, 2 * a + v + 1)
                        dve.tensor_copy(v_tok[:, 0:4, v * P:(v + 1) * P],
                                        ps[:, 6, :].rearrange("p (b c) -> p b c", b=4))
                        dve.tensor_copy(v_tok[:, 4, v * P:(v + 1) * P], ps[:, 7, 0:P]).then_inc(v_ready, 1)
                    w0 = 40 * a

                    def masked(w):
                        nb, tile = WORK[w - w0]
                        ga, r = tile // 4, tile % 4
                        lo, hi = KEYS[nb]
                        hi = 512 if nb < 4 else hi
                        if w - w0 >= 2:
                            dve.wait_ge(t_done, 2 * (w - 1))
                        for hd in range(2):
                            dve.wait_ge(s_done, 2 * w + hd + 1)
                            st = stat[:, w % 2, hd, :]
                            own.link(dve.tensor_tensor_reduce(
                                out=prob[w % 2][hd][:, lo:hi], in0=ps[:, 2 * (w % 2) + hd, lo:hi],
                                in1=band[:, lo:hi], scale=1.0, scalar=-3e38, op0=ALU.add, op1=ALU.max,
                                accum_out=st[:, 0:1]))
                            head = 8 * ga + 4 * hd + r
                            dve.tensor_scalar(st[:, 1:2], st[:, 0:1], -(HD ** -0.5), neg_sink[:, a, head:head + 1],
                                              ALU.mult, ALU.min).then_inc(max_made, 1)

                    def normed(w):
                        nb, _ = WORK[w - w0]
                        lo, hi = KEYS[nb]
                        hi = 512 if nb < 4 else hi
                        dve.wait_ge(exp_made, 2 * w + 2)
                        st = stat[:, w % 2, :, :]
                        own.link(dve.tensor_tensor(st[:, :, 4:5], st[:, :, 2:3], st[:, :, 3:4], ALU.add))
                        own.link(dve.reciprocal(st[:, :, 5:6], st[:, :, 4:5]))
                        for hd in range(2):
                            dve.tensor_scalar(prob[w % 2][hd][:, lo:hi], prob[w % 2][hd][:, lo:hi],
                                              st[:, hd, 5:6], None, ALU.mult).then_inc(p_ready, 1)

                    def out_lo(w):
                        nb, tile = WORK[w - w0]
                        cols = slice(TOKEN_BLOCKS[nb], TOKEN_BLOCKS[nb] + P)
                        dve.wait_ge(oh_made, w + 1)
                        dve.tensor_tensor(h_lo[:, tile, cols], ps[:, 6 + w % 2, 0:P],
                                          h_hi[:, tile, cols].bitcast(F32), ALU.subtract).then_inc(ol_made, 1)

                    for w in range(w0, w0 + 43):
                        if w < w0 + 40:
                            masked(w)
                        if 1 <= w - w0 <= 40:
                            normed(w - 1)
                        if w - w0 >= 3:
                            out_lo(w - 3)
                    for n in range(12, 20):
                        update(u0 + n, n % 2, n - 12, gate)
                        split_next(u0 + n)
                else:
                    if kind == "fnet":
                        for g in range(4):
                            for tb in range(5):
                                dve.wait_ge(fth_made, 7 * g + tb + 1)
                                dve.tensor_tensor(ab_lo[:, tb, :], ps[:, 4 + tb % 4, :],
                                                  ab_hi[:, tb, :].bitcast(F32), ALU.subtract).then_inc(ftl_made, 1)
                            for c in range(2):
                                dve.wait_ge(fth_made, 7 * g + 5 + c + 1)
                                for at, n, cnd in STREAMS:
                                    op = dve.tensor_tensor(h_lo[:, 2 * g + c, at:at + n],
                                                           ps[:, 2 * c + cnd, 0:n],
                                                           h_hi[:, 2 * g + c, at:at + n].bitcast(F32), ALU.subtract)
                                op.then_inc(ftl_made, 1)
                    for n in range(KT):
                        update(u0 + n, n % 2, n, gate)
                        split_next(u0 + n)
                norm(layer, True)
                gate = mods[layer % 2][:, 40:40 + KT, :]
                last = layer + 1 == DEPTH
                if kind == "attn":
                    dve.wait_ge(out_sent, 32 * (layer // 3 + 1))

                def up_step(u, par, half_u, v, pair, tile, k_next, c=None, c_tile=None, c_end=None, c_end_tile=None):
                    isint = isinstance(v, int)
                    cw = (lambda n: conv[:, v, n:n + 1]) if isint else (lambda n: conv[:, bass.ds(v, 1), n])
                    dve.wait_ge(taken[par], half_u + 1)
                    own.link(dve.scalar_tensor_tensor(conv_out[par][:], u_pad[par][:, 0:NT], cw(0),
                                                      conv_out[par][:], ALU.mult, ALU.add))
                    dve.scalar_tensor_tensor(conv_out[par][:], u_pad[par][:, 2:NT + 2], cw(2), conv_out[par][:],
                                             ALU.mult, ALU.add).then_inc(conv_done, 1)
                    split_lo(u + 2, par, k_next)
                    if par == 0:
                        if c is not None:
                            ada_copy(c)
                    else:
                        dve.wait_ge(silu_made, pair + 1)
                        dve.wait_ge(conv_done, v + 3)
                        dve.wait_ge(fl_made, pair + 1)
                        dve.tensor_tensor(prod[:], gate_act[:], conv_out[1][:], ALU.mult).then_inc(prod_made, 1)
                        dve.wait_ge(prod_made, pair + 2)
                        if isint:
                            fh, fl = f_hi[:, tile, :], f_lo[:, tile, :]
                        else:
                            fh, fl = (ff[:, bass.ds(tile, 1), :].rearrange("p a n -> p (a n)") for ff in (f_hi, f_lo))
                        own.link(dve.tensor_scalar(fh, prod[:], 1.0, None, ALU.mult))
                        dve.tensor_tensor(fl, prod[:], fh.bitcast(F32), ALU.subtract).then_inc(fl_made, 1)
                        if c is not None:
                            ada_add(c, layer + 1, c_tile)
                        if c_end is not None:
                            ada_copy(c_end)

                for half in range(2):
                    ub = u0 + MIX_UNITS[kind] + half * (2 * HALF + KT)
                    v0 = (2 * layer + half) * 2 * HALF
                    ch = half * NCH // 2
                    c0 = NCH * (layer + 1) + ch
                    with dve.Fori(0, HALF // 2) as i:
                        own.enter(i, 6)
                        for n in range(4):
                            up_step(i * 4 + (ub + n), n % 2, i * 2 + (ub + n) // 2, i * 4 + (v0 + n),
                                    i * 2 + (v0 + n) // 2,
                                    i * 2 + n // 2, KT, None if last else i * 2 + (c0 + n // 2),
                                    i * (2 * CT) + CT * (ch + n // 2))
                    own.leave(HALF // 2)
                    for n in range(2 * HALF - 2, 2 * HALF):
                        c = c0 + HALF - 1
                        up_step(ub + n, n % 2, (ub + n) // 2, v0 + n, (v0 + n) // 2, n // 2, HALF, None if last else c,
                                CT * (ch + HALF - 1), None if last else c + 1)
                    ud = ub + 2 * HALF
                    for n in range(2):
                        update(ud + n, n, n, gate)
                        split_next(ud + n)
                        if n == 0 and not last:
                            ada_add(c0 + HALF, layer + 1, CT * (ch + HALF))
                    with dve.Fori(0, KT // 2 - 2) as i:
                        for n in range(2):
                            update(i * 2 + (ud + 2 + n), n, i * 2 + (2 + n), gate)
                            split_lo(i * 2 + (ud + 4 + n), n, HALF)
                    for n in range(KT - 2, KT):
                        update(ud + n, n % 2, n, gate)
                        split_next(ud + n)


def shape_constants():
    f = np.float32
    p = np.arange(P)
    tok = np.arange(LAT)
    d = p % HD
    pos = np.where((d // 32 == 0)[:, None], (tok // 64)[None], (tok % 64)[None]).astype(f)
    inv_freq = (1.0 / (f(10000.0) ** (np.arange(0, 32, 2, dtype=f) / f(32)))).astype(f)
    angle = pos * inv_freq[d % 16][:, None]
    sign = np.where(d % 32 < 16, -1.0, 1.0)[:, None]
    q, k = np.arange(P)[:, None], np.arange(P)[None]
    band = np.zeros((P, 512), f)
    band[:, 0:128] = np.where(k >= q, 0.0, NEG)
    band[:, 256:384] = np.where(k <= q, 0.0, NEG)
    inv = np.zeros((4, POOL_W - 2 * POOL_PAD), f)
    for g, w in enumerate(WINDOWS):
        for n, at in ((LAT, POOL_LAT), (CTX, POOL_CTX)):
            tt = np.arange(n)
            count = np.clip(tt + w - w // 2, 0, n) - np.clip(tt - w // 2, 0, n)
            inv[g, at - POOL_PAD:at - POOL_PAD + n] = 1.0 / count
    dft = np.zeros((11, P, 512), f)
    ang = 2 * np.pi * ((tok[:, None] * tok[None]) % LAT) / LAT
    dft[0:4] = (np.cos(ang) / np.sqrt(LAT * 256.0)).reshape(4, P, LAT)
    dft[4:8] = (-np.sin(ang) / np.sqrt(LAT * 256.0)).reshape(4, P, LAT)
    ch = np.arange(256)
    ang = 2 * np.pi * ((ch[:, None] * ch[None]) % 256) / 256
    dft[8:10] = np.concatenate([np.cos(ang), np.sin(ang)], 1).reshape(2, P, 512)
    ang = 2 * np.pi * ((p[:, None] * p[None]) % CTX) / CTX
    dft[10, :, 0:128] = np.cos(ang) / np.sqrt(CTX * 256.0)
    dft[10, :, 128:256] = -np.sin(ang) / np.sqrt(CTX * 256.0)
    pick = np.zeros((P, 2), f)
    for j in range(4):
        pick[32 * j, 0] = pick[32 * j + 1, 1] = 1.0
    return {
        "rope_cos": np.cos(angle).astype(f), "rope_sin": (sign * np.sin(angle)).astype(f), "band": band,
        "inv_count": np.broadcast_to(inv, (P,) + inv.shape), "dft": dft, "pick": pick,
        "ones_head": (p[:, None] // HD == p[None] // HD).astype(f), "ident": np.eye(P, dtype=f),
    }


def lay_out(i):
    def token_columns(lat, ctx_rows):
        out = np.zeros((P, KT, NT), np.float32)
        for rows, at in ((lat, LAT0), (ctx_rows, CTX0)):
            out[:, :, at:at + len(rows)] = rows.T.reshape(KT, P, len(rows)).transpose(1, 0, 2)
        return out

    def unit_rows(w, k):
        lead = w.shape[:-2]
        n = w.shape[-1] // P
        w = w.reshape(lead + (k, P, n, P))
        w = np.moveaxis(w, (-2, -3), (len(lead), len(lead) + 1))
        return w.reshape(-1, P, k * P)

    def column(v):
        v = v.reshape(v.shape[:-1] + (-1, P))
        return np.moveaxis(v, -1, 0)

    def twice(v):
        return np.repeat(v[..., None], 2, -1)

    cond = np.zeros((P, KT, 32), np.float32)
    cond[:, :, 0] = i["c"][0].reshape(KT, P).T
    cond[:, :, 1] = i["c_ctx"].reshape(KT, P).T
    heads = [8 * (tl // 4) + 4 * hd + tl % 4 for tl in range(KT) for hd in range(2)]
    qcols = np.concatenate([np.arange(HD * h, HD * h + HD) for h in heads])
    cols = np.concatenate([qcols, np.arange(D, D + 512)])
    pairs = [n for j in range(FT) for n in (j, FT + j)]
    w_in = unit_rows(i["ffn_w_in"], KT).reshape(DEPTH, 2 * FT, P, KT * P)[:, pairs].reshape(-1, P, KT * P)
    conv = np.concatenate([i["ffn_conv_w"], i["ffn_conv_b"][:, None]], 1)
    conv = column(conv)[:, :, :, pairs].transpose(0, 1, 3, 2).reshape(P, DEPTH * 2 * FT, 4)
    head_gain = np.stack([np.tile(i["attn_q_norm"], (1, 2)), np.tile(i["attn_k_norm"], (1, 2))], -1)
    ck = i["cache_k"][0].reshape(2, P, 2, P).transpose(0, 3, 2, 1)
    out = {
        "x": token_columns(i["x_sample"][0], i["x_prompt"][0]),
        "cond": cond,
        "ada_w": i["ada_w"].reshape(DEPTH, KT, P, NCH, AW).transpose(0, 3, 2, 1, 4).reshape(-1, P, KT * AW),
        "ada_bias": twice(column(i["ada_b"])),
        "gains": twice(np.stack([column(i["norm_mix"]), column(i["norm_ffn"])], 2)),
        "pool_scale": twice(column(i["pool_scale"])[:, 0]),
        "w_qkv": unit_rows(i["attn_w_qkv"][:, :, cols], KT),
        "w_o": unit_rows(i["attn_w_o"][:, qcols], KT),
        "w_pool": unit_rows(i["pool_w"][0], 2),
        "w_fnet": unit_rows(i["fnet_w"], KT),
        "w_in": w_in,
        "w_out": unit_rows(i["ffn_w_out"].reshape(DEPTH, 2, HALF * P, D), HALF),
        "conv": conv,
        "head_gain": head_gain.transpose(1, 0, 2),
        "sink": np.broadcast_to(i["attn_sink"], (P, 2, NHEADS)),
        "cache_k": ck,
        "cache_v": i["cache_v"][0].reshape(2, P, 256),
    }
    return out


def kernel(**inputs):
    import concourse.bacc as bacc
    from concourse.bass_utils import run_bass_kernel_spmd

    arrays = lay_out({k: np.asarray(v) for k, v in inputs.items()})
    arrays.update(shape_constants())
    arrays = {f"in_{k}": np.ascontiguousarray(v) for k, v in arrays.items()}
    nc = bacc.Bacc("TRN2", target_bir_lowering=False, num_devices=1)
    t = {k[3:]: nc.dram_tensor(k, v.shape, F32, kind="ExternalInput").ap() for k, v in arrays.items()}
    for name, shape in (("y", (P, KT, NT)), ("new_k", (2, P, 2, CTX)), ("new_v", (2, P, 2, CTX))):
        t[name] = nc.dram_tensor(f"out_{name}", shape, F32, kind="ExternalOutput").ap()
    build(nc, t)
    r = run_bass_kernel_spmd(nc, [arrays], core_ids=[0]).results[0]
    y = r["out_y"].transpose(1, 0, 2).reshape(D, NT)
    caches = [r[f"out_{n}"].transpose(0, 3, 2, 1).reshape(1, 2, CTX, 4, HD) for n in ("new_k", "new_v")]
    return (np.ascontiguousarray(y[:, CTX0:CTX0 + CTX].T)[None], np.ascontiguousarray(y[:, LAT0:LAT0 + LAT].T)[None],
            np.ascontiguousarray(caches[0]), np.ascontiguousarray(caches[1]))
```

```python
from contextlib import ExitStack

import numpy as np

import concourse.bass as bass
from concourse import mybir

F32 = mybir.dt.float32
F32R = mybir.dt.float32r
ALU = mybir.AluOpType
ACT = mybir.ActivationFunctionType

P = 128
D = 1024
KT = D // P
LAT, CTX = 512, 128
LAT0, CTX0 = 1, 514
NT = 644
NH = NT // 2
DEPTH = 4
KINDS = ("attn", "pool", "fnet", "attn")
HD = 64
NHEADS = 16
FF = 2816
FT = FF // P
HALF = FT // 2
AW = 256
NCH = 6 * D // AW
CT = AW // P
EPS = 1e-6
NEG = -1e30
POOL_PAD = 8
POOL_W = 672
POOL_LAT, POOL_CTX = 8, 536
WINDOWS = (2, 4, 8, 16)

MIX_UNITS = {"attn": 20, "pool": 8, "fnet": 8}
FFN_UNITS = 2 * (2 * HALF + KT)
FIRST_CHUNKS = 2 * D // AW
SH0 = NT - 2
UNIT0 = [sum(MIX_UNITS[k] + FFN_UNITS for k in KINDS[:i]) for i in range(DEPTH + 1)]
SQ0 = [sum(2 * KT + (10 if k == "attn" else 0) for k in KINDS[:i]) for i in range(DEPTH)]
RMS0 = [sum(2 + (10 if k == "attn" else 0) for k in KINDS[:i]) for i in range(DEPTH)]
STREAMS = ((LAT0, LAT, 0), (CTX0, CTX, 1))


class Chain:

    def __init__(self, eng, sem):
        self.eng, self.sem, self.n, self.off = eng, sem, 0, 0

    def link(self, ins):
        self.n += 1
        ins.then_inc(self.sem, 1)
        self.eng.wait_ge(self.sem, self.n + self.off)

    def enter(self, i, per):
        self.off, self.start, self.per = i * per, self.n, per

    def leave(self, iterations):
        assert self.n - self.start == self.per
        self.off, self.n = 0, self.start + self.per * iterations


def build(nc, t):
    with ExitStack() as ctx:
        def sb(name, shape, dt=F32, stack=None):
            return (stack or ctx).enter_context(nc.sbuf_tensor(name, shape, dt))

        def sem(name):
            return ctx.enter_context(nc.semaphore(name))

        x = sb("x", [P, KT, NT])
        h_hi = sb("h_hi", [P, KT, NT], F32R)
        h_lo = sb("h_lo", [P, KT, NT], F32R)
        w_raw = [sb(f"w_raw{s}", [P, HALF, P]) for s in range(2)]
        w_hi = [sb(f"w_hi{s}", [P, HALF, P], F32R) for s in range(2)]
        w_lo = [sb(f"w_lo{s}", [P, HALF, P], F32R) for s in range(2)]
        ada_w = [sb(f"ada_w{s}", [P, KT, AW]) for s in range(2)]
        ada_rows = sb("ada_rows", [P, AW])
        cond = sb("cond", [P, KT, 32])
        cond_act = sb("cond_act", [P, KT, 32])
        mods = [sb(f"mods{s}", [P, 48, 2]) for s in range(2)]
        ada_bias = sb("ada_bias", [P, DEPTH, 48, 2])
        gains = sb("gains", [P, DEPTH, 2, KT, 2])
        gain_now = sb("gain_now", [P, KT, 2])
        pool_scale = sb("pool_scale", [P, KT, 2])
        pool_gate = sb("pool_gate", [P, KT, 2])
        conv = sb("conv", [P, DEPTH * 2 * FT, 4])
        head_gain = sb("head_gain", [P, 2, 2])
        sink = sb("sink", [P, 2, NHEADS])
        neg_sink = sb("neg_sink", [P, 2, NHEADS])
        ones = sb("ones", [P, 1])
        two_heads = sb("two_heads", [P, 2])
        ident = sb("ident", [P, P])
        pick = sb("pick", [P, 2])
        eps = sb("eps", [P, 1])
        u_pad = [sb(f"u_pad{s}", [P, NT + 2]) for s in range(2)]

        rstd = sb("rstd", [P, NT])
        rms = sb("rms", [P, 5, 2])
        inv_rms = sb("inv_rms", [P, 5, 2])

        with ExitStack() as a:
            sq = [sb(f"sq{s}", [P, NT], F32, a) for s in range(2)]
            sq_sum = sb("sq_sum", [P, NT], F32, a)
            inv_wide = sb("inv_wide", [P, 5, P], F32, a)
            sb("unused", [P, NT - 5 * P], F32, a)
            xn = [sb(f"xn{s}", [P, NT], F32, a) for s in range(2)]
        with ExitStack() as a:
            conv_out = [sb(f"conv_out{s}", [P, NT], F32, a) for s in range(2)]
            gate_act = sb("gate_act", [P, NT], F32, a)
            prod = sb("prod", [P, NT], F32, a)
            scaled = [sb(f"scaled{s}", [P, NT], F32, a) for s in range(2)]
        tmp_store = sb("tmp_store", [P, 6 * (NT + 12)])

        with ExitStack() as a:
            f_hi = sb("f_hi", [P, HALF, NT], F32R, a)
            f_lo = sb("f_lo", [P, HALF, NT], F32R, a)
        with ExitStack() as a:
            qkv = sb("qkv", [P, 12, NT], F32, a)
            v_tok = sb("v_tok", [P, 5, 256], F32, a)
            ck = sb("ck", [P, 2, P], F32, a)
            cv = sb("cv", [P, 256], F32, a)
            rope_cos = sb("rope_cos", [P, LAT], F32, a)
            rope_sin = sb("rope_sin", [P, LAT], F32, a)
            band = sb("band", [P, 512], F32, a)
            swapped = sb("swapped", [P, LAT], F32, a)
            prob = [[sb(f"prob{s}{hd}", [P, 512], F32, a) for hd in range(2)] for s in range(2)]
            probT = [[sb(f"probT{s}{hd}", [P, 512], F32, a) for hd in range(2)] for s in range(2)]
            stat = sb("stat", [P, 2, 2, 8], F32, a)
        with ExitStack() as a:
            hp = [sb(f"hp{s}", [P, POOL_W], F32, a) for s in range(2)]
            win = [sb(f"win{s}", [P, POOL_W], F32, a) for s in range(2)]
            inv_count = sb("inv_count", [P, 4, POOL_W - 16], F32, a)
            pooled = [sb(f"pooled{s}", [P, POOL_W - 16], F32, a) for s in range(2)]
        with ExitStack() as a:
            tab_hi = sb("tab_hi", [P, 11, 512], F32R, a)
            tab_lo = sb("tab_lo", [P, 11, 512], F32R, a)
            with ExitStack() as b:
                ab_hi = sb("ab_hi", [P, 5, 512], F32R, b)
                ab_lo = sb("ab_lo", [P, 5, 512], F32R, b)
            tab_raw = sb("tab_raw", [P, 10, 512], F32, a)
        stage_store = sb("stage_store", [P, 64 * 256 + 64])
        assert stage_store is not None and tmp_store is not None

        ps = ctx.enter_context(nc.psum_tensor("ps", [P, 8, 512], F32))
        INV_LAT, INV_CTX, ADA_ROWS, ADA_COLS = 4, 5, 6, 7
        SUMS = slice(256, 266)
        Q0, K0, V0 = 4, 2, 0

        const_in = sem("const_in")
        x_in = sem("x_in")
        stage_in = sem("stage_in")
        raw_in = [sem(f"raw_in{s}") for s in range(2)]
        hi_made = sem("hi_made")
        lo_made = sem("lo_made")
        unit_done = sem("unit_done")
        taken = [sem(f"taken{s}") for s in range(2)]
        setup_done = sem("setup_done")
        sq_made = sem("sq_made")
        sq_added = sem("sq_added")
        sum_done = sem("sum_done")
        heads_summed = sem("heads_summed")
        inv_made = sem("inv_made")
        inv_small = sem("inv_small")
        inv_turned = sem("inv_turned")
        qk_normed = sem("qk_normed")
        gain_made = sem("gain_made")
        qkv_out = sem("qkv_out")
        u_padded = sem("u_padded")
        conv_init = sem("conv_init")
        rms_made = sem("rms_made")
        rstd_made = sem("rstd_made")
        xn_made = sem("xn_made")
        hh_made = sem("hh_made")
        hl_made = sem("hl_made")
        cond_made = sem("cond_made")
        ada_in = [sem(f"ada_in{s}") for s in range(2)]
        ada_mm = sem("ada_mm")
        ada_row = sem("ada_row")
        ada_col = sem("ada_col")
        ada_done = sem("ada_done")
        conv_done = sem("conv_done")
        silu_made = sem("silu_made")
        prod_made = sem("prod_made")
        fl_made = sem("fl_made")
        qk_ready = sem("qk_ready")
        v_turned = sem("v_turned")
        v_ready = sem("v_ready")
        s_done = sem("s_done")
        max_made = sem("max_made")
        exp_made = sem("exp_made")
        p_ready = sem("p_ready")
        t_done = sem("t_done")
        pt_made = sem("pt_made")
        o_done = sem("o_done")
        oh_made = sem("oh_made")
        ol_made = sem("ol_made")
        pool_made = sem("pool_made")
        ph_made = sem("ph_made")
        tab_in = [sem(f"tab_in{s}") for s in range(2)]
        tabh_made = sem("tabh_made")
        tabl_made = sem("tabl_made")
        ft_mm = sem("ft_mm")
        fth_made = sem("fth_made")
        ftl_made = sem("ftl_made")
        out_sent = sem("out_sent")
        dve_own = sem("dve_own")

        def wait_taken(eng, u):
            eng.wait_ge(taken[u % 2], u // 2 + 1)

        def sq_base(layer, second):
            return SQ0[layer] + (KT + (10 if KINDS[layer] == "attn" else 0) if second else 0)

        def rms_base(layer, second):
            return RMS0[layer] + (1 + (10 if KINDS[layer] == "attn" else 0) if second else 0)

        def last_update(layer, second, kk):
            return UNIT0[layer] + (MIX_UNITS[KINDS[layer]] if second else 0) - KT + kk

        def explicit(layer, second):
            return KINDS[layer] in ("pool", "fnet") and not second

        def halves(ap):
            return ap.rearrange("p (a b) -> p a b", a=2)

        def product(s):
            return ps[:, 2 * s:2 * s + 2, 0:NH]

        units = []
        for layer, kind in enumerate(KINDS):
            if kind == "attn":
                a = layer // 3
                units += [(KT, t["w_qkv"], 12 * a + n) for n in range(12)]
                units += [(KT, t["w_o"], KT * a + n) for n in range(KT)]
            elif kind == "pool":
                units += [(2, t["w_pool"], n) for n in range(KT)]
            else:
                units += [(KT, t["w_fnet"], n) for n in range(KT)]
            for half in range(2):
                units += [(KT, t["w_in"], (2 * layer + half) * 2 * HALF + n) for n in range(2 * HALF)]
                units += [(HALF, t["w_out"], (2 * layer + half) * KT + n) for n in range(KT)]
        assert len(units) == UNIT0[DEPTH]

        CONSTS = ((cond, "cond"), (ada_bias, "ada_bias"), (gains, "gains"), (pool_scale, "pool_scale"),
                  (pick, "pick"), (two_heads, "two_heads"), (ident, "ident"), (conv, "conv"),
                  (head_gain, "head_gain"), (sink, "sink"))
        JOINED = ((LAT0, CTX0 - LAT0, 0), (CTX0, CTX, 1))
        PADS = ((0, LAT0), (LAT0 + LAT, 1), (CTX0 + CTX, NT - CTX0 - CTX))
        N_SETUP = 5 + 2 * len(PADS)
        STAGE_IN = (5, 6, 6, 11)
        TOKEN_BLOCKS = [LAT0 + P * n for n in range(LAT // P)] + [CTX0]
        KEYS = ((128, 384), (0, 384), (0, 384), (0, 256), (128, 256))
        BLOCKS = ((1, 2, 3), (0, 1, 2, 3), (0, 1, 2, 3), (0, 1, 3), (1,))
        WORK = [(nb, tile) for nb in range(5) for tile in range(KT)]

        block = ctx.enter_context(nc.Block())

        @block.sync
        def _(sp):
            def load_unit(u, par, k, src):
                if not isinstance(u, int) or u >= 2:
                    sp.wait_ge(lo_made, u - 1)
                sp.dma_start(w_raw[par][:, 0:k, :], src).then_inc(raw_in[par], 16)

            def load_units(u0, n):
                for u in range(u0, u0 + n):
                    k, arr, row = units[u]
                    load_unit(u, u % 2, k, arr[row].rearrange("p (k c) -> p k c", k=k))

            def load_chunk(c, par, src):
                if not isinstance(c, int) or c >= 2:
                    sp.wait_ge(ada_mm, c - 1)
                sp.dma_start(ada_w[par][:], src).then_inc(ada_in[par], 16)

            def chunk_rows(c):
                return t["ada_w"][c].rearrange("p (k c) -> p k c", k=KT)

            def looped(arr, k, row):
                return arr[bass.ds(row, 1)].rearrange("a p (k c) -> p (a k) c", k=k)

            for dst, src in CONSTS:
                sp.dma_start(dst[:], t[src]).then_inc(const_in, 16)
            load_units(0, 2)
            for c in range(2):
                load_chunk(c, c, chunk_rows(c))
            sp.dma_start(x[:], t["x"]).then_inc(x_in, 16)
            for c in range(2, FIRST_CHUNKS):
                load_chunk(c, c % 2, chunk_rows(c))

            for layer, kind in enumerate(KINDS):
                u0 = UNIT0[layer]
                if layer:
                    load_units(u0, 2)
                    sp.wait_ge(unit_done, u0)
                a = layer // 3
                if kind == "attn":
                    for dst, src in ((rope_cos[:], t["rope_cos"]), (rope_sin[:], t["rope_sin"]),
                                     (band[:], t["band"]), (ck[:], t["cache_k"][a]), (cv[:], t["cache_v"][a])):
                        sp.dma_start(dst, src).then_inc(stage_in, 16)
                elif kind == "pool":
                    sp.dma_start(inv_count[:], t["inv_count"]).then_inc(stage_in, 16)
                else:
                    for n in range(2):
                        sp.dma_start(tab_raw[:, 5 * n:5 * n + 5, :],
                                     t["dft"][5 * n:5 * n + 5].rearrange("k p c -> p k c")).then_inc(tab_in[n], 16)
                    sp.wait_ge(tabl_made, 1)
                    sp.dma_start(tab_raw[:, 0, :], t["dft"][10]).then_inc(tab_in[0], 16)
                for n in range(MIX_UNITS[kind]):
                    if n >= 2:
                        load_units(u0 + n, 1)
                    if layer == 0 and FIRST_CHUNKS + n < NCH:
                        load_chunk(FIRST_CHUNKS + n, n % 2, chunk_rows(FIRST_CHUNKS + n))
                if kind == "attn":
                    sp.wait_ge(qk_ready, 10 * (a + 1))
                    sp.wait_ge(qkv_out, 12 * (a + 1))
                    sp.dma_start(t["new_k"][a], qkv[:, K0:K0 + 2, CTX0:CTX0 + CTX]).then_inc(out_sent, 16)
                    sp.dma_start(t["new_v"][a], qkv[:, V0:V0 + 2, CTX0:CTX0 + CTX]).then_inc(out_sent, 16)
                for half in range(2):
                    ub = u0 + MIX_UNITS[kind] + half * (2 * HALF + KT)
                    up_row = (2 * layer + half) * 2 * HALF
                    c0 = NCH * (layer + 1) + half * NCH // 2
                    with sp.Fori(0, HALF // 2) as i:
                        for n in range(4):
                            load_unit(i * 4 + (ub + n), n % 2, KT, looped(t["w_in"], KT, i * 4 + (up_row + n)))
                            if n % 2 and layer + 1 < DEPTH:
                                c = i * 2 + (c0 + n // 2)
                                load_chunk(c, n // 2, looped(t["ada_w"], KT, c))
                    load_units(ub + 2 * HALF - 2, 2)
                    if layer + 1 < DEPTH:
                        for c in range(c0 + HALF - 1, c0 + HALF + 1):
                            load_chunk(c, c % 2, chunk_rows(c))
                    with sp.Fori(0, KT // 2) as i:
                        for n in range(2):
                            load_unit(i * 2 + (ub + 2 * HALF + n), n, HALF,
                                      looped(t["w_out"], HALF, i * 2 + ((2 * layer + half) * KT + n)))
            for o in range(KT):
                wait_taken(sp, UNIT0[DEPTH] - KT + o)
                sp.dma_start(t["y"][:, o, :], x[:, o, :]).then_inc(out_sent, 16)
            sp.wait_ge(out_sent, 16 * (4 + KT))

        @block.gpsimd
        def _(pool):
            pool.memset(ones[:], 1.0).then_inc(setup_done, 1)
            pool.memset(eps[:], EPS).then_inc(setup_done, 1)
            pool.sem_inc(conv_done, 2)
            pool.sem_inc(prod_made, 1)
            pool.sem_inc(fl_made, 1)
            for s in range(2):
                pool.memset(u_pad[s][:], 0.0).then_inc(setup_done, 1)
            pool.memset(rstd[:], 1.0).then_inc(setup_done, 1)
            for hx in (h_hi, h_lo):
                for a0, n in PADS:
                    pool.memset(hx[:, :, a0:a0 + n].bitcast(F32), 0.0).then_inc(setup_done, 1)
            for layer in range(DEPTH):
                for second in (False, True):
                    m = 2 * layer + second
                    for kk in range(1, KT):
                        pool.wait_ge(sq_made, sq_base(layer, second) + kk + 1)
                        if kk > 1:
                            pool.wait_ge(sq_added, (KT - 1) * m + kk - 1)
                        pool.tensor_tensor(sq_sum[:], sq_sum[:], sq[kk % 2][:], ALU.add).then_inc(sq_added, 1)

        @block.tensor
        def _(pe):
            def unit(u, par, k, rhs, ready=None, prior=None, middle=None):
                pe.wait_ge(lo_made, u + 1)
                if prior is None or not isinstance(prior, int) or prior > 0:
                    pe.wait_ge(taken[par], prior)
                for kk in range(k):
                    if middle and kk == k // 2:
                        middle()
                    if ready:
                        ready(kk)
                    b_hi, b_lo = rhs(kk)
                    for n, (w, b) in enumerate(((w_hi, b_hi), (w_hi, b_lo), (w_lo, b_hi))):
                        for hf in range(2):
                            mm = pe.matmul(ps[:, 2 * par + hf, 0:NH], w[par][:, kk, :],
                                           b[:, hf * NH:(hf + 1) * NH],
                                           start=(kk == 0 and n == 0), stop=(kk == k - 1 and n == 2))
                mm.then_inc(unit_done, 1)

            def h_tiles(kk):
                return h_hi[:, kk, :], h_lo[:, kk, :]

            def f_tiles(kk):
                return f_hi[:, kk, :], f_lo[:, kk, :]

            def unit_pair(u, layer, second):
                pe.wait_ge(lo_made, u + 2)
                if u:
                    wait_taken(pe, u - 2)
                    wait_taken(pe, u - 1)
                for kk in range(KT):
                    pe.wait_ge(hl_made, KT * (2 * layer + second) + kk + 1)
                    for s in range(2):
                        for n, (w, b) in enumerate(((w_hi, h_hi), (w_hi, h_lo), (w_lo, h_hi))):
                            for hf in range(2):
                                mm = pe.matmul(ps[:, 2 * s + hf, 0:NH], w[s][:, kk, :],
                                               b[:, kk, hf * NH:(hf + 1) * NH],
                                               start=(kk == 0 and n == 0), stop=(kk == KT - 1 and n == 2))
                        if kk == KT - 1:
                            mm.then_inc(unit_done, 1)
                    if kk == KT // 2:
                        sum_squares(layer, second)
                turn_back(rms_base(layer, second))

            def block_sums(src, sel, cols):
                for tb in range(5):
                    at = TOKEN_BLOCKS[tb]
                    c0 = SUMS.start + 2 * tb
                    mm = pe.matmul(ps[:, INV_CTX, c0:c0 + cols], src[:, at:at + P], sel, start=True, stop=True)
                return mm

            def turn_back(r):
                pe.wait_ge(inv_made, r + 1)
                for tb in range(5):
                    out = ps[:, INV_LAT, tb * P:(tb + 1) * P] if tb < 4 else ps[:, INV_CTX, 0:P]
                    mm = pe.transpose(out, inv_wide[:, tb, :], ident[:])
                mm.then_inc(inv_turned, 1)

            def sum_squares(layer, second):
                m = 2 * layer + second
                pe.wait_ge(sq_added, (KT - 1) * (m + 1))
                if m:
                    pe.wait_ge(rstd_made, m)
                if second and KINDS[layer] == "attn":
                    pe.wait_ge(ol_made, 40 * (layer // 3 + 1))
                block_sums(sq_sum, ones[:], 1).then_inc(sum_done, 1)

            def sum_heads(layer, i):
                a = layer // 3
                pe.wait_ge(sq_made, SQ0[layer] + KT + i + 1)
                pe.wait_ge(rstd_made, 2 * layer + 1)
                if i:
                    pe.wait_ge(qk_normed, 10 * a + i)
                block_sums(sq[i % 2], two_heads[:], 2).then_inc(heads_summed, 1)

            def turn_heads(layer, i):
                turn_back(RMS0[layer] + 1 + i)

            def ada_multiply(c, par, turn):
                pe.wait_ge(ada_in[par], turn * 16 + 16)
                if not isinstance(c, int) or c >= 1:
                    pe.wait_ge(ada_row, c)
                for r in range(2):
                    for j in range(4):
                        mm = pe.matmul(ps[32 * j:32 * j + 32, ADA_ROWS, 0:AW], cond_act[:, 4 * r + j, :],
                                       ada_w[par][:, 4 * r + j, :], start=(r == 0), stop=(r == 1),
                                       skip_group_check=True)
                mm.then_inc(ada_mm, 1)

            def ada_turn(c):
                pe.wait_ge(ada_row, c + 1)
                if not isinstance(c, int) or c >= 1:
                    pe.wait_ge(ada_done, c)
                for n in range(CT):
                    mm = pe.matmul(ps[:, ADA_COLS, 2 * n:2 * n + 2], ada_rows[:, n * P:(n + 1) * P], pick[:],
                                   start=True, stop=True)
                mm.then_inc(ada_col, 1)

            pe.wait_ge(const_in, 16 * len(CONSTS))
            pe.wait_ge(setup_done, N_SETUP)
            pe.wait_ge(cond_made, 1)
            for c in range(FIRST_CHUNKS):
                ada_multiply(c, c % 2, c // 2)
                if c:
                    ada_turn(c - 1)
            ada_turn(FIRST_CHUNKS - 1)

            for layer, kind in enumerate(KINDS):
                u0 = UNIT0[layer]
                def first_layers_chunk(n):
                    c = FIRST_CHUNKS + n
                    if layer == 0 and c < NCH:
                        ada_multiply(c, c % 2, c // 2)
                    if layer == 0 and n and c - 1 < NCH:
                        ada_turn(c - 1)

                if explicit(layer, False):
                    sum_squares(layer, False)
                    turn_back(rms_base(layer, False))
                if kind == "attn":
                    a = layer // 3
                    unit_pair(u0, layer, False)
                    first_layers_chunk(0)
                    for n in range(1, 12):
                        if n >= 2:
                            unit(u0 + n, n % 2, KT, h_tiles, None, (u0 + n) // 2,
                                 (lambda: sum_heads(layer, n - 3)) if n >= 3 else None)
                        first_layers_chunk(n)
                        if n >= 3:
                            turn_heads(layer, n - 3)
                    if layer == 0:
                        ada_turn(FIRST_CHUNKS + 11)
                        pe.wait_ge(ada_done, FIRST_CHUNKS + 12)
                    sum_heads(layer, 9)
                    for v in range(2):
                        if v or a:
                            pe.wait_ge(v_ready, 2 * a + v)
                        for tb in range(5):
                            at = TOKEN_BLOCKS[tb]
                            mm = pe.transpose(ps[:, 6 + tb // 4, (tb % 4) * P:(tb % 4 + 1) * P],
                                              qkv[:, V0 + v, at:at + P], ident[:])
                        mm.then_inc(v_turned, 1)
                        if v == 0:
                            turn_heads(layer, 9)
                    pe.wait_ge(v_ready, 2 * (a + 1))
                    pe.wait_ge(stage_in, 16 * STAGE_IN[layer])
                    w0 = 40 * a

                    def scores(w):
                        nb, tile = WORK[w - w0]
                        ga = tile // 4
                        if w - w0 >= 2:
                            pe.wait_ge(max_made, 2 * (w - 1))
                        pe.wait_ge(qk_ready, 10 * a + tile + 3)
                        for hd in range(2):
                            rows = slice(HD * hd, HD * hd + HD)
                            q = qkv[rows, Q0 + tile, TOKEN_BLOCKS[nb]:TOKEN_BLOCKS[nb] + P]
                            out = ps[:, 2 * (w % 2) + hd, :]
                            lo, hi = KEYS[nb]
                            first = TOKEN_BLOCKS[nb] + lo - P
                            mm = pe.matmul(out[:, lo:hi], q, qkv[rows, K0 + ga, first:first + hi - lo],
                                           start=True, stop=True)
                            if nb < 4:
                                mm = pe.matmul(out[:, 384:512], q, ck[rows, ga, :], start=True, stop=True)
                            mm.then_inc(s_done, 1)

                    def turn(w):
                        nb, _ = WORK[w - w0]
                        for hd in range(2):
                            pe.wait_ge(p_ready, 2 * w + hd + 1)
                            if w == w0:
                                pe.wait_ge(qk_normed, 10 * (a + 1))
                            if w - w0 >= 1:
                                pe.wait_ge(pt_made, 2 * (w - 1) + hd + 1)
                            for b in BLOCKS[nb]:
                                mm = pe.transpose(ps[:, 4 + hd, b * P:(b + 1) * P],
                                                  prob[w % 2][hd][:, b * P:(b + 1) * P], ident[:])
                            mm.then_inc(t_done, 1)

                    def values(w):
                        nb, tile = WORK[w - w0]
                        ga = tile // 4
                        if w - w0 >= 2:
                            pe.wait_ge(ol_made, w - 1)
                        pe.wait_ge(pt_made, 2 * w + 2)
                        for b in BLOCKS[nb]:
                            for hd in range(2):
                                kv = slice(HD * (2 * ga + hd), HD * (2 * ga + hd + 1))
                                v = cv[:, kv] if b == 3 else v_tok[:, nb - 1 + b, kv]
                                mm = pe.matmul(ps[HD * hd:HD * hd + HD, 6 + w % 2, 0:P], v,
                                               probT[w % 2][hd][:, b * P:(b + 1) * P],
                                               start=(b == BLOCKS[nb][0]), stop=(b == BLOCKS[nb][-1]))
                        mm.then_inc(o_done, 1)

                    for w in range(w0, w0 + 42):
                        if w < w0 + 40:
                            scores(w)
                        if w - w0 >= 2:
                            values(w - 2)
                        if 1 <= w - w0 <= 40:
                            turn(w - 1)
                    pe.wait_ge(ol_made, 40 * (a + 1))
                    for n in range(12, 20):
                        unit(u0 + n, n % 2, KT, h_tiles, None, (u0 + n) // 2)
                        if layer == 0 and FIRST_CHUNKS + n < NCH:
                            ada_multiply(FIRST_CHUNKS + n, n % 2, (FIRST_CHUNKS + n) // 2)
                        if layer == 0 and 12 < n <= NCH - FIRST_CHUNKS:
                            ada_turn(FIRST_CHUNKS + n - 1)
                elif kind == "pool":
                    for n in range(KT):
                        g = n // 2

                        def ready(kk):
                            pe.wait_ge(hl_made, KT * 2 * layer + 2 * g + kk + 1)
                        unit(u0 + n, n % 2, 2, lambda kk: (h_hi[:, 2 * g + kk, :], h_lo[:, 2 * g + kk, :]),
                             ready, (u0 + n) // 2)
                else:
                    pe.wait_ge(tabl_made, 2)
                    for g in range(4):
                        for tb in range(5):
                            e = 7 * g + tb
                            if tb == 0:
                                pe.wait_ge(hl_made, KT * 2 * layer + 2 * g + 2)
                            if tb == 4:
                                pe.wait_ge(ftl_made, 7 * g + 1)
                            elif g:
                                pe.wait_ge(ftl_made, 7 * (g - 1) + (5 if tb == 0 else tb + 1))
                            at = TOKEN_BLOCKS[tb]
                            for kk in range(2):
                                for n, (hx, tab) in enumerate(((h_hi, tab_hi), (h_hi, tab_lo), (h_lo, tab_hi))):
                                    mm = pe.matmul(ps[:, 4 + tb % 4, :], hx[:, 2 * g + kk, at:at + P],
                                                   tab[:, kk, :], start=(kk == 0 and n == 0),
                                                   stop=(kk == 1 and n == 2))
                            mm.then_inc(ft_mm, 1)
                        pe.wait_ge(tabl_made, 11)
                        pe.wait_ge(ftl_made, 7 * g + 5)
                        for c in range(2):
                            if g:
                                pe.wait_ge(ftl_made, 7 * (g - 1) + 5 + c + 1)
                            for tb in range(5):
                                latent = tb < 4
                                out = ps[:, 2 * c, :] if latent else ps[:, 2 * c + 1, 0:CTX]
                                for part in range(2):
                                    col = part * 256 + c * P
                                    for n, (ab, tab) in enumerate(((ab_hi, tab_hi), (ab_hi, tab_lo),
                                                                   (ab_lo, tab_hi))):
                                        rhs = (tab[:, 2 + 4 * part + tb, :] if latent
                                               else tab[:, 10, part * P:part * P + P])
                                        mm = pe.matmul(out, ab[:, tb, col:col + P], rhs,
                                                       start=(tb in (0, 4) and part == 0 and n == 0),
                                                       stop=(tb in (3, 4) and part == 1 and n == 2))
                            mm.then_inc(ft_mm, 1)
                    pe.wait_ge(ftl_made, 28)
                    for n in range(KT):
                        unit(u0 + n, n % 2, KT, h_tiles, None, (u0 + n) // 2)

                last = layer + 1 == DEPTH
                for half in range(2):
                    ub = u0 + MIX_UNITS[kind] + half * (2 * HALF + KT)
                    c0 = NCH * (layer + 1) + half * NCH // 2
                    fl0 = (2 * layer + half) * HALF
                    if half == 0:
                        unit_pair(ub, layer, True)
                    else:
                        unit(ub, 0, KT, h_tiles, None, ub // 2)
                        unit(ub + 1, 1, KT, h_tiles, None, ub // 2)
                    if not last:
                        ada_multiply(c0, 0, c0 // 2)
                    with pe.Fori(0, HALF // 2) as i:
                        for n in range(4):
                            u = ub + 2 + n
                            unit(i * 4 + u, n % 2, KT, h_tiles, None, i * 2 + u // 2)
                            if not last:
                                c = c0 + n // 2
                                if n % 2 == 0:
                                    ada_turn(i * 2 + c)
                                else:
                                    ada_multiply(i * 2 + (c + 1), (c + 1) % 2, i + (c + 1) // 2)
                    if not last:
                        ada_turn(c0 + HALF - 1)
                        ada_multiply(c0 + HALF, (c0 + HALF) % 2, (c0 + HALF) // 2)

                    def gated(kk):
                        pe.wait_ge(fl_made, fl0 + kk + 2)
                    unit(ub + 2 * HALF, 0, HALF, f_tiles, gated, (ub + 2 * HALF) // 2)
                    if not last:
                        ada_turn(c0 + HALF)
                    unit(ub + 2 * HALF + 1, 1, HALF, f_tiles, None, (ub + 2 * HALF) // 2)
                    with pe.Fori(0, KT // 2 - 1) as i:
                        for n in range(2):
                            u = i * 2 + (ub + 2 * HALF + 2 + n)
                            unit(u, n, HALF, f_tiles, None, i + (ub + 2 * HALF + 2) // 2)

        @block.scalar
        def _(act):
            def split_hi(u, par, k, turn):
                if not isinstance(u, int) or u >= 2:
                    act.wait_ge(unit_done, u - 1)
                act.wait_ge(raw_in[par], turn * 16 + 16)
                act.activation(w_hi[par][:, 0:k, :], w_raw[par][:, 0:k, :], ACT.Copy).then_inc(hi_made, 1)

            def split_next(u):
                if u + 2 < len(units):
                    split_hi(u + 2, u % 2, units[u + 2][0], (u + 2) // 2)

            def square_free(layer, second, kk):
                m = 2 * layer + second
                if kk == 0:
                    if m:
                        act.wait_ge(sum_done, m)
                elif kk >= 3:
                    act.wait_ge(sq_added, (KT - 1) * m + kk - 2)
                elif m:
                    act.wait_ge(sq_added, (KT - 1) * m)
                    if second and KINDS[layer] == "attn":
                        act.wait_ge(heads_summed, 10 * (layer // 3 + 1))

            def square(kk, src):
                dst = sq_sum if kk == 0 else sq[kk % 2]
                act.activation(dst[:], src, ACT.Square).then_inc(sq_made, 1)

            def square_tile(layer, second, kk):
                if layer == 0 and not second:
                    act.wait_ge(x_in, 16)
                else:
                    wait_taken(act, last_update(layer, second, kk))
                square_free(layer, second, kk)
                square(kk, x[:, kk, :])

            def root(i, done, used, scale, cols):
                act.wait_ge(done, used)
                if i:
                    act.wait_ge(inv_made, i)
                act.activation(rms[:, :, 0:cols],
                               ps[:, INV_CTX, SUMS].rearrange("p (b c) -> p b c", c=2)[:, :, 0:cols], ACT.Sqrt,
                               bias=eps[:, 0:1], scale=scale).then_inc(rms_made, 1)

            def norm(layer, second):
                m = 2 * layer + second
                r = rms_base(layer, second)
                shift = 24 if second else 0
                md = mods[layer % 2]
                if not explicit(layer, second):
                    act.wait_ge(gain_made, m + 1)
                    act.activation(h_hi[:, :, SH0:NT], md[:, shift:shift + KT, :], ACT.Copy)
                    for kk in range(KT):
                        for at, n, cnd in STREAMS:
                            op = act.activation(h_hi[:, kk, at:at + n], x[:, kk, at:at + n], ACT.Identity,
                                                scale=gain_now[:, kk, cnd:cnd + 1])
                        op.then_inc(hh_made, 1)
                    root(r, sum_done, m + 1, 1.0 / D, 1)
                    return
                root(r, sum_done, m + 1, 1.0 / D, 1)
                for kk in range(KT):
                    act.wait_ge(xn_made, KT * (layer - 1) + kk + 1)
                    pooling = KINDS[layer] == "pool" and not second
                    if pooling and kk >= 2:
                        act.wait_ge(pool_made, kk - 1)
                    for at, n, cnd in STREAMS:
                        if pooling:
                            p0 = POOL_LAT if cnd == 0 else POOL_CTX
                            dst = hp[kk % 2][:, p0:p0 + n]
                        else:
                            dst = h_hi[:, kk, at:at + n]
                        op = act.activation(dst, xn[kk % 2][:, at:at + n], ACT.Identity,
                                            bias=md[:, shift + kk, cnd:cnd + 1])
                    op.then_inc(hh_made, 1)
                    if pooling:
                        if kk >= 1:
                            pool_hi(layer, kk - 1)
                if KINDS[layer] == "pool" and not second:
                    pool_hi(layer, KT - 1)

            def pool_hi(layer, kk):
                act.wait_ge(pool_made, kk + 1)
                for at, n, cnd in STREAMS:
                    p0 = (POOL_LAT if cnd == 0 else POOL_CTX) - POOL_PAD
                    op = act.activation(h_hi[:, kk, at:at + n], pooled[kk % 2][:, p0:p0 + n], ACT.Copy)
                op.then_inc(ph_made, 1)

            act.wait_ge(const_in, 16 * len(CONSTS))
            act.wait_ge(setup_done, N_SETUP)
            act.activation(cond_act[:], cond[:], ACT.Silu).then_inc(cond_made, 1)
            for u in range(2):
                split_hi(u, u, units[u][0], 0)
            for kk in range(KT):
                square_tile(0, False, kk)
            for layer, kind in enumerate(KINDS):
                u0 = UNIT0[layer]
                norm(layer, False)
                if kind == "attn":
                    a = layer // 3
                    for n in range(12):
                        i = n - K0
                        if i >= 1:
                            root(RMS0[layer] + i, heads_summed, 10 * a + i, 1.0 / HD, 2)
                        split_next(u0 + n)
                        wait_taken(act, u0 + n)
                        if i >= 2:
                            act.wait_ge(heads_summed, 10 * a + i - 1)
                        elif i >= 0 and layer:
                            act.wait_ge(sq_added, (KT - 1) * (2 * layer + 1))
                        for at, nn, cnd in JOINED:
                            src, bias = scaled[n % 2][:, at:at + nn], scaled[n % 2][:, SH0 + cnd:SH0 + cnd + 1]
                            if i >= 0:
                                op = act.activation(sq[i % 2][:, at:at + nn], src, ACT.Square, bias=bias)
                                if cnd:
                                    op.then_inc(sq_made, 1)
                            op = act.activation(qkv[:, n, at:at + nn], src, ACT.Identity, bias=bias)
                        op.then_inc(qkv_out, 1)
                    root(RMS0[layer] + 10, heads_summed, 10 * (a + 1), 1.0 / HD, 2)
                    w0 = 40 * a

                    def exps(w):
                        nb, tile = WORK[w - w0]
                        ga, r = tile // 4, tile % 4
                        lo, hi = KEYS[nb]
                        hi = 512 if nb < 4 else hi
                        for hd in range(2):
                            head = 8 * ga + 4 * hd + r
                            st = stat[:, w % 2, hd, :]
                            act.wait_ge(max_made, 2 * w + hd + 1)
                            act.activation(prob[w % 2][hd][:, lo:hi], prob[w % 2][hd][:, lo:hi], ACT.Exp,
                                           bias=st[:, 1:2], scale=HD ** -0.5, accum_out=st[:, 2:3])
                            act.activation(st[:, 3:4], sink[:, a, head:head + 1], ACT.Exp,
                                           bias=st[:, 1:2]).then_inc(exp_made, 1)

                    def turned(w):
                        nb, _ = WORK[w - w0]
                        b0, b1 = BLOCKS[nb][0] * P, (BLOCKS[nb][-1] + 1) * P
                        if w - w0 >= 2:
                            act.wait_ge(o_done, w - 1)
                        for hd in range(2):
                            act.wait_ge(t_done, 2 * w + hd + 1)
                            act.activation(probT[w % 2][hd][:, b0:b1], ps[:, 4 + hd, b0:b1],
                                           ACT.Copy).then_inc(pt_made, 1)

                    def out_hi(w):
                        nb, tile = WORK[w - w0]
                        act.wait_ge(o_done, w + 1)
                        act.activation(h_hi[:, tile, TOKEN_BLOCKS[nb]:TOKEN_BLOCKS[nb] + P],
                                       ps[:, 6 + w % 2, 0:P], ACT.Copy).then_inc(oh_made, 1)

                    for w in range(w0, w0 + 42):
                        if w < w0 + 40:
                            exps(w)
                        if w - w0 >= 2:
                            out_hi(w - 2)
                        if 1 <= w - w0 <= 40:
                            turned(w - 1)
                if kind == "fnet":
                    act.wait_ge(tabl_made, 11)
                    for g in range(4):
                        for tb in range(5):
                            act.wait_ge(ft_mm, 7 * g + tb + 1)
                            act.activation(ab_hi[:, tb, :], ps[:, 4 + tb % 4, :], ACT.Copy).then_inc(fth_made, 1)
                        for c in range(2):
                            act.wait_ge(ft_mm, 7 * g + 5 + c + 1)
                            act.activation(h_hi[:, 2 * g + c, LAT0:LAT0 + LAT], ps[:, 2 * c, :], ACT.Copy)
                            act.activation(h_hi[:, 2 * g + c, CTX0:CTX0 + CTX], ps[:, 2 * c + 1, 0:CTX],
                                           ACT.Copy).then_inc(fth_made, 1)
                for n in range(KT):
                    split_next(u0 + MIX_UNITS[kind] - KT + n)
                    square_tile(layer, True, n)
                norm(layer, True)

                def up_step(u, par, half_u, pair, v, k_next):
                    isint = isinstance(v, int)
                    split_hi(u + 2, par, k_next, half_u + 1)
                    act.wait_ge(taken[par], half_u + 1)
                    act.wait_ge(conv_done, v + 1)
                    act.wait_ge(prod_made, pair + 1)
                    for at, n, cnd in STREAMS:
                        op = act.activation(u_pad[par][:, at + 1:at + 1 + n], scaled[par][:, at:at + n],
                                            ACT.Identity, bias=scaled[par][:, SH0 + cnd:SH0 + cnd + 1])
                    op.then_inc(u_padded, 1)
                    act.wait_ge(u_padded, v + 1)
                    act.wait_ge(cond_made, 1)
                    act.activation(conv_out[par][:], u_pad[par][:, 1:NT + 1], ACT.Identity,
                                   bias=conv[:, v, 3:4] if isint else conv[:, bass.ds(v, 1), 3],
                                   scale=conv[:, v, 1:2] if isint else conv[:, bass.ds(v, 1), 1]
                                   ).then_inc(conv_init, 1)
                    if par == 0:
                        act.wait_ge(conv_done, v + 3)
                        act.activation(gate_act[:], conv_out[0][:], ACT.Silu).then_inc(silu_made, 1)

                for half in range(2):
                    ub = u0 + MIX_UNITS[kind] + half * (2 * HALF + KT)
                    v0 = (2 * layer + half) * 2 * HALF
                    with act.Fori(0, HALF // 2) as i:
                        for n in range(4):
                            up_step(i * 4 + (ub + n), n % 2, i * 2 + (ub + n) // 2,
                                    i * 2 + (v0 + n) // 2, i * 4 + (v0 + n), KT)
                    for n in range(2 * HALF - 2, 2 * HALF):
                        up_step(ub + n, n % 2, (ub + n) // 2, (v0 + n) // 2, v0 + n, HALF)
                    ud = ub + 2 * HALF
                    if half == 0 or layer + 1 == DEPTH:
                        with act.Fori(0, KT // 2 - 1) as i:
                            for n in range(2):
                                split_hi(i * 2 + (ud + n + 2), n, HALF, i + (ud + 2) // 2)
                        for n in range(KT - 2, KT):
                            split_next(ud + n)
                    else:
                        for n in range(2):
                            split_next(ud + n)
                            square_tile(layer + 1, False, n)
                        with act.Fori(0, KT // 2 - 2) as i:
                            for n in range(2):
                                act.wait_ge(taken[n], i + (ud + 2) // 2 + 1)
                                act.wait_ge(sq_added, i * 2 + ((KT - 1) * 2 * (layer + 1) + n))
                                split_hi(i * 2 + (ud + n + 4), n, HALF, i + (ud + 4) // 2)
                                act.activation(sq[n][:], x[:, bass.ds(i * 2 + (2 + n), 1), :].rearrange(
                                    "p a n -> p (a n)"), ACT.Square).then_inc(sq_made, 1)
                        for n in range(KT - 2, KT):
                            split_next(ud + n)
                            square_tile(layer + 1, False, n)
                if layer + 1 < DEPTH and KINDS[layer + 1] == "fnet":
                    for n in range(11):
                        act.wait_ge(tab_in[n // 5 % 2], 16 * (n // 10 + 1))
                        act.activation(tab_hi[:, n, :], tab_raw[:, n % 10, :], ACT.Copy).then_inc(tabh_made, 1)

        @block.vector
        def _(dve):
            own = Chain(dve, dve_own)

            def split_lo(u, par, k):
                dve.wait_ge(hi_made, u + 1)
                dve.tensor_tensor(w_lo[par][:, 0:k, :], w_raw[par][:, 0:k, :], w_hi[par][:, 0:k, :].bitcast(F32),
                                  ALU.subtract).then_inc(lo_made, 1)

            def split_next(u):
                if u + 2 < len(units):
                    split_lo(u + 2, u % 2, units[u + 2][0])

            def ada_copy(c):
                dve.wait_ge(ada_mm, c + 1)
                if not isinstance(c, int) or c >= 1:
                    dve.wait_ge(ada_col, c)
                dve.tensor_copy(ada_rows[:], ps[:, ADA_ROWS, 0:AW]).then_inc(ada_row, 1)

            def ada_add(c, layer, tile):
                dve.wait_ge(ada_col, c + 1)
                cols = ps[:, ADA_COLS, 0:2 * CT].rearrange("p (n c) -> p n c", c=2)
                if isinstance(tile, int):
                    sl = slice(tile, tile + CT)
                    dve.tensor_tensor(mods[layer % 2][:, sl, :], cols, ada_bias[:, layer, sl, :],
                                      ALU.add).then_inc(ada_done, 1)
                else:
                    dve.tensor_tensor(mods[layer % 2][:, bass.ds(tile, CT), :], cols,
                                      ada_bias[:, layer, bass.ds(tile, CT), :], ALU.add).then_inc(ada_done, 1)

            def invert(r, cols):
                dve.wait_ge(rms_made, r + 1)
                if r:
                    dve.wait_ge(inv_turned, r)
                dve.reciprocal(inv_rms[:, :, 0:cols], rms[:, :, 0:cols]).then_inc(inv_small, 1)
                dve.wait_ge(inv_small, r + 1)
                dve.tensor_copy(inv_wide[:].rearrange("p b (c n) -> p b c n", c=cols),
                                inv_rms[:, :, 0:cols].unsqueeze(3).broadcast_to((P, 5, cols, P // cols))
                                ).then_inc(inv_made, 1)

            def norm(layer, second):
                m = 2 * layer + second
                r = rms_base(layer, second)
                base = KT * m
                md = mods[layer % 2]
                dve.wait_ge(ada_done, NCH * (layer + 1) if m else FIRST_CHUNKS)
                sc = 32 if second else 8
                dve.scalar_tensor_tensor(gain_now[:], md[:, sc:sc + KT, :], 1.0,
                                         gains[:, layer, int(second), :, :], ALU.add, ALU.mult).then_inc(gain_made, 1)
                dve.wait_ge(gain_made, m + 1)
                if KINDS[layer] == "pool" and not second:
                    own.link(dve.tensor_tensor(pool_gate[:], md[:, 16:16 + KT, :], pool_scale[:], ALU.mult))
                if m == 0:
                    dve.wait_ge(x_in, 16)
                shift = 24 if second else 0
                if not explicit(layer, second):
                    for kk in range(KT):
                        dve.wait_ge(hh_made, base + kk + 1)
                        if kk == 0:
                            dve.tensor_tensor(h_lo[:, :, SH0:NT], md[:, shift:shift + KT, :],
                                              h_hi[:, :, SH0:NT].bitcast(F32), ALU.subtract)
                        for at, n, cnd in STREAMS:
                            op = dve.scalar_tensor_tensor(h_lo[:, kk, at:at + n], x[:, kk, at:at + n],
                                                          gain_now[:, kk, cnd:cnd + 1],
                                                          h_hi[:, kk, at:at + n].bitcast(F32),
                                                          ALU.mult, ALU.subtract)
                        op.then_inc(hl_made, 1)
                invert(r, 1)
                dve.wait_ge(inv_turned, r + 1)
                dve.tensor_copy(rstd[:, LAT0:LAT0 + LAT], ps[:, INV_LAT, :])
                dve.tensor_copy(rstd[:, CTX0:CTX0 + CTX], ps[:, INV_CTX, 0:CTX]).then_inc(rstd_made, 1)
                dve.wait_ge(rstd_made, m + 1)
                if not explicit(layer, second):
                    return
                pooling = KINDS[layer] == "pool" and not second

                def scaled(kk):
                    if kk >= 2:
                        if pooling:
                            dve.wait_ge(hh_made, base + kk - 1)
                        else:
                            dve.wait_ge(hl_made, base + kk - 1)
                    for at, n, cnd in STREAMS:
                        op = dve.scalar_tensor_tensor(xn[kk % 2][:, at:at + n], x[:, kk, at:at + n],
                                                      gain_now[:, kk, cnd:cnd + 1], rstd[:, at:at + n],
                                                      ALU.mult, ALU.mult)
                    op.then_inc(xn_made, 1)

                def low(kk):
                    dve.wait_ge(hh_made, base + kk + 1)
                    dve.wait_ge(xn_made, KT * (layer - 1) + kk + 1)
                    for at, n, cnd in STREAMS:
                        op = dve.scalar_tensor_tensor(h_lo[:, kk, at:at + n], xn[kk % 2][:, at:at + n],
                                                      md[:, shift + kk, cnd:cnd + 1],
                                                      h_hi[:, kk, at:at + n].bitcast(F32), ALU.add, ALU.subtract)
                    op.then_inc(hl_made, 1)

                for kk in range(KT + 1):
                    if kk < KT:
                        scaled(kk)
                    if kk >= 1:
                        if pooling:
                            pool_tile(layer, kk - 1, base)
                        else:
                            low(kk - 1)

            def pool_tile(layer, kk, base):
                dve.wait_ge(hh_made, base + kk + 1)
                g = kk // 2
                src, width = hp[kk % 2], 1
                if kk == 0:
                    dve.wait_ge(stage_in, 16 * STAGE_IN[layer])
                for step in range(g + 1):
                    dst = win[step % 2]
                    c0 = 2 * width - 1
                    own.link(dve.tensor_tensor(dst[:, c0:POOL_W], src[:, c0:POOL_W],
                                               src[:, c0 - width:POOL_W - width], ALU.add))
                    src, width = dst, 2 * width
                ahead = width - width // 2 - 1
                pl = pooled[kk % 2]
                if kk >= 2:
                    dve.wait_ge(hl_made, base + kk - 1)
                own.link(dve.tensor_tensor(pl[:], src[:, POOL_PAD + ahead:POOL_W - POOL_PAD + ahead],
                                           inv_count[:, g, :], ALU.mult))
                dve.tensor_tensor(pl[:], pl[:], hp[kk % 2][:, POOL_PAD:POOL_W - POOL_PAD],
                                  ALU.subtract).then_inc(pool_made, 1)
                dve.wait_ge(pool_made, kk + 1)
                dve.wait_ge(ph_made, kk + 1)
                for at, n, cnd in STREAMS:
                    p0 = (POOL_LAT if cnd == 0 else POOL_CTX) - POOL_PAD
                    op = dve.tensor_tensor(h_lo[:, kk, at:at + n], pl[:, p0:p0 + n],
                                           h_hi[:, kk, at:at + n].bitcast(F32), ALU.subtract)
                op.then_inc(hl_made, 1)

            def rescale(u, par):
                dve.wait_ge(unit_done, u + 1)
                dve.tensor_tensor(halves(scaled[par][:]), product(par), halves(rstd[:]),
                                  ALU.mult).then_inc(taken[par], 1)

            def update(u, par, o, gate):
                dve.wait_ge(unit_done, u + 1)
                for at, n, bank, col, cnd in ((1, NH - 1, 0, 1, 0), (NH, LAT + 1 - NH, 1, 0, 0),
                                              (CTX0, CTX, 1, CTX0 - NH, 1)):
                    if isinstance(o, int):
                        xt, gt = x[:, o, at:at + n], gate[:, o, cnd:cnd + 1]
                    else:
                        xt = x[:, bass.ds(o, 1), at:at + n].rearrange("p a n -> p (a n)")
                        gt = gate[:, bass.ds(o, 1), cnd]
                    op = dve.scalar_tensor_tensor(xt, ps[:, 2 * par + bank, col:col + n], gt, xt,
                                                  ALU.mult, ALU.add)
                op.then_inc(taken[par], 1)

            dve.wait_ge(const_in, 16 * len(CONSTS))
            own.link(dve.tensor_scalar(neg_sink[:], sink[:], -1.0, None, ALU.mult))
            for u in range(2):
                split_lo(u, u, units[u][0])
            for c in range(FIRST_CHUNKS):
                ada_copy(c)
                if c:
                    ada_add(c - 1, 0, CT * (c - 1))
            ada_add(FIRST_CHUNKS - 1, 0, CT * (FIRST_CHUNKS - 1))

            for layer, kind in enumerate(KINDS):
                u0 = UNIT0[layer]
                if kind == "pool":
                    dve.wait_ge(unit_done, u0)
                    for s in range(2):
                        dve.memset(hp[s][:, 0:POOL_LAT], 0.0)
                        dve.memset(hp[s][:, POOL_LAT + LAT:POOL_CTX], 0.0)
                        own.link(dve.memset(hp[s][:, POOL_CTX + CTX:POOL_W], 0.0))
                def split_tables(rows):
                    for n in rows:
                        dve.wait_ge(tabh_made, n + 1)
                        dve.tensor_tensor(tab_lo[:, n, :], tab_raw[:, n % 10, :], tab_hi[:, n, :].bitcast(F32),
                                          ALU.subtract).then_inc(tabl_made, 1)
                if kind == "fnet":
                    split_tables(range(2))
                norm(layer, False)
                if kind == "fnet":
                    split_tables(range(2, 11))
                gate = pool_gate if kind == "pool" else mods[layer % 2][:, 16:16 + KT, :]
                if kind == "attn":
                    a = layer // 3
                    r0 = RMS0[layer] + 1
                    dve.wait_ge(stage_in, 16 * STAGE_IN[layer])

                    def rotate(i):
                        n = K0 + i
                        dve.wait_ge(inv_turned, r0 + i + 1)
                        dve.wait_ge(qkv_out, 12 * a + n + 1)
                        lat = qkv[:, n, LAT0:LAT0 + LAT]
                        which = 0 if n >= Q0 else 1
                        for tokens, inv in ((lat, ps[:, INV_LAT, :]),
                                            (qkv[:, n, CTX0:CTX0 + CTX], ps[:, INV_CTX, 0:CTX])):
                            op = dve.scalar_tensor_tensor(tokens, tokens, head_gain[:, a, which:which + 1], inv,
                                                          ALU.mult, ALU.mult)
                        op.then_inc(qk_normed, 1)
                        dve.wait_ge(qk_normed, 10 * a + i + 1)
                        own.link(dve.stream_shuffle(swapped[:], lat, [(p + 16) % 32 for p in range(32)]))
                        own.link(dve.tensor_tensor(swapped[:], swapped[:], rope_sin[:], ALU.mult))
                        own.link(dve.tensor_tensor(lat, lat, rope_cos[:], ALU.mult))
                        dve.tensor_tensor(lat, lat, swapped[:], ALU.add).then_inc(qk_ready, 1)

                    for n in range(12):
                        if n >= 2:
                            dve.wait_ge(qkv_out, 12 * a + n - 1)
                        if n >= 3:
                            invert(r0 + n - 3, 2)
                        rescale(u0 + n, n % 2)
                        split_next(u0 + n)
                        if layer == 0:
                            ada_copy(FIRST_CHUNKS + n)
                            if n:
                                ada_add(FIRST_CHUNKS + n - 1, 0, CT * (FIRST_CHUNKS + n - 1))
                        if n >= 3:
                            rotate(n - 3)
                    if layer == 0:
                        ada_add(FIRST_CHUNKS + 11, 0, CT * (FIRST_CHUNKS + 11))
                    invert(r0 + 9, 2)
                    for v in range(2):
                        dve.wait_ge(v_turned, 2 * a + v + 1)
                        dve.tensor_copy(v_tok[:, 0:4, v * P:(v + 1) * P],
                                        ps[:, 6, :].rearrange("p (b c) -> p b c", b=4))
                        dve.tensor_copy(v_tok[:, 4, v * P:(v + 1) * P], ps[:, 7, 0:P]).then_inc(v_ready, 1)
                    rotate(9)
                    w0 = 40 * a

                    def masked(w):
                        nb, tile = WORK[w - w0]
                        ga, r = tile // 4, tile % 4
                        lo, hi = KEYS[nb]
                        hi = 512 if nb < 4 else hi
                        if w - w0 >= 2:
                            dve.wait_ge(t_done, 2 * (w - 1))
                        for hd in range(2):
                            dve.wait_ge(s_done, 2 * w + hd + 1)
                            st = stat[:, w % 2, hd, :]
                            own.link(dve.tensor_tensor_reduce(
                                out=prob[w % 2][hd][:, lo:hi], in0=ps[:, 2 * (w % 2) + hd, lo:hi],
                                in1=band[:, lo:hi], scale=1.0, scalar=-3e38, op0=ALU.add, op1=ALU.max,
                                accum_out=st[:, 0:1]))
                            head = 8 * ga + 4 * hd + r
                            dve.tensor_scalar(st[:, 1:2], st[:, 0:1], -(HD ** -0.5), neg_sink[:, a, head:head + 1],
                                              ALU.mult, ALU.min).then_inc(max_made, 1)

                    def normed(w):
                        nb, _ = WORK[w - w0]
                        lo, hi = KEYS[nb]
                        hi = 512 if nb < 4 else hi
                        dve.wait_ge(exp_made, 2 * w + 2)
                        st = stat[:, w % 2, :, :]
                        own.link(dve.tensor_tensor(st[:, :, 4:5], st[:, :, 2:3], st[:, :, 3:4], ALU.add))
                        own.link(dve.reciprocal(st[:, :, 5:6], st[:, :, 4:5]))
                        for hd in range(2):
                            dve.tensor_scalar(prob[w % 2][hd][:, lo:hi], prob[w % 2][hd][:, lo:hi],
                                              st[:, hd, 5:6], None, ALU.mult).then_inc(p_ready, 1)

                    def out_lo(w):
                        nb, tile = WORK[w - w0]
                        cols = slice(TOKEN_BLOCKS[nb], TOKEN_BLOCKS[nb] + P)
                        dve.wait_ge(oh_made, w + 1)
                        dve.tensor_tensor(h_lo[:, tile, cols], ps[:, 6 + w % 2, 0:P],
                                          h_hi[:, tile, cols].bitcast(F32), ALU.subtract).then_inc(ol_made, 1)

                    for w in range(w0, w0 + 43):
                        if 1 <= w - w0 <= 40:
                            normed(w - 1)
                        if w < w0 + 40:
                            masked(w)
                        if w - w0 >= 3:
                            out_lo(w - 3)
                    for n in range(12, 20):
                        update(u0 + n, n % 2, n - 12, gate)
                        split_next(u0 + n)
                        c = FIRST_CHUNKS + n
                        if layer == 0 and c < NCH:
                            ada_copy(c)
                        if layer == 0 and 12 < n <= NCH - FIRST_CHUNKS:
                            ada_add(c - 1, 0, CT * (c - 1))
                else:
                    if kind == "fnet":
                        for g in range(4):
                            for tb in range(5):
                                dve.wait_ge(fth_made, 7 * g + tb + 1)
                                dve.tensor_tensor(ab_lo[:, tb, :], ps[:, 4 + tb % 4, :],
                                                  ab_hi[:, tb, :].bitcast(F32), ALU.subtract).then_inc(ftl_made, 1)
                            for c in range(2):
                                dve.wait_ge(fth_made, 7 * g + 5 + c + 1)
                                for at, n, cnd in STREAMS:
                                    op = dve.tensor_tensor(h_lo[:, 2 * g + c, at:at + n],
                                                           ps[:, 2 * c + cnd, 0:n],
                                                           h_hi[:, 2 * g + c, at:at + n].bitcast(F32), ALU.subtract)
                                op.then_inc(ftl_made, 1)
                    for n in range(KT):
                        update(u0 + n, n % 2, n, gate)
                        split_next(u0 + n)
                norm(layer, True)
                gate = mods[layer % 2][:, 40:40 + KT, :]
                last = layer + 1 == DEPTH
                if kind == "attn":
                    dve.wait_ge(out_sent, 32 * (layer // 3 + 1))

                def up_step(u, par, v, pair, tile, k_next, c=None, c_tile=None, c_end=None, c_end_tile=None):
                    isint = isinstance(v, int)
                    cw = (lambda n: conv[:, v, n:n + 1]) if isint else (lambda n: conv[:, bass.ds(v, 1), n])
                    rescale(u, par)
                    split_lo(u + 2, par, k_next)
                    dve.wait_ge(conv_init, v + 1)
                    own.link(dve.scalar_tensor_tensor(conv_out[par][:], u_pad[par][:, 0:NT], cw(0),
                                                      conv_out[par][:], ALU.mult, ALU.add))
                    dve.scalar_tensor_tensor(conv_out[par][:], u_pad[par][:, 2:NT + 2], cw(2), conv_out[par][:],
                                             ALU.mult, ALU.add).then_inc(conv_done, 1)
                    if par == 0:
                        if c is not None:
                            ada_copy(c)
                    else:
                        dve.wait_ge(silu_made, pair + 1)
                        dve.wait_ge(conv_done, v + 3)
                        dve.wait_ge(fl_made, pair + 1)
                        dve.tensor_tensor(prod[:], gate_act[:], conv_out[1][:], ALU.mult).then_inc(prod_made, 1)
                        dve.wait_ge(prod_made, pair + 2)
                        if isint:
                            fh, fl = f_hi[:, tile, :], f_lo[:, tile, :]
                        else:
                            fh, fl = (ff[:, bass.ds(tile, 1), :].rearrange("p a n -> p (a n)") for ff in (f_hi, f_lo))
                        own.link(dve.tensor_scalar(fh, prod[:], 1.0, None, ALU.mult))
                        dve.tensor_tensor(fl, prod[:], fh.bitcast(F32), ALU.subtract).then_inc(fl_made, 1)
                        if c is not None:
                            ada_add(c, layer + 1, c_tile)
                        if c_end is not None:
                            ada_copy(c_end)

                for half in range(2):
                    ub = u0 + MIX_UNITS[kind] + half * (2 * HALF + KT)
                    v0 = (2 * layer + half) * 2 * HALF
                    ch = half * NCH // 2
                    c0 = NCH * (layer + 1) + ch
                    with dve.Fori(0, HALF // 2) as i:
                        own.enter(i, 6)
                        for n in range(4):
                            up_step(i * 4 + (ub + n), n % 2, i * 4 + (v0 + n), i * 2 + (v0 + n) // 2,
                                    i * 2 + n // 2, KT, None if last else i * 2 + (c0 + n // 2),
                                    i * (2 * CT) + CT * (ch + n // 2))
                    own.leave(HALF // 2)
                    for n in range(2 * HALF - 2, 2 * HALF):
                        c = c0 + HALF - 1
                        up_step(ub + n, n % 2, v0 + n, (v0 + n) // 2, n // 2, HALF, None if last else c,
                                CT * (ch + HALF - 1), None if last else c + 1)
                    ud = ub + 2 * HALF
                    for n in range(2):
                        update(ud + n, n, n, gate)
                        split_next(ud + n)
                        if n == 0 and not last:
                            ada_add(c0 + HALF, layer + 1, CT * (ch + HALF))
                    with dve.Fori(0, KT // 2 - 2) as i:
                        for n in range(2):
                            update(i * 2 + (ud + 2 + n), n, i * 2 + (2 + n), gate)
                            split_lo(i * 2 + (ud + 4 + n), n, HALF)
                    for n in range(KT - 2, KT):
                        update(ud + n, n % 2, n, gate)
                        split_next(ud + n)


def shape_constants():
    f = np.float32
    p = np.arange(P)
    tok = np.arange(LAT)
    d = p % HD
    pos = np.where((d // 32 == 0)[:, None], (tok // 64)[None], (tok % 64)[None]).astype(f)
    inv_freq = (1.0 / (f(10000.0) ** (np.arange(0, 32, 2, dtype=f) / f(32)))).astype(f)
    angle = pos * inv_freq[d % 16][:, None]
    sign = np.where(d % 32 < 16, -1.0, 1.0)[:, None]
    q, k = np.arange(P)[:, None], np.arange(P)[None]
    band = np.zeros((P, 512), f)
    band[:, 0:128] = np.where(k >= q, 0.0, NEG)
    band[:, 256:384] = np.where(k <= q, 0.0, NEG)
    inv = np.zeros((4, POOL_W - 2 * POOL_PAD), f)
    for g, w in enumerate(WINDOWS):
        for n, at in ((LAT, POOL_LAT), (CTX, POOL_CTX)):
            tt = np.arange(n)
            count = np.clip(tt + w - w // 2, 0, n) - np.clip(tt - w // 2, 0, n)
            inv[g, at - POOL_PAD:at - POOL_PAD + n] = 1.0 / count
    dft = np.zeros((11, P, 512), f)
    ang = 2 * np.pi * ((tok[:, None] * tok[None]) % LAT) / LAT
    dft[2:6] = (np.cos(ang) / np.sqrt(LAT * 256.0)).reshape(4, P, LAT)
    dft[6:10] = (-np.sin(ang) / np.sqrt(LAT * 256.0)).reshape(4, P, LAT)
    ch = np.arange(256)
    ang = 2 * np.pi * ((ch[:, None] * ch[None]) % 256) / 256
    dft[0:2] = np.concatenate([np.cos(ang), np.sin(ang)], 1).reshape(2, P, 512)
    ang = 2 * np.pi * ((p[:, None] * p[None]) % CTX) / CTX
    dft[10, :, 0:128] = np.cos(ang) / np.sqrt(CTX * 256.0)
    dft[10, :, 128:256] = -np.sin(ang) / np.sqrt(CTX * 256.0)
    pick = np.zeros((P, 2), f)
    for j in range(4):
        pick[32 * j, 0] = pick[32 * j + 1, 1] = 1.0
    return {
        "rope_cos": np.cos(angle).astype(f), "rope_sin": (sign * np.sin(angle)).astype(f), "band": band,
        "inv_count": np.broadcast_to(inv, (P,) + inv.shape), "dft": dft, "pick": pick,
        "two_heads": (p[:, None] // HD == np.arange(2)[None]).astype(f), "ident": np.eye(P, dtype=f),
    }


def lay_out(i):
    def token_columns(lat, ctx_rows):
        out = np.zeros((P, KT, NT), np.float32)
        for rows, at in ((lat, LAT0), (ctx_rows, CTX0)):
            out[:, :, at:at + len(rows)] = rows.T.reshape(KT, P, len(rows)).transpose(1, 0, 2)
        return out

    def unit_rows(w, k):
        lead = w.shape[:-2]
        n = w.shape[-1] // P
        w = w.reshape(lead + (k, P, n, P))
        w = np.moveaxis(w, (-2, -3), (len(lead), len(lead) + 1))
        return w.reshape(-1, P, k * P)

    def column(v):
        v = v.reshape(v.shape[:-1] + (-1, P))
        return np.moveaxis(v, -1, 0)

    def twice(v):
        return np.repeat(v[..., None], 2, -1)

    cond = np.zeros((P, KT, 32), np.float32)
    cond[:, :, 0] = i["c"][0].reshape(KT, P).T
    cond[:, :, 1] = i["c_ctx"].reshape(KT, P).T
    heads = [8 * (tl // 4) + 4 * hd + tl % 4 for tl in range(KT) for hd in range(2)]
    qcols = np.concatenate([np.arange(HD * h, HD * h + HD) for h in heads])
    cols = np.concatenate([np.arange(D + 256, D + 512), np.arange(D, D + 256), qcols])
    pairs = [n for j in range(FT) for n in (j, FT + j)]
    w_in = unit_rows(i["ffn_w_in"], KT).reshape(DEPTH, 2 * FT, P, KT * P)[:, pairs].reshape(-1, P, KT * P)
    conv = np.concatenate([i["ffn_conv_w"], i["ffn_conv_b"][:, None]], 1)
    conv = column(conv)[:, :, :, pairs].transpose(0, 1, 3, 2).reshape(P, DEPTH * 2 * FT, 4)
    head_gain = np.stack([np.tile(i["attn_q_norm"], (1, 2)), np.tile(i["attn_k_norm"], (1, 2))], -1)
    ck = i["cache_k"][0].reshape(2, P, 2, P).transpose(0, 3, 2, 1)
    out = {
        "x": token_columns(i["x_sample"][0], i["x_prompt"][0]),
        "cond": cond,
        "ada_w": i["ada_w"].reshape(DEPTH, KT, P, NCH, AW).transpose(0, 3, 2, 1, 4).reshape(-1, P, KT * AW),
        "ada_bias": twice(column(i["ada_b"])),
        "gains": twice(np.stack([column(i["norm_mix"]), column(i["norm_ffn"])], 2)),
        "pool_scale": twice(column(i["pool_scale"])[:, 0]),
        "w_qkv": unit_rows(i["attn_w_qkv"][:, :, cols], KT),
        "w_o": unit_rows(i["attn_w_o"][:, qcols], KT),
        "w_pool": unit_rows(i["pool_w"][0], 2),
        "w_fnet": unit_rows(i["fnet_w"], KT),
        "w_in": w_in,
        "w_out": unit_rows(i["ffn_w_out"].reshape(DEPTH, 2, HALF * P, D), HALF),
        "conv": conv,
        "head_gain": head_gain.transpose(1, 0, 2),
        "sink": np.broadcast_to(i["attn_sink"], (P, 2, NHEADS)),
        "cache_k": ck,
        "cache_v": i["cache_v"][0].reshape(2, P, 256),
    }
    return out


def kernel(**inputs):
    import concourse.bacc as bacc
    from concourse.bass_utils import run_bass_kernel_spmd

    arrays = lay_out({k: np.asarray(v) for k, v in inputs.items()})
    arrays.update(shape_constants())
    arrays = {f"in_{k}": np.ascontiguousarray(v) for k, v in arrays.items()}
    nc = bacc.Bacc("TRN2", target_bir_lowering=False, num_devices=1)
    t = {k[3:]: nc.dram_tensor(k, v.shape, F32, kind="ExternalInput").ap() for k, v in arrays.items()}
    for name, shape in (("y", (P, KT, NT)), ("new_k", (2, P, 2, CTX)), ("new_v", (2, P, 2, CTX))):
        t[name] = nc.dram_tensor(f"out_{name}", shape, F32, kind="ExternalOutput").ap()
    build(nc, t)
    r = run_bass_kernel_spmd(nc, [arrays], core_ids=[0]).results[0]
    y = r["out_y"].transpose(1, 0, 2).reshape(D, NT)
    caches = [r[f"out_{n}"].transpose(0, 3, 2, 1).reshape(1, 2, CTX, 4, HD) for n in ("new_k", "new_v")]
    return (np.ascontiguousarray(y[:, CTX0:CTX0 + CTX].T)[None], np.ascontiguousarray(y[:, LAT0:LAT0 + LAT].T)[None],
            np.ascontiguousarray(caches[0]), np.ascontiguousarray(caches[1]))
```

```python
from contextlib import ExitStack

import numpy as np

import concourse.bass as bass
from concourse import mybir

F32 = mybir.dt.float32
F32R = mybir.dt.float32r
ALU = mybir.AluOpType
ACT = mybir.ActivationFunctionType

P = 128
D = 1024
KT = D // P
LAT, CTX = 512, 128
LAT0, CTX0 = 1, 514
NT = 644
NH = NT // 2
DEPTH = 4
KINDS = ("attn", "pool", "fnet", "attn")
HD = 64
NHEADS = 16
FF = 2816
FT = FF // P
HALF = FT // 2
AW = 256
NCH = 6 * D // AW
CT = AW // P
EPS = 1e-6
NEG = -1e30
WINDOWS = (2, 4, 8, 16)
REACH = 8
POOL_SPAN = [(max(P * b - REACH, 0), min(P * (b + 1) + REACH, LAT)) for b in range(LAT // P)]
POOL_AT = (0, P + REACH, P + REACH, 2 * P + 3 * REACH, 3 * P + 4 * REACH)
POOL_COLS = 4 * P + 4 * REACH

MIX_UNITS = {"attn": 20, "pool": 0, "fnet": 8}
FFN_UNITS = 2 * (2 * HALF + KT)
FIRST_CHUNKS = 2 * D // AW
SH0 = NT - 2
UNIT0 = [sum(MIX_UNITS[k] + FFN_UNITS for k in KINDS[:i]) for i in range(DEPTH + 1)]
SQ0 = [sum(2 * KT + (10 if k == "attn" else 0) for k in KINDS[:i]) for i in range(DEPTH)]
RMS0 = [sum(2 + (10 if k == "attn" else 0) for k in KINDS[:i]) for i in range(DEPTH)]
STREAMS = ((LAT0, LAT, 0), (CTX0, CTX, 1))


class Chain:

    def __init__(self, eng, sem):
        self.eng, self.sem, self.n, self.off = eng, sem, 0, 0

    def link(self, ins):
        self.n += 1
        ins.then_inc(self.sem, 1)
        self.eng.wait_ge(self.sem, self.n + self.off)

    def enter(self, i, per):
        self.off, self.start, self.per = i * per, self.n, per

    def leave(self, iterations):
        assert self.n - self.start == self.per
        self.off, self.n = 0, self.start + self.per * iterations


def build(nc, t):
    with ExitStack() as ctx:
        def sb(name, shape, dt=F32, stack=None):
            return (stack or ctx).enter_context(nc.sbuf_tensor(name, shape, dt))

        def sem(name):
            return ctx.enter_context(nc.semaphore(name))

        x = sb("x", [P, KT, NT])
        h_hi = sb("h_hi", [P, KT, NT], F32R)
        h_lo = sb("h_lo", [P, KT, NT], F32R)
        w_raw = [sb(f"w_raw{s}", [P, HALF, P]) for s in range(2)]
        w_hi = [sb(f"w_hi{s}", [P, HALF, P], F32R) for s in range(2)]
        w_lo = [sb(f"w_lo{s}", [P, HALF, P], F32R) for s in range(2)]
        ada_w = [sb(f"ada_w{s}", [P, KT, AW]) for s in range(2)]
        ada_rows = sb("ada_rows", [P, AW])
        cond = sb("cond", [P, KT, 32])
        cond_act = sb("cond_act", [P, KT, 32])
        mods = [sb(f"mods{s}", [P, 48, 2]) for s in range(2)]
        ada_bias = sb("ada_bias", [P, DEPTH, 48, 2])
        gains = sb("gains", [P, DEPTH, 2, KT, 2])
        gain_now = sb("gain_now", [P, KT, 2])
        pool_scale = sb("pool_scale", [P, KT, 2])
        pool_gate = sb("pool_gate", [P, KT, 2])
        conv = sb("conv", [P, DEPTH * 2 * FT, 4])
        head_gain = sb("head_gain", [P, 2, 2])
        sink = sb("sink", [P, 2, NHEADS])
        neg_sink = sb("neg_sink", [P, 2, NHEADS])
        ones = sb("ones", [P, 1])
        two_heads = sb("two_heads", [P, 2])
        ident = sb("ident", [P, P])
        pick = sb("pick", [P, 2])
        eps = sb("eps", [P, 1])
        u_pad = [sb(f"u_pad{s}", [P, NT + 2]) for s in range(2)]

        rstd = sb("rstd", [P, NT])
        rms = sb("rms", [P, 5, 2])
        inv_rms = sb("inv_rms", [P, 5, 2])

        with ExitStack() as a:
            sq = [sb(f"sq{s}", [P, NT], F32, a) for s in range(2)]
            sq_sum = sb("sq_sum", [P, NT], F32, a)
            inv_wide = sb("inv_wide", [P, 5, P], F32, a)
            sb("unused", [P, NT - 5 * P], F32, a)
            xn = [sb(f"xn{s}", [P, NT], F32, a) for s in range(2)]
        with ExitStack() as a:
            conv_out = [sb(f"conv_out{s}", [P, NT], F32, a) for s in range(2)]
            gate_act = sb("gate_act", [P, NT], F32, a)
            prod = sb("prod", [P, NT], F32, a)
            scaled = [sb(f"scaled{s}", [P, NT], F32, a) for s in range(2)]
        tmp_store = sb("tmp_store", [P, 6 * (NT + 12)])

        with ExitStack() as a:
            f_hi = sb("f_hi", [P, HALF, NT], F32R, a)
            f_lo = sb("f_lo", [P, HALF, NT], F32R, a)
        with ExitStack() as a:
            qkv = sb("qkv", [P, 12, NT], F32, a)
            v_tok = sb("v_tok", [P, 5, 256], F32, a)
            ck = sb("ck", [P, 2, P], F32, a)
            cv = sb("cv", [P, 256], F32, a)
            rope_cos = sb("rope_cos", [P, LAT], F32, a)
            rope_sin = sb("rope_sin", [P, LAT], F32, a)
            band = sb("band", [P, 512], F32, a)
            swapped = sb("swapped", [P, LAT], F32, a)
            prob = [[sb(f"prob{s}{hd}", [P, 512], F32, a) for hd in range(2)] for s in range(2)]
            probT = [[sb(f"probT{s}{hd}", [P, 512], F32, a) for hd in range(2)] for s in range(2)]
            stat = sb("stat", [P, 2, 2, 8], F32, a)
        with ExitStack() as a:
            z = [sb(f"z{s}", [P, 5 * P], F32, a) for s in range(2)]
            h_whole = sb("h_whole", [P, KT, NT], F32, a)
            sb("unused_pool", [P, 2 * HALF * NT + 16 - 10 * P - KT * NT], F32, a)
            pool_tab = sb("pool_tab", [P, 4, POOL_COLS], F32, a)
        with ExitStack() as a:
            tab_hi = sb("tab_hi", [P, 10, 512], F32R, a)
            tab_lo = sb("tab_lo", [P, 10, 512], F32R, a)
            ctx_tab = sb("ctx_tab", [P, 256], F32, a)
            sb("unused_fnet", [P, 768], F32, a)
            with ExitStack() as b:
                ab_hi = sb("ab_hi", [P, 4, 512], F32R, b)
                ab_lo = sb("ab_lo", [P, 4, 512], F32R, b)
                ab_ctx = sb("ab_ctx", [P, 512], F32, b)
            tab_raw = sb("tab_raw", [P, 10, 512], F32, a)
        stage_store = sb("stage_store", [P, 64 * 256 + 64])
        assert stage_store is not None and tmp_store is not None

        ps = ctx.enter_context(nc.psum_tensor("ps", [P, 8, 512], F32))
        INV_LAT, INV_CTX, ADA_ROWS, ADA_COLS = 4, 5, 6, 7
        SUMS = slice(256, 266)
        Q0, K0, V0 = 4, 2, 0

        const_in = sem("const_in")
        x_in = sem("x_in")
        stage_in = sem("stage_in")
        raw_in = [sem(f"raw_in{s}") for s in range(2)]
        hi_made = sem("hi_made")
        lo_made = sem("lo_made")
        unit_done = sem("unit_done")
        taken = [sem(f"taken{s}") for s in range(2)]
        setup_done = sem("setup_done")
        sq_made = sem("sq_made")
        sq_added = sem("sq_added")
        sum_done = sem("sum_done")
        heads_summed = sem("heads_summed")
        inv_made = sem("inv_made")
        inv_small = sem("inv_small")
        inv_turned = sem("inv_turned")
        qk_normed = sem("qk_normed")
        gain_made = sem("gain_made")
        qkv_out = sem("qkv_out")
        u_padded = sem("u_padded")
        conv_init = sem("conv_init")
        rms_made = sem("rms_made")
        rstd_made = sem("rstd_made")
        xn_made = sem("xn_made")
        hh_made = sem("hh_made")
        hl_made = sem("hl_made")
        cond_made = sem("cond_made")
        ada_in = [sem(f"ada_in{s}") for s in range(2)]
        ada_mm = sem("ada_mm")
        ada_row = sem("ada_row")
        ada_col = sem("ada_col")
        ada_done = sem("ada_done")
        conv_done = sem("conv_done")
        silu_made = sem("silu_made")
        prod_made = sem("prod_made")
        fl_made = sem("fl_made")
        qk_ready = sem("qk_ready")
        v_turned = sem("v_turned")
        v_ready = sem("v_ready")
        s_done = sem("s_done")
        max_made = sem("max_made")
        exp_made = sem("exp_made")
        p_ready = sem("p_ready")
        t_done = sem("t_done")
        pt_made = sem("pt_made")
        o_done = sem("o_done")
        oh_made = sem("oh_made")
        ol_made = sem("ol_made")
        pool_in = sem("pool_in")
        w_pool_in = sem("w_pool_in")
        pool_done = sem("pool_done")
        pool_taken = sem("pool_taken")
        z_done = sem("z_done")
        z_made = sem("z_made")
        ctx_tab_in = sem("ctx_tab_in")
        tab_in = [sem(f"tab_in{s}") for s in range(2)]
        tabh_made = sem("tabh_made")
        tabl_made = sem("tabl_made")
        ft_mm = sem("ft_mm")
        fth_made = sem("fth_made")
        ftl_made = sem("ftl_made")
        out_sent = sem("out_sent")
        dve_own = sem("dve_own")

        def wait_taken(eng, u):
            eng.wait_ge(taken[u % 2], u // 2 + 1)

        def sq_base(layer, second):
            return SQ0[layer] + (KT + (10 if KINDS[layer] == "attn" else 0) if second else 0)

        def low_base(layer, second):
            return KT * (2 * layer + second - (layer > 1 or (layer == 1 and second)))

        def rms_base(layer, second):
            return RMS0[layer] + (1 + (10 if KINDS[layer] == "attn" else 0) if second else 0)

        def last_update(layer, second, kk):
            return UNIT0[layer] + (MIX_UNITS[KINDS[layer]] if second else 0) - KT + kk

        def explicit(layer, second):
            return KINDS[layer] in ("pool", "fnet") and not second

        def halves(ap):
            return ap.rearrange("p (a b) -> p a b", a=2)

        def z_product(s):
            return ps[:].rearrange("p b n -> p (b n)")[:, (4 + 2 * s) * 512:(4 + 2 * s) * 512 + 5 * P]

        def product(s):
            return ps[:, 2 * s:2 * s + 2, 0:NH]

        units = []
        for layer, kind in enumerate(KINDS):
            if kind == "attn":
                a = layer // 3
                units += [(KT, t["w_qkv"], 12 * a + n) for n in range(12)]
                units += [(KT, t["w_o"], KT * a + n) for n in range(KT)]
            elif kind == "fnet":
                units += [(KT, t["w_fnet"], n) for n in range(KT)]
            for half in range(2):
                units += [(KT, t["w_in"], (2 * layer + half) * 2 * HALF + n) for n in range(2 * HALF)]
                units += [(HALF, t["w_out"], (2 * layer + half) * KT + n) for n in range(KT)]
        assert len(units) == UNIT0[DEPTH]

        CONSTS = ((cond, "cond"), (ada_bias, "ada_bias"), (gains, "gains"), (pool_scale, "pool_scale"),
                  (pick, "pick"), (two_heads, "two_heads"), (ident, "ident"), (conv, "conv"),
                  (head_gain, "head_gain"), (sink, "sink"))
        JOINED = ((LAT0, CTX0 - LAT0, 0), (CTX0, CTX, 1))
        PADS = ((0, LAT0), (LAT0 + LAT, 1), (CTX0 + CTX, NT - CTX0 - CTX))
        N_SETUP = 5 + 2 * len(PADS)
        STAGE_IN = (5, 5, 5, 10)
        TOKEN_BLOCKS = [LAT0 + P * n for n in range(LAT // P)] + [CTX0]
        KEYS = ((128, 384), (0, 384), (0, 384), (0, 256), (128, 256))
        BLOCKS = ((1, 2, 3), (0, 1, 2, 3), (0, 1, 2, 3), (0, 1, 3), (1,))
        WORK = [(nb, tile) for nb in range(5) for tile in range(KT)]

        block = ctx.enter_context(nc.Block())

        @block.sync
        def _(sp):
            def load_unit(u, par, k, src):
                if not isinstance(u, int) or u >= 2:
                    sp.wait_ge(lo_made, u - 1)
                sp.dma_start(w_raw[par][:, 0:k, :], src).then_inc(raw_in[par], 16)

            def load_units(u0, n):
                for u in range(u0, u0 + n):
                    k, arr, row = units[u]
                    load_unit(u, u % 2, k, arr[row].rearrange("p (k c) -> p k c", k=k))

            def load_chunk(c, par, src):
                if not isinstance(c, int) or c >= 2:
                    sp.wait_ge(ada_mm, c - 1)
                sp.dma_start(ada_w[par][:], src).then_inc(ada_in[par], 16)

            def chunk_rows(c):
                return t["ada_w"][c].rearrange("p (k c) -> p k c", k=KT)

            def looped(arr, k, row):
                return arr[bass.ds(row, 1)].rearrange("a p (k c) -> p (a k) c", k=k)

            for dst, src in CONSTS:
                sp.dma_start(dst[:], t[src]).then_inc(const_in, 16)
            load_units(0, 2)
            for c in range(2):
                load_chunk(c, c, chunk_rows(c))
            sp.dma_start(x[:], t["x"]).then_inc(x_in, 16)
            for c in range(2, FIRST_CHUNKS):
                load_chunk(c, c % 2, chunk_rows(c))

            for layer, kind in enumerate(KINDS):
                u0 = UNIT0[layer]
                if layer and kind != "pool":
                    load_units(u0, 2)
                    sp.wait_ge(unit_done, u0)
                a = layer // 3
                if kind == "attn":
                    for dst, src in ((rope_cos[:], t["rope_cos"]), (rope_sin[:], t["rope_sin"]),
                                     (band[:], t["band"]), (ck[:], t["cache_k"][a]), (cv[:], t["cache_v"][a])):
                        sp.dma_start(dst, src).then_inc(stage_in, 16)
                elif kind == "fnet":
                    sp.dma_start(tab_raw[:, 0:6, :], t["dft"][4:10].rearrange("k p c -> p k c")).then_inc(tab_in[1], 16)
                    sp.dma_start(ctx_tab[:], t["dft_ctx"]).then_inc(ctx_tab_in, 16)
                for n in range(MIX_UNITS[kind]):
                    if n >= 2:
                        load_units(u0 + n, 1)
                    if layer == 0 and FIRST_CHUNKS + n < NCH:
                        load_chunk(FIRST_CHUNKS + n, n % 2, chunk_rows(FIRST_CHUNKS + n))
                if kind == "attn":
                    sp.wait_ge(qk_ready, 10 * (a + 1))
                    sp.wait_ge(qkv_out, 12 * (a + 1))
                    sp.dma_start(t["new_k"][a], qkv[:, K0:K0 + 2, CTX0:CTX0 + CTX]).then_inc(out_sent, 16)
                    sp.dma_start(t["new_v"][a], qkv[:, V0:V0 + 2, CTX0:CTX0 + CTX]).then_inc(out_sent, 16)
                if layer + 1 < DEPTH and KINDS[layer + 1] == "pool":
                    sp.wait_ge(o_done, 40 * (a + 1))
                    sp.dma_start(pool_tab[:], t["pool_tab"]).then_inc(pool_in, 16)
                for half in range(2):
                    ub = u0 + MIX_UNITS[kind] + half * (2 * HALF + KT)
                    up_row = (2 * layer + half) * 2 * HALF
                    if half and layer + 1 < DEPTH and KINDS[layer + 1] == "fnet":
                        sp.wait_ge(pool_done, KT)
                        sp.dma_start(tab_raw[:, 6:10, :],
                                     t["dft"][0:4].rearrange("k p c -> p k c")).then_inc(tab_in[0], 16)
                    c0 = NCH * (layer + 1) + half * NCH // 2
                    with sp.Fori(0, HALF // 2) as i:
                        for n in range(4):
                            load_unit(i * 4 + (ub + n), n % 2, KT, looped(t["w_in"], KT, i * 4 + (up_row + n)))
                            if n % 2 and layer + 1 < DEPTH:
                                if kind == "pool":
                                    sp.wait_ge(pool_done, KT)
                                c = i * 2 + (c0 + n // 2)
                                load_chunk(c, n // 2, looped(t["ada_w"], KT, c))
                    load_units(ub + 2 * HALF - 2, 2)
                    if layer + 1 < DEPTH:
                        for c in range(c0 + HALF - 1, c0 + HALF + 1):
                            load_chunk(c, c % 2, chunk_rows(c))
                    with sp.Fori(0, KT // 2) as i:
                        for n in range(2):
                            load_unit(i * 2 + (ub + 2 * HALF + n), n, HALF,
                                      looped(t["w_out"], HALF, i * 2 + ((2 * layer + half) * KT + n)))
                    if half and layer + 1 < DEPTH and KINDS[layer + 1] == "pool":
                        sp.wait_ge(ada_mm, NCH * (layer + 2))
                        sp.dma_start(ada_w[0][:], t["w_pool"]).then_inc(w_pool_in, 16)
            for o in range(KT):
                wait_taken(sp, UNIT0[DEPTH] - KT + o)
                sp.dma_start(t["y"][:, o, :], x[:, o, :]).then_inc(out_sent, 16)
            sp.wait_ge(out_sent, 16 * (4 + KT))

        @block.gpsimd
        def _(pool):
            pool.memset(ones[:], 1.0).then_inc(setup_done, 1)
            pool.memset(eps[:], EPS).then_inc(setup_done, 1)
            pool.sem_inc(conv_done, 2)
            pool.sem_inc(prod_made, 1)
            pool.sem_inc(fl_made, 1)
            for s in range(2):
                pool.memset(u_pad[s][:], 0.0).then_inc(setup_done, 1)
            pool.memset(rstd[:], 1.0).then_inc(setup_done, 1)
            for hx in (h_hi, h_lo):
                for a0, n in PADS:
                    pool.memset(hx[:, :, a0:a0 + n].bitcast(F32), 0.0).then_inc(setup_done, 1)
            for layer in range(DEPTH):
                for second in (False, True):
                    m = 2 * layer + second
                    for kk in range(1, KT):
                        pool.wait_ge(sq_made, sq_base(layer, second) + kk + 1)
                        if kk > 1:
                            pool.wait_ge(sq_added, (KT - 1) * m + kk - 1)
                        pool.tensor_tensor(sq_sum[:], sq_sum[:], sq[kk % 2][:], ALU.add).then_inc(sq_added, 1)

        @block.tensor
        def _(pe):
            def unit(u, par, k, rhs, ready=None, prior=None, middle=None):
                pe.wait_ge(lo_made, u + 1)
                if prior is None or not isinstance(prior, int) or prior > 0:
                    pe.wait_ge(taken[par], prior)
                for kk in range(k):
                    if middle and kk == k // 2:
                        middle()
                    if ready:
                        ready(kk)
                    b_hi, b_lo = rhs(kk)
                    for n, (w, b) in enumerate(((w_hi, b_hi), (w_hi, b_lo), (w_lo, b_hi))):
                        for hf in range(2):
                            mm = pe.matmul(ps[:, 2 * par + hf, 0:NH], w[par][:, kk, :],
                                           b[:, hf * NH:(hf + 1) * NH],
                                           start=(kk == 0 and n == 0), stop=(kk == k - 1 and n == 2))
                mm.then_inc(unit_done, 1)

            def h_tiles(kk):
                return h_hi[:, kk, :], h_lo[:, kk, :]

            def f_tiles(kk):
                return f_hi[:, kk, :], f_lo[:, kk, :]

            def unit_pair(u, layer, second):
                def tile(s, kk):
                    if kk == 0:
                        pe.wait_ge(lo_made, u + s + 1)
                        if u:
                            wait_taken(pe, u - 2 + s)
                    pe.wait_ge(hl_made, low_base(layer, second) + kk + 1)
                    for n, (w, b) in enumerate(((w_hi, h_hi), (w_hi, h_lo), (w_lo, h_hi))):
                        for hf in range(2):
                            mm = pe.matmul(ps[:, 2 * s + hf, 0:NH], w[s][:, kk, :],
                                           b[:, kk, hf * NH:(hf + 1) * NH],
                                           start=(kk == 0 and n == 0), stop=(kk == KT - 1 and n == 2))
                    if kk == KT - 1:
                        mm.then_inc(unit_done, 1)

                together = 5
                for kk in range(together):
                    tile(0, kk)
                    tile(1, kk)
                sum_squares(layer, second)
                for s in range(2):
                    for kk in range(together, KT):
                        tile(s, kk)
                        if (s, kk) == (1, 5):
                            turn_back(rms_base(layer, second))

            def block_sums(src, sel, cols):
                for tb in range(5):
                    at = TOKEN_BLOCKS[tb]
                    c0 = SUMS.start + 2 * tb
                    mm = pe.matmul(ps[:, INV_CTX, c0:c0 + cols], src[:, at:at + P], sel, start=True, stop=True)
                return mm

            def turn_back(r):
                pe.wait_ge(inv_made, r + 1)
                for tb in range(5):
                    out = ps[:, INV_LAT, tb * P:(tb + 1) * P] if tb < 4 else ps[:, INV_CTX, 0:P]
                    mm = pe.transpose(out, inv_wide[:, tb, :], ident[:])
                mm.then_inc(inv_turned, 1)

            def sum_squares(layer, second):
                m = 2 * layer + second
                pe.wait_ge(sq_added, (KT - 1) * (m + 1))
                if m:
                    pe.wait_ge(rstd_made, m)
                if second and KINDS[layer] == "attn":
                    pe.wait_ge(ol_made, 40 * (layer // 3 + 1))
                block_sums(sq_sum, ones[:], 1).then_inc(sum_done, 1)

            def sum_heads(layer, i):
                a = layer // 3
                pe.wait_ge(sq_made, SQ0[layer] + KT + i + 1)
                pe.wait_ge(rstd_made, 2 * layer + 1)
                if i:
                    pe.wait_ge(qk_normed, 10 * a + i)
                block_sums(sq[i % 2], two_heads[:], 2).then_inc(heads_summed, 1)

            def turn_heads(layer, i):
                turn_back(RMS0[layer] + 1 + i)

            def ada_multiply(c, par, turn):
                pe.wait_ge(ada_in[par], turn * 16 + 16)
                if not isinstance(c, int) or c >= 1:
                    pe.wait_ge(ada_row, c)
                for r in range(2):
                    for j in range(4):
                        mm = pe.matmul(ps[32 * j:32 * j + 32, ADA_ROWS, 0:AW], cond_act[:, 4 * r + j, :],
                                       ada_w[par][:, 4 * r + j, :], start=(r == 0), stop=(r == 1),
                                       skip_group_check=True)
                mm.then_inc(ada_mm, 1)

            def ada_turn(c):
                pe.wait_ge(ada_row, c + 1)
                if not isinstance(c, int) or c >= 1:
                    pe.wait_ge(ada_done, c)
                for n in range(CT):
                    mm = pe.matmul(ps[:, ADA_COLS, 2 * n:2 * n + 2], ada_rows[:, n * P:(n + 1) * P], pick[:],
                                   start=True, stop=True)
                mm.then_inc(ada_col, 1)

            pe.wait_ge(const_in, 16 * len(CONSTS))
            pe.wait_ge(setup_done, N_SETUP)
            pe.wait_ge(cond_made, 1)
            for c in range(FIRST_CHUNKS):
                ada_multiply(c, c % 2, c // 2)
                if c:
                    ada_turn(c - 1)
            ada_turn(FIRST_CHUNKS - 1)

            for layer, kind in enumerate(KINDS):
                u0 = UNIT0[layer]
                def first_layers_chunk(n):
                    c = FIRST_CHUNKS + n
                    if layer == 0 and c < NCH:
                        ada_multiply(c, c % 2, c // 2)
                    if layer == 0 and n and c - 1 < NCH:
                        ada_turn(c - 1)

                if explicit(layer, False):
                    sum_squares(layer, False)
                    turn_back(rms_base(layer, False))
                if kind == "attn":
                    a = layer // 3
                    unit_pair(u0, layer, False)
                    first_layers_chunk(0)
                    for n in range(1, 12):
                        if n >= 2:
                            unit(u0 + n, n % 2, KT, h_tiles, None, (u0 + n) // 2,
                                 (lambda: sum_heads(layer, n - 3)) if n >= 3 else None)
                        first_layers_chunk(n)
                        if n >= 3:
                            turn_heads(layer, n - 3)
                    if layer == 0:
                        ada_turn(FIRST_CHUNKS + 11)
                        pe.wait_ge(ada_done, FIRST_CHUNKS + 12)
                    sum_heads(layer, 9)
                    for v in range(2):
                        if v or a:
                            pe.wait_ge(v_ready, 2 * a + v)
                        for tb in range(5):
                            at = TOKEN_BLOCKS[tb]
                            mm = pe.transpose(ps[:, 6 + tb // 4, (tb % 4) * P:(tb % 4 + 1) * P],
                                              qkv[:, V0 + v, at:at + P], ident[:])
                        mm.then_inc(v_turned, 1)
                        if v == 0:
                            turn_heads(layer, 9)
                    pe.wait_ge(v_ready, 2 * (a + 1))
                    pe.wait_ge(stage_in, 16 * STAGE_IN[layer])
                    w0 = 40 * a

                    def scores(w):
                        nb, tile = WORK[w - w0]
                        ga = tile // 4
                        if w - w0 >= 2:
                            pe.wait_ge(max_made, 2 * (w - 1))
                        pe.wait_ge(qk_ready, 10 * a + tile + 3)
                        for hd in range(2):
                            rows = slice(HD * hd, HD * hd + HD)
                            q = qkv[rows, Q0 + tile, TOKEN_BLOCKS[nb]:TOKEN_BLOCKS[nb] + P]
                            out = ps[:, 2 * (w % 2) + hd, :]
                            lo, hi = KEYS[nb]
                            first = TOKEN_BLOCKS[nb] + lo - P
                            mm = pe.matmul(out[:, lo:hi], q, qkv[rows, K0 + ga, first:first + hi - lo],
                                           start=True, stop=True)
                            if nb < 4:
                                mm = pe.matmul(out[:, 384:512], q, ck[rows, ga, :], start=True, stop=True)
                            mm.then_inc(s_done, 1)

                    def turn(w):
                        nb, _ = WORK[w - w0]
                        for hd in range(2):
                            pe.wait_ge(p_ready, 2 * w + hd + 1)
                            if w == w0:
                                pe.wait_ge(qk_normed, 10 * (a + 1))
                            if w - w0 >= 1:
                                pe.wait_ge(pt_made, 2 * (w - 1) + hd + 1)
                            for b in BLOCKS[nb]:
                                mm = pe.transpose(ps[:, 4 + hd, b * P:(b + 1) * P],
                                                  prob[w % 2][hd][:, b * P:(b + 1) * P], ident[:])
                            mm.then_inc(t_done, 1)

                    def values(w):
                        nb, tile = WORK[w - w0]
                        ga = tile // 4
                        if w - w0 >= 2:
                            pe.wait_ge(ol_made, w - 1)
                        pe.wait_ge(pt_made, 2 * w + 2)
                        for b in BLOCKS[nb]:
                            for hd in range(2):
                                kv = slice(HD * (2 * ga + hd), HD * (2 * ga + hd + 1))
                                v = cv[:, kv] if b == 3 else v_tok[:, nb - 1 + b, kv]
                                mm = pe.matmul(ps[HD * hd:HD * hd + HD, 6 + w % 2, 0:P], v,
                                               probT[w % 2][hd][:, b * P:(b + 1) * P],
                                               start=(b == BLOCKS[nb][0]), stop=(b == BLOCKS[nb][-1]))
                        mm.then_inc(o_done, 1)

                    for w in range(w0, w0 + 42):
                        if w < w0 + 40:
                            scores(w)
                        if w - w0 >= 2:
                            values(w - 2)
                        if 1 <= w - w0 <= 40:
                            turn(w - 1)
                    pe.wait_ge(ol_made, 40 * (a + 1))
                    for n in range(12, 20):
                        unit(u0 + n, n % 2, KT, h_tiles, None, (u0 + n) // 2)
                        if layer == 0 and FIRST_CHUNKS + n < NCH:
                            ada_multiply(FIRST_CHUNKS + n, n % 2, (FIRST_CHUNKS + n) // 2)
                        if layer == 0 and 12 < n <= NCH - FIRST_CHUNKS:
                            ada_turn(FIRST_CHUNKS + n - 1)
                elif kind == "pool":
                    def group_product(n):
                        par, g = n % 2, n // 2
                        pe.wait_ge(w_pool_in, 16)
                        pe.wait_ge(hh_made, KT * 2 * layer + 2 * g + 2)
                        pe.wait_ge(rstd_made, 2 * layer + 1)
                        if n >= 2:
                            pe.wait_ge(z_made, n - 1)
                        for tb in range(5):
                            at = TOKEN_BLOCKS[tb]
                            for kk in range(2):
                                mm = pe.matmul(ps[:, 4 + 2 * par + tb // 4, (tb % 4) * P:(tb % 4 + 1) * P],
                                               h_whole[:, 2 * g + kk, at:at + P], ada_w[0][:, n, kk * P:(kk + 1) * P],
                                               start=(kk == 0), stop=(kk == 1))
                        mm.then_inc(z_done, 1)

                    def pooling(n):
                        par, g = n % 2, n // 2
                        pe.wait_ge(pool_in, 16)
                        pe.wait_ge(z_made, n + 1)
                        if n < 2:
                            wait_taken(pe, u0 - 2 + n)
                        else:
                            pe.wait_ge(pool_taken, n - 1)
                        for tb in range(5):
                            t0, t1 = POOL_SPAN[tb] if tb < 4 else (0, CTX)
                            mm = pe.matmul(ps[:, 2 * par + tb // 4, t0:t1], z[par][:, tb * P:(tb + 1) * P],
                                           pool_tab[:, g, POOL_AT[tb]:POOL_AT[tb] + t1 - t0],
                                           start=(tb in (0, 4)), stop=(tb in (3, 4)), skip_group_check=True)
                        mm.then_inc(pool_done, 1)

                    for g in range(4):
                        group_product(2 * g)
                        group_product(2 * g + 1)
                        pooling(2 * g)
                        pooling(2 * g + 1)
                else:
                    pe.wait_ge(tabl_made, 2)
                    for g in range(4):
                        for tb in range(5):
                            e = 7 * g + tb
                            if tb == 0:
                                pe.wait_ge(hl_made, low_base(layer, False) + 2 * g + 2)
                            if tb == 4:
                                pe.wait_ge(ftl_made, 6 * g + 1)
                            elif g:
                                if tb == 0:
                                    pe.wait_ge(fth_made, 7 * (g - 1) + 5)
                                else:
                                    pe.wait_ge(ftl_made, 6 * (g - 1) + tb + 1)
                            at = TOKEN_BLOCKS[tb]
                            for kk in range(2):
                                for n, (hx, tab) in enumerate(((h_hi, tab_hi), (h_hi, tab_lo), (h_lo, tab_hi))):
                                    mm = pe.matmul(ps[:, 4 + tb % 4, :], hx[:, 2 * g + kk, at:at + P],
                                                   tab[:, kk, :], start=(kk == 0 and n == 0),
                                                   stop=(kk == 1 and n == 2))
                            mm.then_inc(ft_mm, 1)
                        pe.wait_ge(tabl_made, 10)
                        pe.wait_ge(ctx_tab_in, 16)
                        pe.wait_ge(ftl_made, 6 * g + 4)
                        pe.wait_ge(fth_made, 7 * g + 5)
                        for c in range(2):
                            if g:
                                pe.wait_ge(ftl_made, 6 * (g - 1) + 4 + c + 1)
                            for tb in range(4):
                                for part in range(2):
                                    col = part * 256 + c * P
                                    for n, (ab, tab) in enumerate(((ab_hi, tab_hi), (ab_hi, tab_lo),
                                                                   (ab_lo, tab_hi))):
                                        pe.matmul(ps[:, 2 * c, :], ab[:, tb, col:col + P],
                                                  tab[:, 2 + 4 * part + tb, :],
                                                  start=(tb == 0 and part == 0 and n == 0),
                                                  stop=(tb == 3 and part == 1 and n == 2))
                            for part in range(2):
                                col = part * 256 + c * P
                                mm = pe.matmul(ps[:, 2 * c + 1, 0:CTX], ab_ctx[:, col:col + P],
                                               ctx_tab[:, part * P:part * P + P], start=(part == 0),
                                               stop=(part == 1))
                            mm.then_inc(ft_mm, 1)
                    pe.wait_ge(ftl_made, 24)
                    for n in range(KT):
                        unit(u0 + n, n % 2, KT, h_tiles, None, (u0 + n) // 2)

                last = layer + 1 == DEPTH
                for half in range(2):
                    ub = u0 + MIX_UNITS[kind] + half * (2 * HALF + KT)
                    c0 = NCH * (layer + 1) + half * NCH // 2
                    fl0 = (2 * layer + half) * HALF
                    if half == 0:
                        unit_pair(ub, layer, True)
                    else:
                        unit(ub, 0, KT, h_tiles, None, ub // 2)
                        unit(ub + 1, 1, KT, h_tiles, None, ub // 2)
                    if not last:
                        ada_multiply(c0, 0, c0 // 2)
                    with pe.Fori(0, HALF // 2) as i:
                        for n in range(4):
                            u = ub + 2 + n
                            unit(i * 4 + u, n % 2, KT, h_tiles, None, i * 2 + u // 2)
                            if not last:
                                c = c0 + n // 2
                                if n % 2 == 0:
                                    ada_turn(i * 2 + c)
                                else:
                                    ada_multiply(i * 2 + (c + 1), (c + 1) % 2, i + (c + 1) // 2)
                    if not last:
                        ada_turn(c0 + HALF - 1)
                        ada_multiply(c0 + HALF, (c0 + HALF) % 2, (c0 + HALF) // 2)

                    def gated(kk):
                        pe.wait_ge(fl_made, fl0 + kk + 2)
                    unit(ub + 2 * HALF, 0, HALF, f_tiles, gated, (ub + 2 * HALF) // 2)
                    if not last:
                        ada_turn(c0 + HALF)
                    unit(ub + 2 * HALF + 1, 1, HALF, f_tiles, None, (ub + 2 * HALF) // 2)
                    with pe.Fori(0, KT // 2 - 1) as i:
                        for n in range(2):
                            u = i * 2 + (ub + 2 * HALF + 2 + n)
                            unit(u, n, HALF, f_tiles, None, i + (ub + 2 * HALF + 2) // 2)

        @block.scalar
        def _(act):
            def split_hi(u, par, k, turn):
                if not isinstance(u, int) or u >= 2:
                    act.wait_ge(unit_done, u - 1)
                act.wait_ge(raw_in[par], turn * 16 + 16)
                act.activation(w_hi[par][:, 0:k, :], w_raw[par][:, 0:k, :], ACT.Copy).then_inc(hi_made, 1)

            def split_next(u):
                if u + 2 < len(units):
                    split_hi(u + 2, u % 2, units[u + 2][0], (u + 2) // 2)

            def square_free(layer, second, kk):
                m = 2 * layer + second
                if kk == 0:
                    if m:
                        act.wait_ge(sum_done, m)
                elif kk >= 3:
                    act.wait_ge(sq_added, (KT - 1) * m + kk - 2)
                elif m:
                    act.wait_ge(sq_added, (KT - 1) * m)
                    if second and KINDS[layer] == "attn":
                        act.wait_ge(heads_summed, 10 * (layer // 3 + 1))

            def square(kk, src):
                dst = sq_sum if kk == 0 else sq[kk % 2]
                act.activation(dst[:], src, ACT.Square).then_inc(sq_made, 1)

            def square_tile(layer, second, kk):
                if layer == 0 and not second:
                    act.wait_ge(x_in, 16)
                elif KINDS[layer] == "pool" and second:
                    act.wait_ge(pool_taken, kk + 1)
                else:
                    wait_taken(act, last_update(layer, second, kk))
                square_free(layer, second, kk)
                square(kk, x[:, kk, :])

            def root(i, done, used, scale, cols):
                act.wait_ge(done, used)
                if i:
                    act.wait_ge(inv_made, i)
                act.activation(rms[:, :, 0:cols],
                               ps[:, INV_CTX, SUMS].rearrange("p (b c) -> p b c", c=2)[:, :, 0:cols], ACT.Sqrt,
                               bias=eps[:, 0:1], scale=scale).then_inc(rms_made, 1)

            def gained(layer, second, tiles):
                m = 2 * layer + second
                shift = 24 if second else 0
                for kk in tiles:
                    if kk == 0:
                        act.wait_ge(gain_made, m + 1)
                        act.activation(h_hi[:, :, SH0:NT], mods[layer % 2][:, shift:shift + KT, :], ACT.Copy)
                    for at, n, cnd in STREAMS:
                        op = act.activation(h_hi[:, kk, at:at + n], x[:, kk, at:at + n], ACT.Identity,
                                            scale=gain_now[:, kk, cnd:cnd + 1])
                    op.then_inc(hh_made, 1)

            def norm(layer, second, first=0):
                m = 2 * layer + second
                if not explicit(layer, second):
                    gained(layer, second, range(first, KT))
                root(rms_base(layer, second), sum_done, m + 1, 1.0 / D, 1)

            def shifted(layer, tiles):
                md = mods[layer % 2]
                for kk in tiles:
                    act.wait_ge(xn_made, KT * (layer - 1) + kk + 1)
                    for at, n, cnd in STREAMS:
                        dst = h_whole if KINDS[layer] == "pool" else h_hi
                        op = act.activation(dst[:, kk, at:at + n], xn[kk % 2][:, at:at + n], ACT.Identity,
                                            bias=md[:, kk, cnd:cnd + 1])
                    op.then_inc(hh_made, 1)

            def high_tables(rows):
                for n in rows:
                    act.wait_ge(tab_in[0 if n < 4 else 1], 16)
                    act.activation(tab_hi[:, n, :], tab_raw[:, (n + 6) % 10, :], ACT.Copy).then_inc(tabh_made, 1)

            act.wait_ge(const_in, 16 * len(CONSTS))
            act.wait_ge(setup_done, N_SETUP)
            act.activation(cond_act[:], cond[:], ACT.Silu).then_inc(cond_made, 1)
            for u in range(2):
                split_hi(u, u, units[u][0], 0)
            for kk in range(KT):
                square_tile(0, False, kk)
            for layer, kind in enumerate(KINDS):
                u0 = UNIT0[layer]
                norm(layer, False, 1 if layer and not explicit(layer, False) else 0)
                if kind == "attn":
                    a = layer // 3
                    for n in range(12):
                        i = n - K0
                        if i >= 1:
                            root(RMS0[layer] + i, heads_summed, 10 * a + i, 1.0 / HD, 2)
                        split_next(u0 + n)
                        wait_taken(act, u0 + n)
                        if i >= 2:
                            act.wait_ge(heads_summed, 10 * a + i - 1)
                        elif i >= 0 and layer:
                            act.wait_ge(sq_added, (KT - 1) * (2 * layer + 1))
                        for at, nn, cnd in JOINED:
                            src, bias = scaled[n % 2][:, at:at + nn], scaled[n % 2][:, SH0 + cnd:SH0 + cnd + 1]
                            if i >= 0:
                                op = act.activation(sq[i % 2][:, at:at + nn], src, ACT.Square, bias=bias)
                                if cnd:
                                    op.then_inc(sq_made, 1)
                            op = act.activation(qkv[:, n, at:at + nn], src, ACT.Identity, bias=bias)
                        op.then_inc(qkv_out, 1)
                    root(RMS0[layer] + 10, heads_summed, 10 * (a + 1), 1.0 / HD, 2)
                    w0 = 40 * a

                    def exps(w):
                        nb, tile = WORK[w - w0]
                        ga, r = tile // 4, tile % 4
                        lo, hi = KEYS[nb]
                        hi = 512 if nb < 4 else hi
                        for hd in range(2):
                            head = 8 * ga + 4 * hd + r
                            st = stat[:, w % 2, hd, :]
                            act.wait_ge(max_made, 2 * w + hd + 1)
                            act.activation(prob[w % 2][hd][:, lo:hi], prob[w % 2][hd][:, lo:hi], ACT.Exp,
                                           bias=st[:, 1:2], scale=HD ** -0.5, accum_out=st[:, 2:3])
                            act.activation(st[:, 3:4], sink[:, a, head:head + 1], ACT.Exp,
                                           bias=st[:, 1:2]).then_inc(exp_made, 1)

                    def turned(w):
                        nb, _ = WORK[w - w0]
                        b0, b1 = BLOCKS[nb][0] * P, (BLOCKS[nb][-1] + 1) * P
                        if w - w0 >= 2:
                            act.wait_ge(o_done, w - 1)
                        for hd in range(2):
                            act.wait_ge(t_done, 2 * w + hd + 1)
                            act.activation(probT[w % 2][hd][:, b0:b1], ps[:, 4 + hd, b0:b1],
                                           ACT.Copy).then_inc(pt_made, 1)

                    def out_hi(w):
                        nb, tile = WORK[w - w0]
                        act.wait_ge(o_done, w + 1)
                        act.activation(h_hi[:, tile, TOKEN_BLOCKS[nb]:TOKEN_BLOCKS[nb] + P],
                                       ps[:, 6 + w % 2, 0:P], ACT.Copy).then_inc(oh_made, 1)

                    for w in range(w0, w0 + 42):
                        if w < w0 + 40:
                            exps(w)
                        if w - w0 >= 2:
                            out_hi(w - 2)
                        if 1 <= w - w0 <= 40:
                            turned(w - 1)
                if kind == "pool":
                    shifted(layer, range(4))
                    for g in range(4):
                        for n in (2 * g, 2 * g + 1):
                            act.wait_ge(z_done, n + 1)
                            if g:
                                act.wait_ge(pool_done, n - 1)
                            act.activation(z[n % 2][:], z_product(n % 2), ACT.Copy).then_inc(z_made, 1)
                        if g < 2:
                            shifted(layer, (2 * g + 4, 2 * g + 5))
                        for n in (2 * g, 2 * g + 1):
                            square_tile(layer, True, n)
                    norm(layer, True)
                if kind == "fnet":
                    shifted(layer, range(4))
                    high_tables(range(4, 10))
                    act.wait_ge(tabl_made, 10)
                    for g in range(4):
                        for tb in range(5):
                            act.wait_ge(ft_mm, 7 * g + tb + 1)
                            act.activation(ab_hi[:, tb, :] if tb < 4 else ab_ctx[:], ps[:, 4 + tb % 4, :],
                                           ACT.Copy).then_inc(fth_made, 1)
                        for c in range(2):
                            act.wait_ge(ft_mm, 7 * g + 5 + c + 1)
                            act.activation(h_hi[:, 2 * g + c, LAT0:LAT0 + LAT], ps[:, 2 * c, :], ACT.Copy)
                            act.activation(h_hi[:, 2 * g + c, CTX0:CTX0 + CTX], ps[:, 2 * c + 1, 0:CTX],
                                           ACT.Copy).then_inc(fth_made, 1)
                        if g < 2:
                            shifted(layer, (2 * g + 4, 2 * g + 5))
                if kind != "pool":
                    for n in range(KT):
                        if n == KT - 1:
                            act.wait_ge(unit_done, u0 + MIX_UNITS[kind])
                            gained(layer, True, (0,))
                        split_next(u0 + MIX_UNITS[kind] - KT + n)
                        square_tile(layer, True, n)
                    norm(layer, True, 1)

                def up_step(u, par, half_u, pair, v, k_next):
                    isint = isinstance(v, int)
                    split_hi(u + 2, par, k_next, half_u + 1)
                    act.wait_ge(taken[par], half_u + 1)
                    act.wait_ge(conv_done, v + 1)
                    act.wait_ge(prod_made, pair + 1)
                    for at, n, cnd in STREAMS:
                        op = act.activation(u_pad[par][:, at + 1:at + 1 + n], scaled[par][:, at:at + n],
                                            ACT.Identity, bias=scaled[par][:, SH0 + cnd:SH0 + cnd + 1])
                    op.then_inc(u_padded, 1)
                    act.wait_ge(u_padded, v + 1)
                    act.wait_ge(cond_made, 1)
                    act.activation(conv_out[par][:], u_pad[par][:, 1:NT + 1], ACT.Identity,
                                   bias=conv[:, v, 3:4] if isint else conv[:, bass.ds(v, 1), 3],
                                   scale=conv[:, v, 1:2] if isint else conv[:, bass.ds(v, 1), 1]
                                   ).then_inc(conv_init, 1)
                    if par == 0:
                        act.wait_ge(conv_done, v + 3)
                        act.activation(gate_act[:], conv_out[0][:], ACT.Silu).then_inc(silu_made, 1)

                for half in range(2):
                    ub = u0 + MIX_UNITS[kind] + half * (2 * HALF + KT)
                    v0 = (2 * layer + half) * 2 * HALF
                    with act.Fori(0, HALF // 2) as i:
                        for n in range(4):
                            up_step(i * 4 + (ub + n), n % 2, i * 2 + (ub + n) // 2,
                                    i * 2 + (v0 + n) // 2, i * 4 + (v0 + n), KT)
                    for n in range(2 * HALF - 2, 2 * HALF):
                        up_step(ub + n, n % 2, (ub + n) // 2, (v0 + n) // 2, v0 + n, HALF)
                    ud = ub + 2 * HALF
                    if half == 0 or layer + 1 == DEPTH:
                        with act.Fori(0, KT // 2 - 1) as i:
                            for n in range(2):
                                split_hi(i * 2 + (ud + n + 2), n, HALF, i + (ud + 2) // 2)
                        for n in range(KT - 2, KT):
                            split_next(ud + n)
                    else:
                        for n in range(2):
                            split_next(ud + n)
                            square_tile(layer + 1, False, n)
                        with act.Fori(0, KT // 2 - 2) as i:
                            for n in range(2):
                                act.wait_ge(taken[n], i + (ud + 2) // 2 + 1)
                                act.wait_ge(sq_added, i * 2 + ((KT - 1) * 2 * (layer + 1) + n))
                                split_hi(i * 2 + (ud + n + 4), n, HALF, i + (ud + 4) // 2)
                                act.activation(sq[n][:], x[:, bass.ds(i * 2 + (2 + n), 1), :].rearrange(
                                    "p a n -> p (a n)"), ACT.Square).then_inc(sq_made, 1)
                        for n in range(KT - 2, KT):
                            if n == KT - 1 and not explicit(layer + 1, False):
                                gained(layer + 1, False, (0,))
                            split_next(ud + n)
                            square_tile(layer + 1, False, n)
                if layer + 1 < DEPTH and KINDS[layer + 1] == "fnet":
                    act.wait_ge(unit_done, UNIT0[layer + 1])
                    high_tables(range(4))

        @block.vector
        def _(dve):
            own = Chain(dve, dve_own)

            def split_lo(u, par, k):
                dve.wait_ge(hi_made, u + 1)
                dve.tensor_tensor(w_lo[par][:, 0:k, :], w_raw[par][:, 0:k, :], w_hi[par][:, 0:k, :].bitcast(F32),
                                  ALU.subtract).then_inc(lo_made, 1)

            def split_next(u):
                if u + 2 < len(units):
                    split_lo(u + 2, u % 2, units[u + 2][0])

            def ada_copy(c):
                dve.wait_ge(ada_mm, c + 1)
                if not isinstance(c, int) or c >= 1:
                    dve.wait_ge(ada_col, c)
                dve.tensor_copy(ada_rows[:], ps[:, ADA_ROWS, 0:AW]).then_inc(ada_row, 1)

            def ada_add(c, layer, tile):
                dve.wait_ge(ada_col, c + 1)
                cols = ps[:, ADA_COLS, 0:2 * CT].rearrange("p (n c) -> p n c", c=2)
                if isinstance(tile, int):
                    sl = slice(tile, tile + CT)
                    dve.tensor_tensor(mods[layer % 2][:, sl, :], cols, ada_bias[:, layer, sl, :],
                                      ALU.add).then_inc(ada_done, 1)
                else:
                    dve.tensor_tensor(mods[layer % 2][:, bass.ds(tile, CT), :], cols,
                                      ada_bias[:, layer, bass.ds(tile, CT), :], ALU.add).then_inc(ada_done, 1)

            def invert(r, cols):
                dve.wait_ge(rms_made, r + 1)
                if r:
                    dve.wait_ge(inv_turned, r)
                dve.reciprocal(inv_rms[:, :, 0:cols], rms[:, :, 0:cols]).then_inc(inv_small, 1)
                dve.wait_ge(inv_small, r + 1)
                dve.tensor_copy(inv_wide[:].rearrange("p b (c n) -> p b c n", c=cols),
                                inv_rms[:, :, 0:cols].unsqueeze(3).broadcast_to((P, 5, cols, P // cols))
                                ).then_inc(inv_made, 1)

            def gain(layer, second):
                m = 2 * layer + second
                md = mods[layer % 2]
                dve.wait_ge(ada_done, NCH * (layer + 1) if m else FIRST_CHUNKS)
                sc = 32 if second else 8
                dve.scalar_tensor_tensor(gain_now[:], md[:, sc:sc + KT, :], 1.0,
                                         gains[:, layer, int(second), :, :], ALU.add, ALU.mult).then_inc(gain_made, 1)
                dve.wait_ge(gain_made, m + 1)
                if KINDS[layer] == "pool" and not second:
                    own.link(dve.tensor_tensor(pool_gate[:], md[:, 16:16 + KT, :], pool_scale[:], ALU.mult))

            def gained_low(layer, second, tiles):
                m = 2 * layer + second
                shift = 24 if second else 0
                for kk in tiles:
                    dve.wait_ge(hh_made, KT * m + kk + 1)
                    if kk == 0:
                        dve.tensor_tensor(h_lo[:, :, SH0:NT], mods[layer % 2][:, shift:shift + KT, :],
                                          h_hi[:, :, SH0:NT].bitcast(F32), ALU.subtract)
                    for at, n, cnd in STREAMS:
                        op = dve.scalar_tensor_tensor(h_lo[:, kk, at:at + n], x[:, kk, at:at + n],
                                                      gain_now[:, kk, cnd:cnd + 1],
                                                      h_hi[:, kk, at:at + n].bitcast(F32),
                                                      ALU.mult, ALU.subtract)
                    op.then_inc(hl_made, 1)

            def norm(layer, second, first=0):
                m = 2 * layer + second
                r = rms_base(layer, second)
                if first == 0:
                    gain(layer, second)
                if m == 0:
                    dve.wait_ge(x_in, 16)
                if not explicit(layer, second):
                    gained_low(layer, second, range(first, KT))
                invert(r, 1)
                dve.wait_ge(inv_turned, r + 1)
                dve.tensor_copy(rstd[:, LAT0:LAT0 + LAT], ps[:, INV_LAT, :])
                dve.tensor_copy(rstd[:, CTX0:CTX0 + CTX], ps[:, INV_CTX, 0:CTX]).then_inc(rstd_made, 1)
                dve.wait_ge(rstd_made, m + 1)

            def normed_tiles(layer, tiles):
                base, md = KT * 2 * layer, mods[layer % 2]
                for kk in tiles:
                    if kk >= 2:
                        if KINDS[layer] == "pool":
                            dve.wait_ge(hh_made, base + kk - 1)
                        else:
                            dve.wait_ge(hl_made, low_base(layer, False) + kk - 1)
                    for at, n, cnd in STREAMS:
                        op = dve.scalar_tensor_tensor(xn[kk % 2][:, at:at + n], x[:, kk, at:at + n],
                                                      gain_now[:, kk, cnd:cnd + 1], rstd[:, at:at + n],
                                                      ALU.mult, ALU.mult)
                    op.then_inc(xn_made, 1)
                if KINDS[layer] == "pool":
                    return
                for kk in tiles:
                    dve.wait_ge(hh_made, base + kk + 1)
                    dve.wait_ge(xn_made, KT * (layer - 1) + kk + 1)
                    for at, n, cnd in STREAMS:
                        op = dve.scalar_tensor_tensor(h_lo[:, kk, at:at + n], xn[kk % 2][:, at:at + n],
                                                      md[:, kk, cnd:cnd + 1],
                                                      h_hi[:, kk, at:at + n].bitcast(F32), ALU.add, ALU.subtract)
                    op.then_inc(hl_made, 1)

            def rescale(u, par):
                dve.wait_ge(unit_done, u + 1)
                dve.tensor_tensor(halves(scaled[par][:]), product(par), halves(rstd[:]),
                                  ALU.mult).then_inc(taken[par], 1)

            def update(u, par, o, gate):
                dve.wait_ge(unit_done, u + 1)
                for at, n, bank, col, cnd in ((1, NH - 1, 0, 1, 0), (NH, LAT + 1 - NH, 1, 0, 0),
                                              (CTX0, CTX, 1, CTX0 - NH, 1)):
                    if isinstance(o, int):
                        xt, gt = x[:, o, at:at + n], gate[:, o, cnd:cnd + 1]
                    else:
                        xt = x[:, bass.ds(o, 1), at:at + n].rearrange("p a n -> p (a n)")
                        gt = gate[:, bass.ds(o, 1), cnd]
                    op = dve.scalar_tensor_tensor(xt, ps[:, 2 * par + bank, col:col + n], gt, xt,
                                                  ALU.mult, ALU.add)
                op.then_inc(taken[par], 1)

            dve.wait_ge(const_in, 16 * len(CONSTS))
            own.link(dve.tensor_scalar(neg_sink[:], sink[:], -1.0, None, ALU.mult))
            for u in range(2):
                split_lo(u, u, units[u][0])
            for c in range(FIRST_CHUNKS):
                ada_copy(c)
                if c:
                    ada_add(c - 1, 0, CT * (c - 1))
            ada_add(FIRST_CHUNKS - 1, 0, CT * (FIRST_CHUNKS - 1))

            for layer, kind in enumerate(KINDS):
                u0 = UNIT0[layer]
                def split_tables(rows):
                    for n in rows:
                        dve.wait_ge(tabh_made, n + 1)
                        dve.tensor_tensor(tab_lo[:, n, :], tab_raw[:, (n + 6) % 10, :], tab_hi[:, n, :].bitcast(F32),
                                          ALU.subtract).then_inc(tabl_made, 1)
                if kind == "fnet":
                    split_tables(range(4))
                norm(layer, False, 1 if layer and not explicit(layer, False) else 0)
                if kind in ("pool", "fnet"):
                    normed_tiles(layer, (0, 1))
                    normed_tiles(layer, (2, 3))
                if kind == "fnet":
                    split_tables(range(4, 10))
                gate = pool_gate if kind == "pool" else mods[layer % 2][:, 16:16 + KT, :]
                if kind == "attn":
                    a = layer // 3
                    r0 = RMS0[layer] + 1
                    dve.wait_ge(stage_in, 16 * STAGE_IN[layer])

                    def rotate(i):
                        n = K0 + i
                        dve.wait_ge(inv_turned, r0 + i + 1)
                        dve.wait_ge(qkv_out, 12 * a + n + 1)
                        lat = qkv[:, n, LAT0:LAT0 + LAT]
                        which = 0 if n >= Q0 else 1
                        for tokens, inv in ((lat, ps[:, INV_LAT, :]),
                                            (qkv[:, n, CTX0:CTX0 + CTX], ps[:, INV_CTX, 0:CTX])):
                            op = dve.scalar_tensor_tensor(tokens, tokens, head_gain[:, a, which:which + 1], inv,
                                                          ALU.mult, ALU.mult)
                        op.then_inc(qk_normed, 1)
                        dve.wait_ge(qk_normed, 10 * a + i + 1)
                        own.link(dve.stream_shuffle(swapped[:], lat, [(p + 16) % 32 for p in range(32)]))
                        own.link(dve.tensor_tensor(swapped[:], swapped[:], rope_sin[:], ALU.mult))
                        own.link(dve.tensor_tensor(lat, lat, rope_cos[:], ALU.mult))
                        dve.tensor_tensor(lat, lat, swapped[:], ALU.add).then_inc(qk_ready, 1)

                    for n in range(12):
                        if n >= 2:
                            dve.wait_ge(qkv_out, 12 * a + n - 1)
                        if n >= 3:
                            invert(r0 + n - 3, 2)
                        rescale(u0 + n, n % 2)
                        split_next(u0 + n)
                        if layer == 0:
                            ada_copy(FIRST_CHUNKS + n)
                            if n:
                                ada_add(FIRST_CHUNKS + n - 1, 0, CT * (FIRST_CHUNKS + n - 1))
                        if n >= 3:
                            rotate(n - 3)
                    if layer == 0:
                        ada_add(FIRST_CHUNKS + 11, 0, CT * (FIRST_CHUNKS + 11))
                    invert(r0 + 9, 2)
                    for v in range(2):
                        dve.wait_ge(v_turned, 2 * a + v + 1)
                        dve.tensor_copy(v_tok[:, 0:4, v * P:(v + 1) * P],
                                        ps[:, 6, :].rearrange("p (b c) -> p b c", b=4))
                        dve.tensor_copy(v_tok[:, 4, v * P:(v + 1) * P], ps[:, 7, 0:P]).then_inc(v_ready, 1)
                    rotate(9)
                    w0 = 40 * a

                    def masked(w):
                        nb, tile = WORK[w - w0]
                        ga, r = tile // 4, tile % 4
                        lo, hi = KEYS[nb]
                        hi = 512 if nb < 4 else hi
                        if w - w0 >= 2:
                            dve.wait_ge(t_done, 2 * (w - 1))
                        for hd in range(2):
                            dve.wait_ge(s_done, 2 * w + hd + 1)
                            st = stat[:, w % 2, hd, :]
                            own.link(dve.tensor_tensor_reduce(
                                out=prob[w % 2][hd][:, lo:hi], in0=ps[:, 2 * (w % 2) + hd, lo:hi],
                                in1=band[:, lo:hi], scale=1.0, scalar=-3e38, op0=ALU.add, op1=ALU.max,
                                accum_out=st[:, 0:1]))
                            head = 8 * ga + 4 * hd + r
                            dve.tensor_scalar(st[:, 1:2], st[:, 0:1], -(HD ** -0.5), neg_sink[:, a, head:head + 1],
                                              ALU.mult, ALU.min).then_inc(max_made, 1)

                    def normed(w):
                        nb, _ = WORK[w - w0]
                        lo, hi = KEYS[nb]
                        hi = 512 if nb < 4 else hi
                        dve.wait_ge(exp_made, 2 * w + 2)
                        st = stat[:, w % 2, :, :]
                        own.link(dve.tensor_tensor(st[:, :, 4:5], st[:, :, 2:3], st[:, :, 3:4], ALU.add))
                        own.link(dve.reciprocal(st[:, :, 5:6], st[:, :, 4:5]))
                        for hd in range(2):
                            dve.tensor_scalar(prob[w % 2][hd][:, lo:hi], prob[w % 2][hd][:, lo:hi],
                                              st[:, hd, 5:6], None, ALU.mult).then_inc(p_ready, 1)

                    def out_lo(w):
                        nb, tile = WORK[w - w0]
                        cols = slice(TOKEN_BLOCKS[nb], TOKEN_BLOCKS[nb] + P)
                        dve.wait_ge(oh_made, w + 1)
                        dve.tensor_tensor(h_lo[:, tile, cols], ps[:, 6 + w % 2, 0:P],
                                          h_hi[:, tile, cols].bitcast(F32), ALU.subtract).then_inc(ol_made, 1)

                    for w in range(w0, w0 + 43):
                        if 1 <= w - w0 <= 40:
                            normed(w - 1)
                        if w < w0 + 40:
                            masked(w)
                        if w - w0 >= 3:
                            out_lo(w - 3)
                    for n in range(12, 20):
                        if n == 19:
                            gain(layer, True)
                        update(u0 + n, n % 2, n - 12, gate)
                        if n == 19:
                            gained_low(layer, True, (0,))
                        split_next(u0 + n)
                        c = FIRST_CHUNKS + n
                        if layer == 0 and c < NCH:
                            ada_copy(c)
                        if layer == 0 and 12 < n <= NCH - FIRST_CHUNKS:
                            ada_add(c - 1, 0, CT * (c - 1))
                else:
                    if kind == "fnet":
                        for g in range(4):
                            for tb in range(4):
                                dve.wait_ge(fth_made, 7 * g + tb + 1)
                                dve.tensor_tensor(ab_lo[:, tb, :], ps[:, 4 + tb % 4, :],
                                                  ab_hi[:, tb, :].bitcast(F32), ALU.subtract).then_inc(ftl_made, 1)
                            for c in range(2):
                                dve.wait_ge(fth_made, 7 * g + 5 + c + 1)
                                for at, n, cnd in STREAMS:
                                    op = dve.tensor_tensor(h_lo[:, 2 * g + c, at:at + n],
                                                           ps[:, 2 * c + cnd, 0:n],
                                                           h_hi[:, 2 * g + c, at:at + n].bitcast(F32), ALU.subtract)
                                op.then_inc(ftl_made, 1)
                            if g < 2:
                                normed_tiles(layer, (2 * g + 4, 2 * g + 5))
                        for n in range(KT):
                            if n == KT - 1:
                                gain(layer, True)
                            update(u0 + n, n % 2, n, gate)
                            if n == KT - 1:
                                gained_low(layer, True, (0,))
                            split_next(u0 + n)
                    else:
                        for g in range(4):
                            if g < 2:
                                normed_tiles(layer, (2 * g + 4, 2 * g + 5))
                            for n in (2 * g, 2 * g + 1):
                                dve.wait_ge(pool_done, n + 1)
                                for at, m, cnd in STREAMS:
                                    op = dve.scalar_tensor_tensor(x[:, n, at:at + m], ps[:, 2 * (n % 2) + cnd, 0:m],
                                                                  gate[:, n, cnd:cnd + 1], x[:, n, at:at + m],
                                                                  ALU.mult, ALU.add)
                                op.then_inc(pool_taken, 1)
                norm(layer, True, 0 if kind == "pool" else 1)
                gate = mods[layer % 2][:, 40:40 + KT, :]
                last = layer + 1 == DEPTH
                if kind == "attn":
                    dve.wait_ge(out_sent, 32 * (layer // 3 + 1))

                def up_step(u, par, v, pair, tile, k_next, c=None, c_tile=None, c_end=None, c_end_tile=None):
                    isint = isinstance(v, int)
                    cw = (lambda n: conv[:, v, n:n + 1]) if isint else (lambda n: conv[:, bass.ds(v, 1), n])
                    rescale(u, par)
                    split_lo(u + 2, par, k_next)
                    dve.wait_ge(conv_init, v + 1)
                    own.link(dve.scalar_tensor_tensor(conv_out[par][:], u_pad[par][:, 0:NT], cw(0),
                                                      conv_out[par][:], ALU.mult, ALU.add))
                    dve.scalar_tensor_tensor(conv_out[par][:], u_pad[par][:, 2:NT + 2], cw(2), conv_out[par][:],
                                             ALU.mult, ALU.add).then_inc(conv_done, 1)
                    if par == 0:
                        if c is not None:
                            ada_copy(c)
                    else:
                        dve.wait_ge(silu_made, pair + 1)
                        dve.wait_ge(conv_done, v + 3)
                        dve.wait_ge(fl_made, pair + 1)
                        dve.tensor_tensor(prod[:], gate_act[:], conv_out[1][:], ALU.mult).then_inc(prod_made, 1)
                        dve.wait_ge(prod_made, pair + 2)
                        if isint:
                            fh, fl = f_hi[:, tile, :], f_lo[:, tile, :]
                        else:
                            fh, fl = (ff[:, bass.ds(tile, 1), :].rearrange("p a n -> p (a n)") for ff in (f_hi, f_lo))
                        own.link(dve.tensor_scalar(fh, prod[:], 1.0, None, ALU.mult))
                        dve.tensor_tensor(fl, prod[:], fh.bitcast(F32), ALU.subtract).then_inc(fl_made, 1)
                        if c is not None:
                            ada_add(c, layer + 1, c_tile)
                        if c_end is not None:
                            ada_copy(c_end)

                for half in range(2):
                    ub = u0 + MIX_UNITS[kind] + half * (2 * HALF + KT)
                    v0 = (2 * layer + half) * 2 * HALF
                    ch = half * NCH // 2
                    c0 = NCH * (layer + 1) + ch
                    with dve.Fori(0, HALF // 2) as i:
                        own.enter(i, 6)
                        for n in range(4):
                            up_step(i * 4 + (ub + n), n % 2, i * 4 + (v0 + n), i * 2 + (v0 + n) // 2,
                                    i * 2 + n // 2, KT, None if last else i * 2 + (c0 + n // 2),
                                    i * (2 * CT) + CT * (ch + n // 2))
                    own.leave(HALF // 2)
                    for n in range(2 * HALF - 2, 2 * HALF):
                        c = c0 + HALF - 1
                        up_step(ub + n, n % 2, v0 + n, (v0 + n) // 2, n // 2, HALF, None if last else c,
                                CT * (ch + HALF - 1), None if last else c + 1)
                    ud = ub + 2 * HALF
                    for n in range(2):
                        update(ud + n, n, n, gate)
                        split_next(ud + n)
                        if n == 0 and not last:
                            ada_add(c0 + HALF, layer + 1, CT * (ch + HALF))
                    with dve.Fori(0, KT // 2 - 2) as i:
                        for n in range(2):
                            update(i * 2 + (ud + 2 + n), n, i * 2 + (2 + n), gate)
                            split_lo(i * 2 + (ud + 4 + n), n, HALF)
                    early = half and not last and not explicit(layer + 1, False)
                    for n in range(KT - 2, KT):
                        if early and n == KT - 1:
                            gain(layer + 1, False)
                        update(ud + n, n % 2, n, gate)
                        if early and n == KT - 1:
                            gained_low(layer + 1, False, (0,))
                        split_next(ud + n)


def shape_constants():
    f = np.float32
    p = np.arange(P)
    tok = np.arange(LAT)
    d = p % HD
    pos = np.where((d // 32 == 0)[:, None], (tok // 64)[None], (tok % 64)[None]).astype(f)
    inv_freq = (1.0 / (f(10000.0) ** (np.arange(0, 32, 2, dtype=f) / f(32)))).astype(f)
    angle = pos * inv_freq[d % 16][:, None]
    sign = np.where(d % 32 < 16, -1.0, 1.0)[:, None]
    q, k = np.arange(P)[:, None], np.arange(P)[None]
    band = np.zeros((P, 512), f)
    band[:, 0:128] = np.where(k >= q, 0.0, NEG)
    band[:, 256:384] = np.where(k <= q, 0.0, NEG)
    pool = np.zeros((4, P, POOL_COLS), f)
    for g, w in enumerate(WINDOWS):
        for n, blocks in ((LAT, (0, 1, 3)), (CTX, (4,))):
            src, dst = np.arange(n)[:, None], np.arange(n)[None]
            first, end = np.clip(dst - w // 2, 0, n), np.clip(dst + w - w // 2, 0, n)
            mean = np.where((src >= first) & (src < end), (1.0 / (end - first)).astype(f), f(0)) - (src == dst)
            for b in blocks:
                t0, t1 = POOL_SPAN[b] if b < 4 else (0, CTX)
                s0 = P * b if b < 4 else 0
                pool[g, :, POOL_AT[b]:POOL_AT[b] + t1 - t0] = mean[s0:s0 + P, t0:t1]
    dft = np.zeros((10, P, 512), f)
    ang = 2 * np.pi * ((tok[:, None] * tok[None]) % LAT) / LAT
    dft[2:6] = (np.cos(ang) / np.sqrt(LAT * 256.0)).reshape(4, P, LAT)
    dft[6:10] = (-np.sin(ang) / np.sqrt(LAT * 256.0)).reshape(4, P, LAT)
    ch = np.arange(256)
    ang = 2 * np.pi * ((ch[:, None] * ch[None]) % 256) / 256
    dft[0:2] = np.concatenate([np.cos(ang), np.sin(ang)], 1).reshape(2, P, 512)
    ang = 2 * np.pi * ((p[:, None] * p[None]) % CTX) / CTX
    dft_ctx = (np.concatenate([np.cos(ang), -np.sin(ang)], 1) / np.sqrt(CTX * 256.0)).astype(f)
    pick = np.zeros((P, 2), f)
    for j in range(4):
        pick[32 * j, 0] = pick[32 * j + 1, 1] = 1.0
    return {
        "rope_cos": np.cos(angle).astype(f), "rope_sin": (sign * np.sin(angle)).astype(f), "band": band,
        "pool_tab": pool.transpose(1, 0, 2), "dft": dft, "dft_ctx": dft_ctx, "pick": pick,
        "two_heads": (p[:, None] // HD == np.arange(2)[None]).astype(f), "ident": np.eye(P, dtype=f),
    }


def lay_out(i):
    def token_columns(lat, ctx_rows):
        out = np.zeros((P, KT, NT), np.float32)
        for rows, at in ((lat, LAT0), (ctx_rows, CTX0)):
            out[:, :, at:at + len(rows)] = rows.T.reshape(KT, P, len(rows)).transpose(1, 0, 2)
        return out

    def unit_rows(w, k):
        lead = w.shape[:-2]
        n = w.shape[-1] // P
        w = w.reshape(lead + (k, P, n, P))
        w = np.moveaxis(w, (-2, -3), (len(lead), len(lead) + 1))
        return w.reshape(-1, P, k * P)

    def column(v):
        v = v.reshape(v.shape[:-1] + (-1, P))
        return np.moveaxis(v, -1, 0)

    def twice(v):
        return np.repeat(v[..., None], 2, -1)

    cond = np.zeros((P, KT, 32), np.float32)
    cond[:, :, 0] = i["c"][0].reshape(KT, P).T
    cond[:, :, 1] = i["c_ctx"].reshape(KT, P).T
    heads = [8 * (tl // 4) + 4 * hd + tl % 4 for tl in range(KT) for hd in range(2)]
    qcols = np.concatenate([np.arange(HD * h, HD * h + HD) for h in heads])
    cols = np.concatenate([np.arange(D + 256, D + 512), np.arange(D, D + 256), qcols])
    pairs = [n for j in range(FT) for n in (j, FT + j)]
    w_in = unit_rows(i["ffn_w_in"], KT).reshape(DEPTH, 2 * FT, P, KT * P)[:, pairs].reshape(-1, P, KT * P)
    conv = np.concatenate([i["ffn_conv_w"], i["ffn_conv_b"][:, None]], 1)
    conv = column(conv)[:, :, :, pairs].transpose(0, 1, 3, 2).reshape(P, DEPTH * 2 * FT, 4)
    head_gain = np.stack([np.tile(i["attn_q_norm"], (1, 2)), np.tile(i["attn_k_norm"], (1, 2))], -1)
    ck = i["cache_k"][0].reshape(2, P, 2, P).transpose(0, 3, 2, 1)
    out = {
        "x": token_columns(i["x_sample"][0], i["x_prompt"][0]),
        "cond": cond,
        "ada_w": i["ada_w"].reshape(DEPTH, KT, P, NCH, AW).transpose(0, 3, 2, 1, 4).reshape(-1, P, KT * AW),
        "ada_bias": twice(column(i["ada_b"])),
        "gains": twice(np.stack([column(i["norm_mix"]), column(i["norm_ffn"])], 2)),
        "pool_scale": twice(column(i["pool_scale"])[:, 0]),
        "w_qkv": unit_rows(i["attn_w_qkv"][:, :, cols], KT),
        "w_o": unit_rows(i["attn_w_o"][:, qcols], KT),
        "w_pool": unit_rows(i["pool_w"][0], 2).transpose(1, 0, 2).reshape(P, KT, 2 * P),
        "w_fnet": unit_rows(i["fnet_w"], KT),
        "w_in": w_in,
        "w_out": unit_rows(i["ffn_w_out"].reshape(DEPTH, 2, HALF * P, D), HALF),
        "conv": conv,
        "head_gain": head_gain.transpose(1, 0, 2),
        "sink": np.broadcast_to(i["attn_sink"], (P, 2, NHEADS)),
        "cache_k": ck,
        "cache_v": i["cache_v"][0].reshape(2, P, 256),
    }
    return out


def kernel(**inputs):
    import concourse.bacc as bacc
    from concourse.bass_utils import run_bass_kernel_spmd

    arrays = lay_out({k: np.asarray(v) for k, v in inputs.items()})
    arrays.update(shape_constants())
    arrays = {f"in_{k}": np.ascontiguousarray(v) for k, v in arrays.items()}
    nc = bacc.Bacc("TRN2", target_bir_lowering=False, num_devices=1)
    t = {k[3:]: nc.dram_tensor(k, v.shape, F32, kind="ExternalInput").ap() for k, v in arrays.items()}
    for name, shape in (("y", (P, KT, NT)), ("new_k", (2, P, 2, CTX)), ("new_v", (2, P, 2, CTX))):
        t[name] = nc.dram_tensor(f"out_{name}", shape, F32, kind="ExternalOutput").ap()
    build(nc, t)
    r = run_bass_kernel_spmd(nc, [arrays], core_ids=[0]).results[0]
    y = r["out_y"].transpose(1, 0, 2).reshape(D, NT)
    caches = [r[f"out_{n}"].transpose(0, 3, 2, 1).reshape(1, 2, CTX, 4, HD) for n in ("new_k", "new_v")]
    return (np.ascontiguousarray(y[:, CTX0:CTX0 + CTX].T)[None], np.ascontiguousarray(y[:, LAT0:LAT0 + LAT].T)[None],
            np.ascontiguousarray(caches[0]), np.ascontiguousarray(caches[1]))
```
